# Optimizing a Trainium2 kernel written in Bass

```python
import jax, jax.numpy as jnp
from jax import lax
import numpy as np

D_MODEL = 1024
BATCH = 1
SEQ = 2048
DEPTH = 1

N_META = 16
GRID_W = 64
D_ATTN = D_MODEL // 2
N_HEADS = 8
N_KV_HEADS = 2
HEAD_DIM = D_ATTN // N_HEADS
KV_GROUP = N_HEADS // N_KV_HEADS
D_KV = N_KV_HEADS * HEAD_DIM
ROPE_AXIS_PAIRS = HEAD_DIM // 4
ROPE_THETA = 10000.0
Q_BLOCK = 128
D_POOL = D_MODEL // 2
POOL_WINDOWS = (2, 4, 8, 16)
N_POOL_GROUPS = len(POOL_WINDOWS)
POOL_GROUP = D_POOL // N_POOL_GROUPS
D_MIX = D_ATTN + D_POOL
D_IN = D_ATTN + 2 * D_KV + D_POOL
D_FF = -(-8 * D_MODEL // (3 * 256)) * 256
EPS = 1e-6

kernel_name = "hybrid_gqa_axialrope_multiscale_pool_swiglu"

def rmsnorm(x, g):
    xf = x.astype(jnp.float32)
    y = xf * lax.rsqrt(jnp.mean(xf * xf, axis=-1, keepdims=True) + EPS)
    return (y * g.astype(jnp.float32)).astype(x.dtype)

def axial_rope_tables(L, n_real):
    rows = n_real // GRID_W
    t = jnp.arange(L, dtype=jnp.int32)
    r = t - N_META
    real = r >= 0
    row = jnp.where(real, r // GRID_W - rows // 2, 0).astype(jnp.float32)
    col = jnp.where(real, r % GRID_W - GRID_W // 2, 0).astype(jnp.float32)
    freqs = ROPE_THETA ** (-jnp.arange(ROPE_AXIS_PAIRS, dtype=jnp.float32) / ROPE_AXIS_PAIRS)
    ang = jnp.stack([row[:, None] * freqs, col[:, None] * freqs], axis=1)
    return jnp.cos(ang), jnp.sin(ang)

def apply_axial_rope(x, cos, sin):
    B, L, H, _ = x.shape
    xf = x.astype(jnp.float32).reshape(B, L, H, 2, 2, ROPE_AXIS_PAIRS)
    x0, x1 = xf[..., 0, :], xf[..., 1, :]
    c = cos[None, :, None]
    s = sin[None, :, None]
    out = jnp.stack([x0 * c - x1 * s, x0 * s + x1 * c], axis=-2)
    return out.reshape(x.shape).astype(x.dtype)

def attend_block(qb, k, v):
    B, Tq = qb.shape[0], qb.shape[1]
    qg = qb.reshape(B, Tq, N_KV_HEADS, KV_GROUP, HEAD_DIM)
    s = jnp.einsum('bqkgd,bskd->bkgqs', qg, k).astype(jnp.float32) * (HEAD_DIM ** -0.5)
    p = jax.nn.softmax(s, axis=-1).astype(v.dtype)
    o = jnp.einsum('bkgqs,bskd->bqkgd', p, v)
    return o.reshape(B, Tq, D_ATTN)

def gqa_bidirectional(q, k, v):
    B, L = q.shape[0], q.shape[1]
    n_real = L - N_META
    nb = n_real // Q_BLOCK
    out_meta = attend_block(q[:, :N_META], k, v)
    q_real = q[:, N_META:].reshape(B, nb, Q_BLOCK, N_HEADS, HEAD_DIM)
    q_real = jnp.moveaxis(q_real, 1, 0)
    out_real = lax.map(lambda qb: attend_block(qb, k, v), q_real)
    out_real = jnp.moveaxis(out_real, 0, 1).reshape(B, n_real, D_ATTN)
    return jnp.concatenate([out_meta, out_real], axis=1)

def multiscale_pool(u, w_pool):
    B, L, _ = u.shape
    t = jnp.arange(L, dtype=jnp.int32)
    diffs = []
    for gi, w in enumerate(POOL_WINDOWS):
        ug = u[..., gi * POOL_GROUP:(gi + 1) * POOL_GROUP].astype(jnp.float32)
        S = jnp.concatenate([jnp.zeros((B, 1, POOL_GROUP), jnp.float32),
                             jnp.cumsum(ug, axis=1)], axis=1)
        lo = jnp.clip(t - w // 2, 0, L)
        hi = jnp.clip(t + w - w // 2, 0, L)
        win_sum = jnp.take(S, hi, axis=1) - jnp.take(S, lo, axis=1)
        cnt = (hi - lo).astype(jnp.float32)[None, :, None]
        diffs.append(win_sum / cnt - ug)
    d = jnp.stack(diffs, axis=2).astype(u.dtype)
    y = jnp.einsum('blgc,gcd->blgd', d, w_pool)
    return y.reshape(B, L, D_POOL)

def setup_inputs(seed: int = 0) -> dict:
    key = jax.random.key(seed)
    ks = jax.random.split(key, 14)
    f32 = jnp.float32

    def gain(k, shape):
        return 1.0 + 0.05 * jax.random.normal(k, shape, f32)

    return {
        "x": jax.random.normal(ks[0], (BATCH, SEQ, D_MODEL), f32),
        "meta_tokens": jax.random.normal(ks[1], (N_META, D_MODEL), f32),
        "norm_mix": gain(ks[2], (DEPTH, D_MODEL)),
        "w_in": jax.random.normal(ks[3], (DEPTH, D_MODEL, D_IN), f32) * D_MODEL ** -0.5,
        "q_norm": gain(ks[4], (DEPTH, HEAD_DIM)),
        "k_norm": gain(ks[5], (DEPTH, HEAD_DIM)),
        "attn_out_norm": gain(ks[6], (DEPTH, D_ATTN)),
        "w_pool": jax.random.normal(ks[7], (DEPTH, N_POOL_GROUPS, POOL_GROUP, POOL_GROUP), f32) * POOL_GROUP ** -0.5,
        "pool_scale": gain(ks[8], (DEPTH, D_POOL)),
        "w_out": jax.random.normal(ks[9], (DEPTH, D_MIX, D_MODEL), f32) * D_MIX ** -0.5,
        "norm_ffn": gain(ks[10], (DEPTH, D_MODEL)),
        "w_ffn_in": jax.random.normal(ks[11], (DEPTH, D_MODEL, 2 * D_FF), f32) * D_MODEL ** -0.5,
        "w_ffn_down": jax.random.normal(ks[12], (DEPTH, D_FF, D_MODEL), f32) * D_FF ** -0.5,
        "norm_final": gain(ks[13], (D_MODEL,)),
    }

def reference(x, meta_tokens, norm_mix, w_in, q_norm, k_norm, attn_out_norm,
              w_pool, pool_scale, w_out, norm_ffn, w_ffn_in, w_ffn_down, norm_final):
    B, n_real, _ = x.shape
    meta = jnp.broadcast_to(meta_tokens[None].astype(x.dtype), (B, N_META, D_MODEL))
    h_res = jnp.concatenate([meta, x], axis=1)
    L = N_META + n_real
    cos, sin = axial_rope_tables(L, n_real)

    for l in range(DEPTH):
        h = rmsnorm(h_res, norm_mix[l])
        proj = h @ w_in[l]
        q = proj[..., :D_ATTN].reshape(B, L, N_HEADS, HEAD_DIM)
        k = proj[..., D_ATTN:D_ATTN + D_KV].reshape(B, L, N_KV_HEADS, HEAD_DIM)
        v = proj[..., D_ATTN + D_KV:D_ATTN + 2 * D_KV].reshape(B, L, N_KV_HEADS, HEAD_DIM)
        u = proj[..., D_ATTN + 2 * D_KV:]

        q = apply_axial_rope(rmsnorm(q, q_norm[l]), cos, sin)
        k = apply_axial_rope(rmsnorm(k, k_norm[l]), cos, sin)
        attn = rmsnorm(gqa_bidirectional(q, k, v), attn_out_norm[l])
        pool = rmsnorm(multiscale_pool(u, w_pool[l]), pool_scale[l])

        mixed = jnp.concatenate([attn, pool], axis=-1)
        h_res = h_res + mixed @ w_out[l]

        h = rmsnorm(h_res, norm_ffn[l])
        gu = h @ w_ffn_in[l]
        h_res = h_res + (jax.nn.silu(gu[..., :D_FF]) * gu[..., D_FF:]) @ w_ffn_down[l]

    return rmsnorm(h_res, norm_final)[:, N_META:]


_drawn_inputs = setup_inputs


def setup_inputs(seed=0):
    import zlib

    import numpy as np

    out = dict(_drawn_inputs(seed))
    spreads = {}
    factors = {}
    for name, (base, spread) in spreads.items():
        noise = np.random.default_rng([zlib.crc32(name.encode()), seed]).standard_normal(out[name].shape)
        drawn = base * np.exp(spread * noise) if base else spread * noise
        out[name] = __import__('jax').numpy.asarray(drawn.astype(out[name].dtype))
    for name, factor in factors.items():
        out[name] = (out[name] * factor).astype(out[name].dtype)
    return out
```

```python
import math
from contextlib import ExitStack

import numpy as np

import concourse.bass as bass
import concourse.mybir as mybir

F32 = mybir.dt.float32
F32R = mybir.dt.float32r
ACT = mybir.ActivationFunctionType
ALU = mybir.AluOpType
AX = mybir.AxisListType
ds = bass.ds

P = 128
D = 1024
SEQ = 2048
META = 16
GRID_W = 64
HEADS, KV, HD = 8, 2, 64
DA = HEADS * HD
DKV = KV * HD
DP = 512
GROUPS = 4
WINDOWS = (2, 4, 8, 16)
DIN = DA + 2 * DKV + DP
DFF = 2816
EPS = 1e-6
ROPE_THETA = 10000.0

L = META + SEQ
KT = D // P
NT = SEQ // P
CT = 2
CW = CT * P
NCH = NT // CT
U0 = DA + 2 * DKV
NKT = NT + 1
UPAD = L + 16
QK = DA + DKV
NH = HEADS + KV
FT = DFF // P
FC = 4
FW = FC * P
NFC = NT // FC


def split_hi(act, hi, src, scale=1.0):
    return act.activation(hi, src, ACT.Copy, scale=scale)


def matmul3(pe, out, st_hi, st_lo, mv_hi, mv_lo, start, stop):
    pe.matmul(out, st_hi, mv_hi, start=start, stop=False)
    pe.matmul(out, st_hi, mv_lo, start=False, stop=False)
    return pe.matmul(out, st_lo, mv_hi, start=False, stop=stop)


class Shared:
    pass


def project(nc, m, x, meta, rope, w_in, norm_mix, q_norm, k_norm):
    with ExitStack() as ctx:
        sb = lambda n, s, d=F32: ctx.enter_context(nc.sbuf_tensor(n, s, d))
        sem = lambda n: ctx.enter_context(nc.semaphore(n))
        ident, ps = m.ident, m.ps
        win_hi = sb("win_hi", [P, KT, DIN], F32R)
        win_lo = sb("win_lo", [P, KT, DIN], F32R)
        x_raw = sb("x_raw", [P, CT, D])
        x_meta = sb("x_meta", [META, D])
        xn = sb("xn", [P, CT, D])
        xn_meta = sb("xn_meta", [META, D])
        hT_hi = sb("hT_hi", [P, KT, CW], F32R)
        hT_lo = sb("hT_lo", [P, KT, CW], F32R)
        hm_hi = sb("hm_hi", [P, KT, META], F32R)
        hm_lo = sb("hm_lo", [P, KT, META], F32R)
        hm = sb("hm", [P, KT, META])
        u_out = sb("u_out", [P, 2, CW])
        w_stage = sb("w_stage", [P, 2, DIN])
        qkv = sb("qkv", [P, CT, QK + DKV])
        sq = sb("sq", [P, QK])
        t1 = sb("t1", [P, QK])
        t2 = sb("t2", [P, QK])
        q_out = sb("q_out", [P, CT, DA])
        k_tok = sb("k_tok", [P, CT, KV, 2, HD])
        cs = sb("cs", [P, CT, 2, HD])
        cs_meta = sb("cs_meta", [META, 2, HD])
        g_in = sb("g_in", [P, KT])
        g_qk = sb("g_qk", [P, 2, HD])
        eps = m.eps
        ssx = sb("ssx", [P, 3])
        sdx = sb("sdx", [P, 3])
        rsx = sb("rsx", [P, 3])
        ssh = sb("ssh", [P, NH])
        sdh = sb("sdh", [P, NH])
        rsh = sb("rsh", [P, NH])

        const_in = sem("p_const_in")
        x_in = [sem(f"p_x_in{j}") for j in range(CT)]
        cs_in = [sem(f"p_cs_in{j}") for j in range(CT)]
        w_staged = [sem(f"p_w_staged{j}") for j in range(2)]
        w_hi_done, w_lo_done = sem("p_w_hi_done"), sem("p_w_lo_done")
        x_ssq, x_sd, x_rs, xn_done = sem("p_x_ssq"), sem("p_x_sd"), sem("p_x_rs"), sem("p_xn_done")
        t_done, h_hi_done, h_lo_done = sem("p_t_done"), sem("p_h_hi_done"), sem("p_h_lo_done")
        hm_done = sem("p_hm_done")
        u_done, u_evac = sem("p_u_done"), sem("p_u_evac")
        u_store = [sem(f"p_u_store{j}") for j in range(2)]
        q_done, q_evac, kv_done, kv_evac = sem("p_q_done"), sem("p_q_evac"), sem("p_kv_done"), sem("p_kv_evac")
        sq_done, gain_done, head_sd, v_hi_done = sem("p_sq_done"), sem("p_gain_done"), sem("p_head_sd"), sem("p_v_hi_done")
        post, qkv_free = sem("p_post"), sem("p_qkv_free")
        q_store = [sem(f"p_q_store{j}") for j in range(CT)]
        kt_done, k_hi_done, k_lo_done = sem("p_kt_done"), sem("p_k_hi_done"), sem("p_k_lo_done")

        POST = 9

        block = ctx.enter_context(nc.Block())

        @block.sync
        def _(sp):
            for dst, src in (
                (ident[:], m.ident_in),
                (x_meta[:], meta),
                (g_in[:], norm_mix),
                (g_qk[:, 0, :], q_norm.unsqueeze(0).broadcast_to([P, HD])),
                (g_qk[:, 1, :], k_norm.unsqueeze(0).broadcast_to([P, HD])),
                (cs_meta[:], rope[SEQ:L].rearrange("p (a n) -> p a n", a=2)),
            ):
                sp.dma_start(dst, src).then_inc(const_in, 16)
            for j in range(CT):
                sp.dma_start(x_raw[:, j, :], x[j * P:(j + 1) * P]).then_inc(x_in[j], 16)
            for k in range(KT):
                if k >= 2:
                    sp.wait_ge(w_lo_done, k - 1)
                sp.dma_start(w_stage[:, k % 2, :], w_in[k * P:(k + 1) * P]).then_inc(w_staged[k % 2], 16)

            for j in range(2):
                sp.sem_inc(u_store[j], 16)
            for j in range(CT):
                sp.sem_inc(q_store[j], 16)
            sp.wait_ge(u_evac, 1)
            sp.dma_start(m.u_d[:, :, 0:META].rearrange("g p n -> p g n"),
                         u_out[:, 0, 0:GROUPS * META].rearrange("p (g n) -> p g n", g=GROUPS)).then_inc(u_store[0], 16)

            def chunk(c, more):
                for j in range(CT):
                    sp.wait_ge(qkv_free, 2 * c + j + 1)
                    sp.dma_start(cs[:, j], rope[ds(c * CW + j * P, P)].rearrange("p (a n) -> p a n", a=2)).then_inc(cs_in[j], 16)
                if more:
                    for j in range(CT):
                        sp.wait_ge(xn_done, 2 * c + j + 2)
                        sp.dma_start(x_raw[:, j, :], x[ds(c * CW + (j + CT) * P, P)]).then_inc(x_in[j], 16)
                for f in range(GROUPS):
                    sp.wait_ge(u_evac, 4 * c + f + 2)
                    sp.dma_start(m.u_d[f, :, ds(c * CW + META, CW)], u_out[:, f % 2, :]).then_inc(u_store[f % 2], 16)
                for j in range(CT):
                    sp.wait_ge(post, POST * (2 * c + j + 2))
                    sp.dma_start(m.q_d[ds(c * CW + j * P, P)], q_out[:, j, :]).then_inc(q_store[j], 16)

            with sp.Fori(0, NCH - 1) as c:
                chunk(c, True)
            chunk(NCH - 1, False)
            sp.wait_ge(u_store[0], 16 * (2 + 2 * NCH))
            sp.wait_ge(u_store[1], 16 * (1 + 2 * NCH))
            for j in range(CT):
                sp.wait_ge(q_store[j], 16 * (NCH + 1))

        @block.gpsimd
        def _(pool):
            def head_gain(n, rows, j, h0):
                lo = h0 * HD
                src = qkv[0:rows, j, lo:QK]
                pool.tensor_tensor(sq[0:rows, lo:QK], src, src, ALU.mult).then_inc(sq_done, 1)
                pool.wait_ge(sq_done, n + 1)
                parts = ([(0, DA, 0)] if h0 == 0 else []) + [(DA, QK, 1)]
                for a, b, which in parts:
                    v = qkv[0:rows, j, a:b].rearrange("p (h n) -> p h n", n=HD)
                    g = g_qk[0:rows, which, :].unsqueeze(1).broadcast_to([rows, (b - a) // HD, HD])
                    pool.tensor_tensor(v, v, g, ALU.mult).then_inc(gain_done, 1)

            pool.wait_ge(const_in, 96)
            pool.wait_ge(kv_evac, 1)
            head_gain(0, META, 1, HEADS)
            with pool.Fori(0, NCH) as c:
                for j in range(CT):
                    pool.wait_ge(q_evac, 2 * c + j + 2)
                    pool.wait_ge(kv_evac, 2 * c + j + 2)
                    pool.wait_ge(post, POST * (2 * c + j) + 2)
                    head_gain(2 * c + j + 1, P, j, 0)

        @block.scalar
        def _(act):
            def norm(n, src, junk, rows, col):
                act.activation(junk, src, ACT.Square, accum_out=ssx[0:rows, col:col + 1]).then_inc(x_ssq, 1)
                act.wait_ge(x_ssq, n)
                act.activation(sdx[0:rows, col:col + 1], ssx[0:rows, col:col + 1], ACT.Sqrt,
                               scale=1.0 / D, bias=eps[0:rows]).then_inc(x_sd, 1)

            def norm_tile(c, j):
                act.wait_ge(x_in[j], 16 * (c + 1))
                act.wait_ge(t_done, 8 * c + 1)
                norm(2 * c + j + 2, x_raw[:, j, :], xn[:, j, :], P, j)

            def head_norm(n, rows, h0):
                act.wait_ge(post, POST * n + 2)
                act.activation(sdh[0:rows, h0:NH], ssh[0:rows, h0:NH], ACT.Sqrt,
                               scale=1.0 / HD, bias=eps[0:rows]).then_inc(head_sd, 1)

            def h_evac(c):
                for k in range(KT):
                    act.wait_ge(t_done, 8 * c + k + 2)
                    split_hi(act, hT_hi[:, k, :], ps[:, k % 2, 0:CW], g_in[:, k:k + 1]).then_inc(h_hi_done, 1)

            def u_out_evac(c):
                for f in range(GROUPS):
                    act.wait_ge(u_done, 4 * c + f + 2)
                    act.wait_ge(u_store[f % 2], 16 * (2 * c + f // 2 + (2 if f % 2 == 0 else 1)))
                    act.copy(u_out[:, f % 2, :], ps[:, 2 + f, 0:CW]).then_inc(u_evac, 1)

            def k_evac(c):
                for g in range(KV):
                    act.wait_ge(kt_done, 2 * c + g + 2)
                    split_hi(act, m.k_st[:, g, ds(c * CW, CW)], ps[:, g, 0:CW]).then_inc(k_hi_done, 1)

            def qkv_evac(c, j):
                i = 2 * c + j
                act.wait_ge(qkv_free, i + 1)
                act.wait_ge(q_done, i + 1)
                act.copy(qkv[:, j, 0:DA], ps[:, 6, :]).then_inc(q_evac, 1)
                act.wait_ge(kv_done, i + 2)
                act.copy(qkv[:, j, DA:], ps[:, 7, 0:2 * DKV]).then_inc(kv_evac, 1)
                act.wait_ge(kv_evac, i + 2)
                v = qkv[:, j, QK:].rearrange("p (g n) -> p g n", g=KV)
                act.copy(m.v_st[:, ds(i, 1), :, 0:HD].rearrange("p a g n -> p (a g) n"), v).then_inc(v_hi_done, 1)
                head_norm(i + 1, P, 0)

            act.wait_ge(m.eps_set, 1)
            act.wait_ge(const_in, 96)
            norm(1, x_meta[:], xn_meta[:], META, 2)
            act.wait_ge(hm_done, 1)
            split_hi(act, hm_hi[:], hm[:]).then_inc(h_hi_done, 1)
            for j in range(CT):
                norm_tile(0, j)
            for k in range(KT):
                act.wait_ge(w_staged[k % 2], 16 * (k // 2 + 1))
                split_hi(act, win_hi[:, k, :], w_stage[:, k % 2, :]).then_inc(w_hi_done, 1)
            act.wait_ge(u_done, 1)
            act.copy(u_out[:, 0, 0:GROUPS * META].rearrange("p (g n) -> p g n", g=GROUPS),
                     ps[:, 2:6, 0:META]).then_inc(u_evac, 1)
            act.sem_inc(q_evac, 1)
            act.wait_ge(kv_done, 1)
            act.copy(qkv[0:META, 1, DA:], ps[0:META, 7, 0:2 * DKV]).then_inc(kv_evac, 1)
            act.wait_ge(kv_evac, 1)
            act.copy(m.v_st[0:META, NT, :, 0:HD],
                     qkv[0:META, 1, QK:].rearrange("p (g n) -> p g n", g=KV)).then_inc(v_hi_done, 1)
            head_norm(0, META, HEADS)
            h_evac(0)
            u_out_evac(0)
            act.wait_ge(kt_done, 1)
            split_hi(act, m.k_st[:, :, SEQ:L],
                     ps[:, 0, 0:KV * META].rearrange("p (g n) -> p g n", g=KV)).then_inc(k_hi_done, 1)
            with act.Fori(0, NCH - 1) as c:
                for j in range(CT):
                    qkv_evac(c, j)
                    norm_tile(c + 1, j)
                h_evac(c + 1)
                u_out_evac(c + 1)
                k_evac(c)
            for j in range(CT):
                qkv_evac(NCH - 1, j)
            k_evac(NCH - 1)

        @block.vector
        def _(dve):
            dve.memset(eps[:], EPS).then_inc(m.eps_set, 1)
            dve.sem_inc(h_lo_done, 1)
            dve.sem_inc(k_lo_done, 2)
            dve.sem_inc(qkv_free, 1)

            def norm(n, out, src, rows, col):
                dve.wait_ge(x_sd, n)
                dve.reciprocal(rsx[0:rows, col:col + 1], sdx[0:rows, col:col + 1]).then_inc(x_rs, 1)
                dve.wait_ge(x_rs, n)
                dve.tensor_scalar(out, src, rsx[0:rows, col:col + 1], None, ALU.mult).then_inc(xn_done, 1)

            def norm_tile(c, j):
                norm(2 * c + j + 2, xn[:, j, :], x_raw[:, j, :], P, j)

            def h_evac(c):
                for k in range(KT):
                    dve.wait_ge(h_hi_done, 8 * c + k + 2)
                    dve.scalar_tensor_tensor(hT_lo[:, k, :], ps[:, k % 2, 0:CW], g_in[:, k:k + 1],
                                             hT_hi[:, k, :].bitcast(F32), ALU.mult, ALU.subtract).then_inc(h_lo_done, 1)

            def k_evac(c):
                for g in range(KV):
                    dve.wait_ge(k_hi_done, 2 * c + g + 2)
                    lo = m.k_st[HD:P, g, ds(c * CW, CW)]
                    dve.tensor_tensor(lo, ps[HD:P, g, 0:CW], lo.bitcast(F32), ALU.subtract).then_inc(k_lo_done, 1)

            def post_tile(n, rows, j, h0, v_lo, v_hi, table):
                base = POST * n
                lo, nh = h0 * HD, NH - h0
                dve.wait_ge(v_hi_done, n + 1)
                v = qkv[0:rows, j, QK:].rearrange("p (g n) -> p g n", g=KV)
                dve.tensor_tensor(v_lo, v, v_hi.bitcast(F32), ALU.subtract).then_inc(post, 1)
                dve.wait_ge(sq_done, n + 1)
                dve.tensor_reduce(ssh[0:rows, h0:NH], sq[0:rows, lo:QK].rearrange("p (h n) -> p h n", n=HD),
                                  AX.X, ALU.add).then_inc(post, 1)
                dve.wait_ge(gain_done, 2 * n + 1)
                if h0 == 0:
                    dve.wait_ge(post, base)
                cos = table[:, 0, :].unsqueeze(1).broadcast_to([rows, nh, HD])
                r3 = qkv[0:rows, j, lo:QK].rearrange("p (h n) -> p h n", n=HD)
                t1v = t1[0:rows, lo:QK].rearrange("p (h n) -> p h n", n=HD)
                dve.tensor_tensor(t1v, r3, cos, ALU.mult).then_inc(post, 1)
                r5 = qkv[0:rows, j, lo:QK].rearrange("p (h b n) -> p h b n", b=2, n=HD // 4)
                t5 = t2[0:rows, lo:QK].rearrange("p (h b n) -> p h b n", b=2, n=HD // 4)
                s5 = table[:, 1, :].rearrange("p (a b n) -> p a b n", a=2, b=2)
                for b in range(2):
                    src = r5[:, :, 1 - b, :].rearrange("p (h a) n -> p h a n", a=2)
                    dst = t5[:, :, b, :].rearrange("p (h a) n -> p h a n", a=2)
                    sin = s5[:, :, b, :].unsqueeze(1).broadcast_to([rows, nh, 2, HD // 4])
                    last = dve.tensor_tensor(dst, src, sin, ALU.mult).then_inc(post, 1)
                dve.wait_ge(post, base + 5)
                dve.sem_inc(qkv_free, 1)
                dve.tensor_tensor(t1[0:rows, lo:QK], t1[0:rows, lo:QK], t2[0:rows, lo:QK], ALU.add).then_inc(post, 1)
                dve.wait_ge(head_sd, n + 1)
                dve.reciprocal(rsh[0:rows, h0:NH], sdh[0:rows, h0:NH]).then_inc(post, 1)
                dve.wait_ge(post, base + 7)
                k_in = t1[0:rows, DA:QK].rearrange("p (g n) -> p g n", g=KV)
                rk = rsh[0:rows, HEADS:NH]
                if h0:
                    for dup in range(2):
                        dve.tensor_tensor(k_tok[0:rows, j, :, dup, :], k_in,
                                          rk.unsqueeze(2).broadcast_to([rows, KV, HD]), ALU.mult).then_inc(post, 1)
                else:
                    for g in range(KV):
                        last = dve.tensor_tensor(
                            k_tok[0:rows, j, g, :, :], k_in[:, g, :].unsqueeze(1).broadcast_to([rows, 2, HD]),
                            rk[:, g:g + 1].unsqueeze(2).broadcast_to([rows, 2, HD]), ALU.mult)
                        if g == KV - 1:
                            last.then_inc(post, 1)

            def post_full(c, j):
                i = 2 * c + j
                dve.wait_ge(cs_in[j], 16 * (c + 1))
                v = m.v_st[:, ds(i, 1), :, :].rearrange("p a g n -> p (a g) n")
                post_tile(i + 1, P, j, 0, v[:, :, HD:], v[:, :, 0:HD], cs[:, j])
                dve.wait_ge(q_store[j], 16 * (c + 1))
                dve.tensor_tensor(q_out[:, j, :].rearrange("p (h n) -> p h n", n=HD),
                                  t1[:, 0:DA].rearrange("p (h n) -> p h n", n=HD),
                                  rsh[:, 0:HEADS].unsqueeze(2).broadcast_to([P, HEADS, HD]), ALU.mult).then_inc(post, 1)

            dve.wait_ge(const_in, 96)
            norm(1, xn_meta[:], x_meta[:], META, 2)
            dve.wait_ge(t_done, 1)
            dve.tensor_tensor(hm[:], ps[:, 1, 0:KT * META].rearrange("p (k n) -> p k n", k=KT),
                              g_in[:].unsqueeze(2).broadcast_to([P, KT, META]), ALU.mult).then_inc(hm_done, 1)
            dve.wait_ge(h_hi_done, 1)
            dve.tensor_tensor(hm_lo[:], hm[:], hm_hi[:].bitcast(F32), ALU.subtract).then_inc(h_lo_done, 1)
            for j in range(CT):
                norm_tile(0, j)
            for k in range(KT):
                dve.wait_ge(w_hi_done, k + 1)
                dve.tensor_tensor(win_lo[:, k, :], w_stage[:, k % 2, :], win_hi[:, k, :].bitcast(F32),
                                  ALU.subtract).then_inc(w_lo_done, 1)
            post_tile(0, META, 1, HEADS, m.v_st[0:META, NT, :, HD:], m.v_st[0:META, NT, :, 0:HD], cs_meta)
            h_evac(0)
            dve.wait_ge(k_hi_done, 1)
            lo = m.k_st[HD:P, :, SEQ:L]
            dve.tensor_tensor(lo, ps[HD:P, 0, 0:KV * META].rearrange("p (g n) -> p g n", g=KV),
                              lo.bitcast(F32), ALU.subtract).then_inc(k_lo_done, 1)
            with dve.Fori(0, NCH - 1) as c:
                for j in range(CT):
                    post_full(c, j)
                    norm_tile(c + 1, j)
                h_evac(c + 1)
                k_evac(c)
            for j in range(CT):
                post_full(NCH - 1, j)
            k_evac(NCH - 1)

        @block.tensor
        def _(pe):
            pe.wait_ge(const_in, 96)
            pe.wait_ge(xn_done, 1)
            for k in range(KT):
                last = pe.transpose(ps[:, 1, k * META:(k + 1) * META], xn_meta[:, k * P:(k + 1) * P],
                                    ident[0:META, 0:META])
            last.then_inc(t_done, 1)
            pe.wait_ge(h_lo_done, 2)
            pe.wait_ge(w_lo_done, KT)
            for f in range(GROUPS):
                w = slice(U0 + f * P, U0 + (f + 1) * P)
                for k in range(KT):
                    last = matmul3(pe, ps[:, 2 + f, 0:META], win_hi[:, k, w], win_lo[:, k, w],
                                   hm_hi[:, k, :], hm_lo[:, k, :], k == 0, k == KT - 1)
            last.then_inc(u_done, 1)
            for k in range(KT):
                last = matmul3(pe, ps[0:META, 7, 0:2 * DKV], hm_hi[:, k, :], hm_lo[:, k, :],
                               win_hi[:, k, DA:U0], win_lo[:, k, DA:U0], k == 0, k == KT - 1)
            last.then_inc(kv_done, 1)

            def h_transpose(c, k):
                pe.wait_ge(h_lo_done, 8 * c + k + 1)
                if k < 2:
                    pe.wait_ge(k_lo_done, 2 * c + 1)
                for j in range(CT):
                    last = pe.transpose(ps[:, k % 2, j * P:(j + 1) * P], xn[:, j, k * P:(k + 1) * P], ident[:])
                last.then_inc(t_done, 1)

            def u_products(c, k):
                pe.wait_ge(h_lo_done, 8 * c + k + 3)
                if k == 0:
                    pe.wait_ge(u_evac, 4 * c + 1)
                for f in range(GROUPS):
                    w = slice(U0 + f * P, U0 + (f + 1) * P)
                    last = matmul3(pe, ps[:, 2 + f, 0:CW], win_hi[:, k, w], win_lo[:, k, w],
                                   hT_hi[:, k, :], hT_lo[:, k, :], k == 0, k == KT - 1)
                    if k == KT - 1:
                        last.then_inc(u_done, 1)

            def k_transpose(c):
                for g in range(KV):
                    for j in range(CT):
                        last = pe.transpose(ps[:, g, j * P:(j + 1) * P],
                                            k_tok[:, j, g, :, :].rearrange("p a n -> p (a n)"), ident[:])
                    last.then_inc(kt_done, 1)

            def qkv_products(c):
                for j in range(CT):
                    t = slice(j * P, (j + 1) * P)
                    pe.wait_ge(q_evac, 2 * c + j + 1)
                    for k in range(KT):
                        last = matmul3(pe, ps[:, 6, :], hT_hi[:, k, t], hT_lo[:, k, t],
                                       win_hi[:, k, 0:DA], win_lo[:, k, 0:DA], k == 0, k == KT - 1)
                    last.then_inc(q_done, 1)
                    pe.wait_ge(kv_evac, 2 * c + j + 1)
                    for k in range(KT):
                        last = matmul3(pe, ps[:, 7, 0:2 * DKV], hT_hi[:, k, t], hT_lo[:, k, t],
                                       win_hi[:, k, DA:U0], win_lo[:, k, DA:U0], k == 0, k == KT - 1)
                    last.then_inc(kv_done, 1)

            def h_and_u(c):
                pe.wait_ge(xn_done, 2 * c + 3)
                for k in range(KT):
                    h_transpose(c, k)
                    if k:
                        u_products(c, k - 1)
                u_products(c, KT - 1)

            h_and_u(0)
            pe.wait_ge(post, POST)
            for g in range(KV):
                last = pe.transpose(ps[:, 0, g * META:(g + 1) * META],
                                    k_tok[0:META, 1, g, :, :].rearrange("p a n -> p (a n)"), ident[0:META, 0:META])
            last.then_inc(kt_done, 1)
            qkv_products(0)
            with pe.Fori(1, NCH) as c:
                h_and_u(c)
                pe.wait_ge(post, 2 * POST * c + POST - 1)
                k_transpose(c - 1)
                qkv_products(c)
            pe.wait_ge(post, 2 * POST * NCH + POST - 1)
            k_transpose(NCH - 1)


def attend(nc, m):
    PAIRS = HEADS // 2
    STEPS = NT * PAIRS
    HALF = 1024
    SCALE = HD ** -0.5
    POS = {(0, 0): 0, (0, 1): 1, (0, 2): 2, (0, 3): 3, (1, 0): 4, (1, 1): 5, "q": 6, (1, 2): 7, (1, 3): 8, "tail": 9}
    with ExitStack() as ctx:
        sb = lambda n, s, d=F32: ctx.enter_context(nc.sbuf_tensor(n, s, d))
        sem = lambda n: ctx.enter_context(nc.semaphore(n))
        ident, ps = m.ident, m.ps
        q_raw = sb("q_raw", [P, HEADS, 2, HD])
        q_hi = sb("q_hi", [P, 2, 2, P], F32R)
        q_lo = sb("q_lo", [P, 2, 2, P], F32R)
        probs = [[sb(f"probs{a}{u}", [P, L]) for u in range(2)] for a in range(2)]
        pT_hi = sb("pT_hi", [P, 2, NKT, 2 * P], F32R)
        pT_lo = sb("pT_lo", [P, 2, NKT, 2 * P], F32R)
        oT = sb("oT", [P, 2 * P])
        o_out = sb("o_out", [P, 2, P])
        mx = sb("mx", [P, 2, 2, 2])
        nmx = sb("nmx", [P, 2, 2])
        sums = sb("sums", [P, 2, 2, 2])
        den = sb("den", [P, 2])
        rden = sb("rden", [P, PAIRS, 2])
        two_eye = sb("two_eye", [P, HD])

        u_sb = sb("u_sb", [P, GROUPS, UPAD])
        pool_ab = [sb(f"pool_ab{j}", [P, UPAD]) for j in range(2)]
        corr = sb("corr", [P, GROUPS, 8])

        u_in, chain, d_store = sem("a_u_in"), sem("a_chain"), sem("a_d_store")
        eye_in = sem("a_eye_in")
        q_in, o_store = sem("a_q_in"), [sem(f"a_o_store{j}") for j in range(2)]
        s_done, mx_done, nmx_done, exp_done = sem("a_s_done"), sem("a_mx_done"), sem("a_nmx_done"), sem("a_exp_done")
        t_done, hi_done, lo_done = sem("a_t_done"), sem("a_hi_done"), sem("a_lo_done")
        pv_done, oT_done, ot_done, o_done = sem("a_pv_done"), sem("a_oT_done"), sem("a_ot_done"), sem("a_o_done")
        den_done, rden_done = sem("a_den_done"), sem("a_rden_done")
        scores = ps[:, 0:5, :].rearrange("p b n -> p (b n)")
        PV, T0 = 5, 6

        def group_index(s, pos):
            return 10 * s - 8 + pos

        block = ctx.enter_context(nc.Block())

        @block.sync
        def _(sp):
            for a in range(2):
                sp.dma_start(two_eye[a * HD:(a + 1) * HD, :], m.ident_in[0:HD, 0:HD]).then_inc(eye_in, 16)
            sp.dma_start(u_sb[:, :, 0:L], m.u_d.rearrange("g p n -> p g n")).then_inc(u_in, 16)
            sp.dma_start(corr[:], m.corr_in).then_inc(u_in, 16)

            def load_q(qt):
                src = m.q_d[ds(qt * P, P)].rearrange("p (h n) -> p h n", n=HD)
                for a in range(2):
                    sp.dma_start(q_raw[:, :, a, :], src).then_inc(q_in, 16)

            def tile(qt, following):
                sp.wait_ge(t_done, 40 * qt + group_index(2, POS["q"]) + 1)
                load_q(following)
                for p in range(PAIRS):
                    sp.wait_ge(o_done, qt * PAIRS + p + 1)
                    sp.dma_start(m.o_d[ds(qt * P, P), p * P:(p + 1) * P], o_out[:, p % 2, :]).then_inc(o_store[p % 2], 16)

            for j in range(2):
                sp.sem_inc(o_store[j], 16)
            load_q(0)
            with sp.Fori(0, NT - 1) as qt:
                tile(qt, qt + 1)
            tile(NT - 1, NT - 1)
            for j in range(2):
                sp.wait_ge(o_store[j], 16 * (2 * NT + 1))

        @block.gpsimd
        def _(pool):
            pooling_windows(pool, u_sb, pool_ab, corr, u_in, chain)
            pool.dma_start(m.d_d.rearrange("g p n -> p g n"), u_sb[:, :, META:L]).then_inc(d_store, 16)
            pool.wait_ge(d_store, 16)

        def q_group(s):
            return (s + 1) if s == 0 else group_index(s, POS["q"])

        @block.tensor
        def _(pe):
            def q_transpose(pn, slot, index, bank):
                for u in range(2):
                    last = pe.transpose(ps[:, T0 + bank, u * P:(u + 1) * P],
                                        q_raw[:, 2 * pn + u, :, :].rearrange("p a n -> p (a n)"), ident[:])
                last.then_inc(t_done, 1)

            def score(s, p, u, first):
                g = p // 2
                for half in range(2):
                    if not first:
                        pe.wait_ge(exp_done, 4 * s + 2 * u + half - 1)
                    last_col = HALF * (half + 1) if half == 0 else L
                    for c0 in range(HALF * half, last_col, 512):
                        w = min(512, last_col - c0)
                        keys = m.k_st[:, g, c0:c0 + w]
                        pe.matmul(scores[:, c0:c0 + w], q_hi[:, p % 2, u, :], keys, start=True, stop=False)
                        last = pe.matmul(scores[:, c0:c0 + w], q_lo[:, p % 2, u, :], keys, start=False, stop=True)
                    last.then_inc(s_done, 1)

            def transpose_group(s, p, u, g):
                pos = POS[(u, g)]
                pe.wait_ge(lo_done, group_index(s, pos) - 1)
                pe.wait_ge(exp_done, 4 * s - 4 + 2 * u + g // 2 + 1)
                src = probs[(p + 1) % 2][u]
                for t in range(4):
                    kt = 4 * g + t
                    last = pe.transpose(ps[:, T0 + pos % 2, t * P:(t + 1) * P], src[:, kt * P:(kt + 1) * P], ident[:])
                last.then_inc(t_done, 1)

            def transpose_tail(s, p):
                pos = POS["tail"]
                pe.wait_ge(lo_done, group_index(s, pos) - 1)
                for u in range(2):
                    last = pe.transpose(ps[0:META, T0 + pos % 2, u * P:(u + 1) * P],
                                        probs[(p + 1) % 2][u][:, SEQ:L], ident[:])
                last.then_inc(t_done, 1)

            def values(s, p, k0, k1):
                slot, g = p % 2, ((p + 2) % 4) // 2
                for kt in range(k0, k1):
                    rows = P if kt < NT else META
                    for part in (pT_hi, pT_lo):
                        last = pe.matmul(ps[:, PV, 0:2 * P], m.v_st[0:rows, kt, g, :], part[0:rows, slot, kt, :],
                                         start=(kt == 0 and part is pT_hi), stop=(kt == NKT - 1 and part is pT_lo))
                if k1 == NKT:
                    last.then_inc(pv_done, 1)

            def step(s, p, n=99, score_on=True):
                t_on = n >= 1 and n <= 64 or n == 99
                v_on = n >= 2 and n <= 65 or n == 99
                o_on = n >= 3
                for u in range(2):
                    if t_on:
                        transpose_group(s, p, u, 0)
                        transpose_group(s, p, u, 1)
                    if score_on:
                        if u == 0:
                            pe.wait_ge(lo_done, n + 1 if n <= 1 else 10 * s - 11)
                        score(s, p, u, n == 0 and u == 0)
                    if u == 0 and o_on:
                        pe.wait_ge(oT_done, s - 2)
                        for h in range(2):
                            last = pe.matmul(ps[:, PV, 2 * P + h * HD:2 * P + (h + 1) * HD], oT[:, h * P:(h + 1) * P],
                                             two_eye[:], start=True, stop=True)
                        last.then_inc(ot_done, 1)
                    if u == 1 and score_on:
                        if n == 0:
                            q_transpose(1, 1, 1, 1)
                        else:
                            pe.wait_ge(lo_done, group_index(s, POS["q"]) - 1)
                            if p == PAIRS - 1:
                                pe.wait_ge(q_in, 8 * s + 40)
                            q_transpose((p + 1) % 4, (p + 1) % 2, None, 0)
                    if u == 0 and v_on:
                        pe.wait_ge(lo_done, 10 * s - 8 if n != 65 else group_index(64, 9))
                        if o_on:
                            pe.wait_ge(o_done, s - 2)
                        values(s, p, 0, 5)
                    elif v_on:
                        values(s, p, 9, 13)
                    if t_on:
                        transpose_group(s, p, u, 2)
                    if v_on:
                        values(s, p, 5 if u == 0 else 13, 9 if u == 0 else NKT)
                    if t_on:
                        transpose_group(s, p, u, 3)
                        if u == 1:
                            transpose_tail(s, p)

            pe.wait_ge(eye_in, 32)
            pe.wait_ge(q_in, 32)
            q_transpose(0, 0, 0, 0)
            for n in range(PAIRS):
                step(n, n, n)
            with pe.Fori(1, NT) as qt:
                for p in range(PAIRS):
                    step(4 * qt + p, p)
            for n in range(STEPS, STEPS + 3):
                step(n, n % PAIRS, n, score_on=False)

        def drain_positions(n):
            if n == 0:
                return [[], ["q0"]]
            if n == STEPS:
                return [[0, 1, 2, 3], [4, 5, 7, 8, 9]]
            return [[0, 1, 2, 3], [4, 5, 6, 7, 8, 9]] if n < STEPS or n == 99 else [[], []]

        def bank_views(p, pos, s):
            if pos == "q0":
                src = ps[:, T0 + 1, 0:2 * P].rearrange("p (u n) -> p u n", u=2)
                return src, q_hi[:, 1], q_lo[:, 1]
            bank = T0 + pos % 2
            slot = (p + 1) % 2
            if pos == POS["q"]:
                src = ps[:, bank, 0:2 * P].rearrange("p (u n) -> p u n", u=2)
                return src, q_hi[:, (p + 1) % 2], q_lo[:, (p + 1) % 2]
            if pos == POS["tail"]:
                return ps[0:META, bank, 0:2 * P], pT_hi[0:META, slot, NT, :], pT_lo[0:META, slot, NT, :]
            u, g = [k for k, v in POS.items() if v == pos][0]
            src = ps[:, bank, :].rearrange("p (t n) -> p t n", t=4)
            cols = (slice(None), slot, slice(4 * g, 4 * g + 4), slice(u * P, (u + 1) * P))
            return src, pT_hi[cols], pT_lo[cols]

        def group_number(s, pos, n):
            if pos == "q0":
                return 1
            return group_index(s, pos) - (1 if n == STEPS and pos > 6 else 0)

        @block.scalar
        def _(act):
            def hi(s, p, pos, n):
                i = group_number(s, pos, n)
                act.wait_ge(t_done, i + 1)
                src, hi_, _ = bank_views(p, pos, s)
                split_hi(act, hi_, src).then_inc(hi_done, 1)

            def exps(s, p, u, half):
                act.wait_ge(nmx_done, 2 * s + u + 1)
                a, b = (0, HALF) if half == 0 else (HALF, L)
                act.activation(probs[p % 2][u][:, a:b], scores[:, a:b], ACT.Exp, scale=SCALE,
                               bias=nmx[:, p % 2, u:u + 1],
                               accum_out=sums[:, p % 2, half, u:u + 1]).then_inc(exp_done, 1)

            def step(s, p, n=99):
                if n >= 3:
                    act.wait_ge(pv_done, s - 2)
                    act.copy(oT[:], ps[:, PV, 0:2 * P]).then_inc(oT_done, 1)
                halves = drain_positions(n)
                on = n < STEPS or n == 99
                for u in range(2):
                    left = list(halves[u])
                    for _ in range(2):
                        if left and n != 0:
                            hi(s, p, left.pop(0), n)
                    if on:
                        exps(s, p, u, 0)
                    for _ in range(2 if u else 1):
                        if left:
                            hi(s, p, left.pop(0), n)
                    if on:
                        exps(s, p, u, 1)
                    for pos in left:
                        hi(s, p, pos, n)

            act.wait_ge(t_done, 1)
            split_hi(act, q_hi[:, 0], ps[:, T0, 0:2 * P].rearrange("p (u n) -> p u n", u=2)).then_inc(hi_done, 1)
            for n in range(PAIRS):
                step(n, n, n)
            with act.Fori(1, NT) as qt:
                for p in range(PAIRS):
                    step(4 * qt + p, p)
            for n in range(STEPS, STEPS + 3):
                step(n, n % PAIRS, n)

        @block.vector
        def _(dve):
            def lo(s, p, pos, n):
                i = group_number(s, pos, n)
                dve.wait_ge(hi_done, i + 1)
                src, hi_, lo_ = bank_views(p, pos, s)
                dve.tensor_tensor(lo_, src, hi_.bitcast(F32), ALU.subtract).then_inc(lo_done, 1)

            def maxima(s, p, u):
                for half, (a, b) in enumerate(((0, HALF), (HALF, L))):
                    dve.wait_ge(s_done, 4 * s + 2 * u + half + 1)
                    dve.tensor_reduce(mx[:, p % 2, u, half:half + 1], scores[:, a:b], AX.X, ALU.max).then_inc(mx_done, 1)
                dve.wait_ge(mx_done, 4 * s + 2 * u + 2)
                dve.tensor_scalar(nmx[:, p % 2, u:u + 1], mx[:, p % 2, u, 0:1], mx[:, p % 2, u, 1:2], -SCALE,
                                  ALU.max, ALU.mult).then_inc(nmx_done, 1)

            def step(s, p, n=99):
                halves = drain_positions(n)
                on = n < STEPS or n == 99
                for u in range(2):
                    if on:
                        maxima(s, p, u)
                    if u == 0 and (1 <= n <= STEPS or n == 99):
                        q = (p + 3) % 4
                        dve.wait_ge(exp_done, 4 * s)
                        dve.tensor_tensor(den[:], sums[:, q % 2, 0, :], sums[:, q % 2, 1, :], ALU.add).then_inc(den_done, 1)
                        dve.wait_ge(den_done, s)
                        dve.reciprocal(rden[:, q, :], den[:]).then_inc(rden_done, 1)
                    left = list(halves[u])
                    if left and n != 0:
                        lo(s, p, left.pop(0), n)
                    if u == 0 and n >= 3:
                        q = (p + 1) % 4
                        dve.wait_ge(ot_done, s - 2)
                        dve.wait_ge(o_store[q % 2], 8 * (s - 3) + (16 if q % 2 == 0 else 8))
                        dve.wait_ge(rden_done, s - 2)
                        for h in range(2):
                            last = dve.tensor_scalar(o_out[:, q % 2, h * HD:(h + 1) * HD],
                                                     ps[:, PV, 2 * P + h * HD:2 * P + (h + 1) * HD],
                                                     rden[:, q, h:h + 1], None, ALU.mult)
                        last.then_inc(o_done, 1)
                    for pos in left:
                        lo(s, p, pos, n)

            dve.wait_ge(hi_done, 1)
            dve.tensor_tensor(q_lo[:, 0], ps[:, T0, 0:2 * P].rearrange("p (u n) -> p u n", u=2),
                              q_hi[:, 0].bitcast(F32), ALU.subtract).then_inc(lo_done, 1)
            for n in range(PAIRS):
                step(n, n, n)
            with dve.Fori(1, NT) as qt:
                for p in range(PAIRS):
                    step(4 * qt + p, p)
            for n in range(STEPS, STEPS + 3):
                step(n, n % PAIRS, n)


def pooling_windows(pool, u, pool_ab, corr, u_in, chain):
    n = [0]

    def link(ins):
        n[0] += 1
        ins.then_inc(chain, 1)
        pool.wait_ge(chain, n[0])

    link(pool.memset(u[:, :, L:UPAD], 0.0))
    pool.wait_ge(u_in, 32)
    for g, w in enumerate(WINDOWS):
        src, have = u[:, g, :], 1
        reach = w // 2
        while have < w:
            have *= 2
            h = have // 2
            ahead = reach - have // 2
            a, b = META - ahead, L + ahead
            dst = pool_ab[(have.bit_length() + g) % 2]
            before, behind = (1, 0) if have == 2 else (h // 2, h // 2)
            link(pool.tensor_tensor(dst[:, a:b], src[:, a - before:b - before], src[:, a + behind:b + behind], ALU.add))
            src = dst
        link(pool.tensor_scalar(src[:, META:L], src[:, META:L], 1.0 / w, 1.0, ALU.mult, ALU.mult))
        link(pool.tensor_tensor(src[:, L - 8:L], src[:, L - 8:L], corr[:, g, :], ALU.mult))
        link(pool.tensor_tensor(u[:, g, META:L], src[:, META:L], u[:, g, META:L], ALU.subtract))


def mix(nc, m, x, w_pool, w_out, attn_norm, pool_scale):
    with ExitStack() as ctx:
        sb = lambda n, s, d=F32: ctx.enter_context(nc.sbuf_tensor(n, s, d))
        sem = lambda n: ctx.enter_context(nc.semaphore(n))
        ident, ps, eps = m.ident, m.ps, m.eps
        wo_hi = sb("wo_hi", [P, KT, D], F32R)
        wo_lo = sb("wo_lo", [P, KT, D], F32R)
        wp_hi = sb("wp_hi", [P, GROUPS, P], F32R)
        wp_lo = sb("wp_lo", [P, GROUPS, P], F32R)
        stage = sb("stage", [P, 2, D])
        d_raw = sb("d_raw", [P, GROUPS, CW])
        d_hi = sb("d_hi", [P, GROUPS, CW], F32R)
        d_lo = sb("d_lo", [P, GROUPS, CW], F32R)
        o_raw = sb("o_raw", [P, CT, DA])
        mt = sb("mt", [P, CT, D])
        mT_hi = sb("mT_hi", [P, KT, CW], F32R)
        mT_lo = sb("mT_lo", [P, KT, CW], F32R)
        x_res = sb("x_res", [P, CT, D])
        g_mix = sb("g_mix", [P, KT])
        ss = sb("mss", [P, CT, 2])
        sd = sb("msd", [P, CT, 2])
        rs = sb("mrs", [P, CT, 2])

        const_in, d_in = sem("m_const_in"), sem("m_d_in")
        w_staged = [sem(f"m_w_staged{j}") for j in range(2)]
        w_hi_done, w_lo_done = sem("m_w_hi_done"), sem("m_w_lo_done")
        o_in = [sem(f"m_o_in{j}") for j in range(CT)]
        x_in = [sem(f"m_x_in{j}") for j in range(CT)]
        x_store = [sem(f"m_x_store{j}") for j in range(CT)]
        d_hi_done, d_lo_done, y_done = sem("m_d_hi_done"), sem("m_d_lo_done"), sem("m_y_done")
        ssq_done, sd_done, rs_done, mt_done = sem("m_ssq_done"), sem("m_sd_done"), sem("m_rs_done"), sem("m_mt_done")
        t_done, hi_done, lo_done = sem("m_t_done"), sem("m_hi_done"), sem("m_lo_done")
        out_done, res_done = sem("m_out_done"), sem("m_res_done")

        block = ctx.enter_context(nc.Block())

        @block.sync
        def _(sp):
            for dst, src in (
                (g_mix[:, 0:4], attn_norm),
                (g_mix[:, 4:8], pool_scale),
            ):
                sp.dma_start(dst, src).then_inc(const_in, 16)
            sp.dma_start(stage[:, 0, 0:DP].rearrange("p (g n) -> p g n", g=GROUPS),
                         w_pool.rearrange("g p n -> p g n")).then_inc(w_staged[0], 16)
            sp.dma_start(d_raw[:], m.d_d[:, :, 0:CW].rearrange("g p n -> p g n")).then_inc(d_in, 16)
            for j in range(CT):
                sp.dma_start(o_raw[:, j, :], m.o_d[j * P:(j + 1) * P]).then_inc(o_in[j], 16)
            for k in range(KT):
                if k >= 1:
                    sp.wait_ge(w_lo_done, k)
                sp.dma_start(stage[:, (k + 1) % 2, :], w_out[k * P:(k + 1) * P]).then_inc(w_staged[(k + 1) % 2], 16)

            def store(c):
                for j in range(CT):
                    sp.wait_ge(res_done, 2 * c + j + 3)
                    sp.dma_start(m.x2_d[ds(c * CW + j * P, P)], x_res[:, j, :]).then_inc(x_store[j], 16)

            with sp.Fori(1, NCH) as c:
                sp.wait_ge(d_lo_done, c)
                sp.dma_start(d_raw[:], m.d_d[:, :, ds(c * CW, CW)].rearrange("g p n -> p g n")).then_inc(d_in, 16)
                for j in range(CT):
                    sp.wait_ge(mt_done, 2 * c + j - 1)
                    sp.dma_start(o_raw[:, j, :], m.o_d[ds(c * CW + j * P, P)]).then_inc(o_in[j], 16)
                store(c - 1)
            store(NCH - 1)
            for j in range(CT):
                sp.wait_ge(x_store[j], 16 * (NCH + 1))

        @block.gpsimd
        def _(pool):
            for j in range(CT):
                pool.sem_inc(x_store[j], 16)
            with pool.Fori(0, NCH) as c:
                for j in range(CT):
                    pool.wait_ge(x_store[j], 16 * (c + 1))
                    pool.dma_start(x_res[:, j, :], x[ds(c * CW + j * P, P)]).then_inc(x_in[j], 16)

        @block.scalar
        def _(act):
            def split_d(c):
                act.wait_ge(y_done, 2 * c + 1)
                act.wait_ge(d_in, 16 * (c + 1))
                split_hi(act, d_hi[:], d_raw[:]).then_inc(d_hi_done, 1)

            def norm_tile(c, j):
                i = 2 * c + j
                act.wait_ge(o_in[j], 16 * (c + 1))
                act.wait_ge(t_done, 8 * c + 1)
                act.activation(mt[:, j, 0:DA], o_raw[:, j, :], ACT.Square, accum_out=ss[:, j, 0:1]).then_inc(ssq_done, 1)
                act.wait_ge(y_done, i + 2)
                act.activation(mt[:, j, DA:], ps[:, j, :], ACT.Square, accum_out=ss[:, j, 1:2]).then_inc(ssq_done, 1)
                act.wait_ge(ssq_done, 2 * i + 2)
                act.activation(sd[:, j, :], ss[:, j, :], ACT.Sqrt, scale=1.0 / DA, bias=eps[:]).then_inc(sd_done, 1)

            def evac(c):
                for k in range(KT):
                    act.wait_ge(t_done, 8 * c + k + 2)
                    split_hi(act, mT_hi[:, k, :], ps[:, 2 + k % 2, 0:CW], g_mix[:, k:k + 1]).then_inc(hi_done, 1)

            act.sem_inc(y_done, 1)
            act.sem_inc(t_done, 1)
            act.wait_ge(const_in, 32)
            act.wait_ge(w_staged[0], 16)
            split_hi(act, wp_hi[:], stage[:, 0, 0:DP].rearrange("p (g n) -> p g n", g=GROUPS)).then_inc(w_hi_done, 1)
            split_d(0)
            for j in range(CT):
                norm_tile(0, j)
            for k in range(KT):
                act.wait_ge(w_staged[(k + 1) % 2], 16 * ((k + 1) // 2 + 1))
                split_hi(act, wo_hi[:, k, :], stage[:, (k + 1) % 2, :]).then_inc(w_hi_done, 1)
            with act.Fori(0, NCH - 1) as c:
                evac(c)
                split_d(c + 1)
                for j in range(CT):
                    norm_tile(c + 1, j)
            evac(NCH - 1)

        @block.vector
        def _(dve):
            def split_d(c):
                dve.wait_ge(d_hi_done, c + 1)
                dve.tensor_tensor(d_lo[:], d_raw[:], d_hi[:].bitcast(F32),
                                  ALU.subtract).then_inc(d_lo_done, 1)

            def norm_tile(c, j):
                i = 2 * c + j
                dve.wait_ge(sd_done, i + 1)
                dve.reciprocal(rs[:, j, :], sd[:, j, :]).then_inc(rs_done, 1)
                dve.wait_ge(rs_done, i + 1)
                dve.tensor_scalar(mt[:, j, 0:DA], o_raw[:, j, :], rs[:, j, 0:1], None, ALU.mult)
                dve.tensor_scalar(mt[:, j, DA:], ps[:, j, :], rs[:, j, 1:2], None, ALU.mult).then_inc(mt_done, 1)

            def evac(c):
                for k in range(KT):
                    dve.wait_ge(hi_done, 8 * c + k + 1)
                    dve.scalar_tensor_tensor(mT_lo[:, k, :], ps[:, 2 + k % 2, 0:CW], g_mix[:, k:k + 1],
                                             mT_hi[:, k, :].bitcast(F32), ALU.mult, ALU.subtract).then_inc(lo_done, 1)

            def residual(c, j):
                dve.wait_ge(out_done, 2 * c + j + 1)
                dve.wait_ge(x_in[j], 16 * (c + 1))
                dve.tensor_tensor(x_res[:, j, :], ps[:, 4 + 2 * j:6 + 2 * j, :].rearrange("p b n -> p (b n)"),
                                  x_res[:, j, :], ALU.add).then_inc(res_done, 1)

            dve.sem_inc(lo_done, 2)
            dve.sem_inc(res_done, 2)
            dve.wait_ge(const_in, 32)
            dve.wait_ge(w_hi_done, 1)
            dve.tensor_tensor(wp_lo[:], stage[:, 0, 0:DP].rearrange("p (g n) -> p g n", g=GROUPS),
                              wp_hi[:].bitcast(F32), ALU.subtract).then_inc(w_lo_done, 1)
            split_d(0)
            for j in range(CT):
                norm_tile(0, j)
            for k in range(KT):
                dve.wait_ge(w_hi_done, k + 2)
                dve.tensor_tensor(wo_lo[:, k, :], stage[:, (k + 1) % 2, :], wo_hi[:, k, :].bitcast(F32),
                                  ALU.subtract).then_inc(w_lo_done, 1)
            with dve.Fori(0, NCH - 1) as c:
                evac(c)
                split_d(c + 1)
                residual(c, 0)
                for j in range(CT):
                    norm_tile(c + 1, j)
                residual(c, 1)
            evac(NCH - 1)
            residual(NCH - 1, 0)
            residual(NCH - 1, 1)

        @block.tensor
        def _(pe):
            def pool_map(c, j):
                t = slice(j * P, (j + 1) * P)
                if j == 0:
                    pe.wait_ge(d_lo_done, c + 1)
                for g in range(GROUPS):
                    last = matmul3(pe, ps[:, j, g * P:(g + 1) * P], d_hi[:, g, t], d_lo[:, g, t],
                                   wp_hi[:, g, :], wp_lo[:, g, :], True, True)
                last.then_inc(y_done, 1)

            def transposes(c):
                pe.wait_ge(mt_done, 2 * c + 2)
                for k in range(KT):
                    pe.wait_ge(lo_done, 8 * c + k + 1)
                    for j in range(CT):
                        last = pe.transpose(ps[:, 2 + k % 2, j * P:(j + 1) * P], mt[:, j, k * P:(k + 1) * P], ident[:])
                    last.then_inc(t_done, 1)

            def project_out(c, j):
                t = slice(j * P, (j + 1) * P)
                pe.wait_ge(res_done, 2 * c + j + 1)
                for half in range(2):
                    w = slice(half * 512, (half + 1) * 512)
                    for k in range(KT):
                        if j == 0 and half == 0:
                            pe.wait_ge(lo_done, 8 * c + k + 3)
                        last = matmul3(pe, ps[:, 4 + 2 * j + half, :], mT_hi[:, k, t], mT_lo[:, k, t],
                                       wo_hi[:, k, w], wo_lo[:, k, w], k == 0, k == KT - 1)
                last.then_inc(out_done, 1)

            for j in range(CT):
                pool_map(0, j)
            pe.wait_ge(w_lo_done, KT + 1)
            with pe.Fori(0, NCH - 1) as c:
                transposes(c)
                project_out(c, 0)
                for j in range(CT):
                    pool_map(c + 1, j)
                project_out(c, 1)
            transposes(NCH - 1)
            project_out(NCH - 1, 0)
            project_out(NCH - 1, 1)


def feed(nc, m, w_ffn_in, w_ffn_down, norm_ffn, norm_final, out):
    UP_PAIRS, DOWN_PAIRS = FT, FT // 2
    PAIRS = UP_PAIRS + DOWN_PAIRS
    with ExitStack() as ctx:
        sb = lambda n, s, d=F32: ctx.enter_context(nc.sbuf_tensor(n, s, d))
        sem = lambda n: ctx.enter_context(nc.semaphore(n))
        ident, ps, eps = m.ident, m.ps, m.eps
        x2 = sb("x2", [P, FC, D])
        hT_hi = sb("fT_hi", [P, KT, FW], F32R)
        hT_lo = sb("fT_lo", [P, KT, FW], F32R)
        gu_hi = sb("gu_hi", [P, FT, FW], F32R)
        gu_lo = sb("gu_lo", [P, FT, FW], F32R)
        w_raw = sb("w_raw", [P, 2, D])
        w_hi = sb("w_hi", [P, 2, D], F32R)
        w_lo = sb("w_lo", [P, 2, D], F32R)
        silu = sb("silu", [P, FW])
        gu = sb("gu", [P, FW])
        res = sb("res", [P, FC, D])
        junk = sb("junk", [P, D])
        g_final = sb("g_final", [P, D])
        g_ffn = sb("g_ffn", [P, KT])
        ss = sb("fss", [P, 2, FC])
        sd = sb("fsd", [P, 2, FC])
        rs = sb("frs", [P, 2, FC])

        const_in, x2_in = sem("f_const_in"), sem("f_x2_in")
        w_in = [sem(f"f_w_in{j}") for j in range(2)]
        w_hi_done, w_lo_done, w_used = sem("f_w_hi_done"), sem("f_w_lo_done"), sem("f_w_used")
        ssq_done, sd_done, rs_done, xn_done = sem("f_ssq_done"), sem("f_sd_done"), sem("f_rs_done"), sem("f_xn_done")
        t_done, h_hi_done, h_lo_done = sem("f_t_done"), sem("f_h_hi_done"), sem("f_h_lo_done")
        silu_done, gu_done, gu_hi_done, gu_lo_done = sem("f_silu_done"), sem("f_gu_done"), sem("f_gu_hi_done"), sem("f_gu_lo_done")
        down_done, res_done = sem("f_down_done"), sem("f_res_done")
        res_in = [sem(f"f_res_in{j}") for j in range(FC)]
        out_store = [sem(f"f_out_store{j}") for j in range(FC)]
        fssq_done, fsd_done, frs_done, fin_done = sem("f_fssq_done"), sem("f_fsd_done"), sem("f_frs_done"), sem("f_fin_done")

        block = ctx.enter_context(nc.Block())

        @block.sync
        def _(sp):
            def load(b, slot, src):
                sp.wait_ge(w_lo_done, b + 1)
                sp.dma_start(w_raw[:, slot, :].rearrange("p (k n) -> p k n", n=src.shape[-1]), src).then_inc(w_in[slot], 16)

            w_up = w_ffn_in.rearrange("(k p) n -> p k n", p=P)
            with sp.Fori(0, NFC) as c:
                with sp.Fori(0, UP_PAIRS) as f:
                    for a in range(2):
                        load(2 * PAIRS * c + 2 * f + a, a, w_up[:, :, ds(f * P + a * DFF, P)])
                with sp.Fori(0, DOWN_PAIRS) as i:
                    for a in range(2):
                        load(2 * PAIRS * c + 2 * i + (2 * UP_PAIRS + a), a,
                             w_ffn_down[ds(i * 2 * P + a * P, P)].unsqueeze(1))

        @block.gpsimd
        def _(pool):
            def load_x2(c):
                pool.dma_start(x2[:], m.x2_d[ds(c * FW, FW)].rearrange("(j p) n -> p j n", p=P)).then_inc(x2_in, 16)

            def load_res(c):
                for j in range(FC):
                    pool.wait_ge(out_store[j], 16 * (c + 1))
                    pool.dma_start(res[:, j, :], m.x2_d[ds(c * FW + j * P, P)]).then_inc(res_in[j], 16)

            for j in range(FC):
                pool.sem_inc(out_store[j], 16)
            load_x2(0)
            pool.dma_start(g_ffn[:], norm_ffn).then_inc(const_in, 16)
            pool.dma_start(g_final[:], norm_final.unsqueeze(0).broadcast_to([P, D])).then_inc(const_in, 16)
            with pool.Fori(0, NFC - 1) as c:
                load_res(c)
                pool.wait_ge(t_done, KT * (c + 1))
                load_x2(c + 1)
            load_res(NFC - 1)
            for j in range(FC):
                pool.wait_ge(out_store[j], 16 * (NFC + 1))

        @block.scalar
        def _(act):
            def split(w, slot):
                act.wait_ge(w_in[slot], 16 * w + 16)
                act.wait_ge(w_used, 2 * w + slot + 1)
                split_hi(act, w_hi[:, slot, :], w_raw[:, slot, :]).then_inc(w_hi_done, 1)

            def norm_tile(c, j):
                act.wait_ge(x2_in, 16 * (c + 1))
                act.activation(junk[:], x2[:, j, :], ACT.Square, accum_out=ss[:, 0, j:j + 1]).then_inc(ssq_done, 1)
                act.wait_ge(ssq_done, FC * c + j + 1)
                act.activation(sd[:, 0, j:j + 1], ss[:, 0, j:j + 1], ACT.Sqrt, scale=1.0 / D, bias=eps[:]).then_inc(sd_done, 1)

            def evac(c):
                for k in range(KT):
                    act.wait_ge(t_done, KT * c + k + 1)
                    split_hi(act, hT_hi[:, k, :], ps[:, k % 2, :], g_ffn[:, k:k + 1]).then_inc(h_hi_done, 1)

            def up(c):
                with act.Fori(0, UP_PAIRS) as f:
                    act.wait_ge(w_used, 2 * PAIRS * c + 2 * f + 3)
                    act.activation(silu[:], ps[:, 2, :], ACT.Silu).then_inc(silu_done, 1)
                    split(PAIRS * c + f + 1, 0)
                    act.wait_ge(gu_done, UP_PAIRS * c + f + 2)
                    split_hi(act, gu_hi[:, ds(f, 1), :].rearrange("p a n -> p (a n)"), gu[:]).then_inc(gu_hi_done, 1)
                    split(PAIRS * c + f + 1, 1)

            def down(c, normed):
                cuts = (0, 3, 6, 9, DOWN_PAIRS) if normed else (0, DOWN_PAIRS - 1)
                for j, (a, b) in enumerate(zip(cuts, cuts[1:])):
                    with act.Fori(a, b) as i:
                        for slot in range(2):
                            split(PAIRS * c + i + (UP_PAIRS + 1), slot)
                    if normed:
                        norm_tile(c + 1, j)

            def final(c):
                for j in range(FC):
                    act.wait_ge(res_done, FC * c + j + FC + 1)
                    act.activation(junk[:], res[:, j, :], ACT.Square, accum_out=ss[:, 1, j:j + 1]).then_inc(fssq_done, 1)
                    act.wait_ge(fssq_done, FC * c + j + 1)
                    act.activation(sd[:, 1, j:j + 1], ss[:, 1, j:j + 1], ACT.Sqrt, scale=1.0 / D, bias=eps[:]).then_inc(fsd_done, 1)
                for j in range(FC):
                    act.wait_ge(fin_done, FC * c + j + 1)
                    act.dma_start(out[ds(c * FW + j * P, P)], res[:, j, :]).then_inc(out_store[j], 16)

            act.sem_inc(silu_done, 1)
            act.wait_ge(const_in, 32)
            split(0, 0)
            split(0, 1)
            for j in range(FC):
                norm_tile(0, j)
            evac(0)
            with act.Fori(0, NFC - 1) as c:
                up(c)
                down(c, True)
                evac(c + 1)
                final(c)
            up(NFC - 1)
            down(NFC - 1, False)
            final(NFC - 1)

        @block.vector
        def _(dve):
            def split(w, slot):
                dve.wait_ge(w_hi_done, 2 * w + slot + 1)
                dve.tensor_tensor(w_lo[:, slot, :], w_raw[:, slot, :], w_hi[:, slot, :].bitcast(F32),
                                  ALU.subtract).then_inc(w_lo_done, 1)

            def norm_tile(c, j):
                dve.wait_ge(sd_done, FC * c + j + 1)
                dve.reciprocal(rs[:, 0, j:j + 1], sd[:, 0, j:j + 1]).then_inc(rs_done, 1)
                dve.wait_ge(rs_done, FC * c + j + 1)
                dve.tensor_scalar(x2[:, j, :], x2[:, j, :], rs[:, 0, j:j + 1], None, ALU.mult).then_inc(xn_done, 1)

            def evac(c):
                for k in range(KT):
                    dve.wait_ge(h_hi_done, KT * c + k + 1)
                    dve.scalar_tensor_tensor(hT_lo[:, k, :], ps[:, k % 2, :], g_ffn[:, k:k + 1],
                                             hT_hi[:, k, :].bitcast(F32), ALU.mult, ALU.subtract).then_inc(h_lo_done, 1)

            def up(c):
                with dve.Fori(0, UP_PAIRS) as f:
                    split(PAIRS * c + f + 1, 0)
                    dve.wait_ge(silu_done, UP_PAIRS * c + f + 2)
                    dve.wait_ge(w_used, 2 * PAIRS * c + 2 * f + 4)
                    dve.tensor_tensor(gu[:], silu[:], ps[:, 3, :], ALU.mult).then_inc(gu_done, 1)
                    dve.wait_ge(gu_hi_done, UP_PAIRS * c + f + 1)
                    dve.tensor_tensor(gu_lo[:, ds(f, 1), :].rearrange("p a n -> p (a n)"), gu[:],
                                      gu_hi[:, ds(f, 1), :].rearrange("p a n -> p (a n)").bitcast(F32),
                                      ALU.subtract).then_inc(gu_lo_done, 1)
                    split(PAIRS * c + f + 1, 1)

            def down(c, normed):
                cuts = (0, 3, 6, 9, DOWN_PAIRS) if normed else (0, DOWN_PAIRS - 1)
                for j, (a, b) in enumerate(zip(cuts, cuts[1:])):
                    with dve.Fori(a, b) as i:
                        for slot in range(2):
                            split(PAIRS * c + i + (UP_PAIRS + 1), slot)
                    if normed:
                        norm_tile(c + 1, j)

            def residual(c, j):
                dve.wait_ge(down_done, FC * c + j + 1)
                dve.wait_ge(res_in[j], 16 * (c + 1))
                dve.tensor_tensor(res[:, j, :], ps[:, 2 * j:2 * j + 2, :].rearrange("p b n -> p (b n)"),
                                  res[:, j, :], ALU.add).then_inc(res_done, 1)

            def final(c):
                for j in range(FC):
                    dve.wait_ge(fsd_done, FC * c + j + 1)
                    dve.reciprocal(rs[:, 1, j:j + 1], sd[:, 1, j:j + 1]).then_inc(frs_done, 1)
                    dve.wait_ge(frs_done, FC * c + j + 1)
                    dve.scalar_tensor_tensor(res[:, j, :], res[:, j, :], rs[:, 1, j:j + 1], g_final[:],
                                             ALU.mult, ALU.mult).then_inc(fin_done, 1)

            dve.sem_inc(w_lo_done, 2)
            dve.sem_inc(h_lo_done, 2)
            dve.sem_inc(gu_done, 1)
            dve.sem_inc(res_done, FC)
            dve.wait_ge(const_in, 32)
            split(0, 0)
            split(0, 1)
            for j in range(FC):
                norm_tile(0, j)
            evac(0)
            with dve.Fori(0, NFC - 1) as c:
                up(c)
                down(c, True)
                residual(c, 0)
                residual(c, 1)
                evac(c + 1)
                residual(c, 2)
                residual(c, 3)
                final(c)
            up(NFC - 1)
            down(NFC - 1, False)
            for j in range(FC):
                residual(NFC - 1, j)
            final(NFC - 1)

        @block.tensor
        def _(pe):
            pe.sem_inc(w_used, 2)
            with pe.Fori(0, NFC) as c:
                pe.wait_ge(xn_done, FC * (c + 1))
                pe.wait_ge(res_done, FC * c + 1)
                for k in range(KT):
                    pe.wait_ge(h_lo_done, KT * c + k + 1)
                    if k == KT - 1:
                        pe.wait_ge(res_done, FC * c + 2)
                    for j in range(FC):
                        last = pe.transpose(ps[:, k % 2, j * P:(j + 1) * P], x2[:, j, k * P:(k + 1) * P], ident[:])
                    last.then_inc(t_done, 1)
                with pe.Fori(0, UP_PAIRS) as f:
                    for a in range(2):
                        pe.wait_ge(w_lo_done, 2 * PAIRS * c + 2 * f + a + 3)
                        pe.wait_ge(gu_done if a else silu_done, UP_PAIRS * c + f + 1)
                        for k in range(KT):
                            if a == 0:
                                pe.wait_ge(h_lo_done, KT * c + k + 3)
                            w = slice(k * P, (k + 1) * P)
                            last = matmul3(pe, ps[:, 2 + a, :], w_hi[:, a, w], w_lo[:, a, w],
                                           hT_hi[:, k, :], hT_lo[:, k, :], k == 0, k == KT - 1)
                        last.then_inc(w_used, 1)
                pe.wait_ge(res_done, FC * c + FC)
                for f in range(FT):
                    slot = f % 2
                    pe.wait_ge(w_lo_done, 2 * PAIRS * c + (2 * UP_PAIRS + f + 3))
                    pe.wait_ge(gu_lo_done, UP_PAIRS * c + f + 1)
                    if f == 0:
                        pe.wait_ge(silu_done, UP_PAIRS * c + UP_PAIRS + 1)
                        pe.wait_ge(gu_done, UP_PAIRS * c + UP_PAIRS + 1)
                    for j in range(FC):
                        t = slice(j * P, (j + 1) * P)
                        for half in range(2):
                            w = slice(half * 512, (half + 1) * 512)
                            last = matmul3(pe, ps[:, 2 * j + half, :], gu_hi[:, f, t], gu_lo[:, f, t],
                                           w_hi[:, slot, w], w_lo[:, slot, w], f == 0, f == FT - 1)
                        if f == FT - 1:
                            last.then_inc(down_done, 1)
                    if f < FT - 1:
                        last.then_inc(w_used, 1)
                pe.wait_ge(down_done, FC * (c + 1))
                pe.sem_inc(w_used, 1)


def build(nc, x, meta_tokens, norm_mix, w_in, q_norm, k_norm, attn_out_norm, w_pool, pool_scale, w_out,
          norm_ffn, w_ffn_in, w_ffn_down, norm_final, rope, ident, corr, out):
    m = Shared()
    m.ident_in, m.corr_in = ident, corr
    m.q_d = nc.dram_tensor("q_d", (SEQ, DA), F32).ap()
    m.u_d = nc.dram_tensor("u_d", (GROUPS, P, L), F32).ap()
    m.d_d = nc.dram_tensor("d_d", (GROUPS, P, SEQ), F32).ap()
    m.o_d = nc.dram_tensor("o_d", (SEQ, DA), F32).ap()
    m.x2_d = nc.dram_tensor("x2_d", (SEQ, D), F32).ap()
    with ExitStack() as ctx:
        m.ident = ctx.enter_context(nc.sbuf_tensor("ident", [P, P], F32))
        m.eps = ctx.enter_context(nc.sbuf_tensor("eps", [P, 1], F32))
        m.ps = ctx.enter_context(nc.psum_tensor("ps", [P, 8, 512], F32))
        m.eps_set = ctx.enter_context(nc.semaphore("eps_set"))
        with ExitStack() as kv:
            m.k_st = kv.enter_context(nc.sbuf_tensor("k_st", [P, KV, L], F32R))
            m.v_st = kv.enter_context(nc.sbuf_tensor("v_st", [P, NKT, KV, 2 * HD], F32R))
            project(nc, m, x, meta_tokens, rope, w_in, norm_mix, q_norm, k_norm)
            attend(nc, m)
        mix(nc, m, x, w_pool, w_out, attn_out_norm, pool_scale)
        feed(nc, m, w_ffn_in, w_ffn_down, norm_ffn, norm_final, out)


def shape_tables():
    pairs = HD // 4
    f32 = np.float32
    t = np.arange(SEQ)
    row = (t // GRID_W - SEQ // GRID_W // 2).astype(f32)
    col = (t % GRID_W - GRID_W // 2).astype(f32)
    freqs = f32(ROPE_THETA) ** (-np.arange(pairs, dtype=f32) / f32(pairs))
    ang = np.zeros((L, 2, pairs), f32)
    ang[:SEQ, 0] = row[:, None] * freqs
    ang[:SEQ, 1] = col[:, None] * freqs
    cos, sin = np.cos(ang), np.sin(ang)
    table = np.stack([np.stack([cos, cos], 2), np.stack([-sin, sin], 2)], 1)
    corr = np.ones((P, GROUPS, 8), f32)
    for g, w in enumerate(WINDOWS):
        for i in range(8):
            pos = L - 8 + i
            corr[:, g, i] = w / (min(pos + w // 2, L) - (pos - w // 2))
    return table.reshape(L, 2 * HD).astype(f32), np.eye(P, dtype=f32), corr


def kernel(x, meta_tokens, norm_mix, w_in, q_norm, k_norm, attn_out_norm, w_pool, pool_scale, w_out,
           norm_ffn, w_ffn_in, w_ffn_down, norm_final):
    import concourse.bacc as bacc
    from concourse.bass_utils import run_bass_kernel_spmd

    nc = bacc.Bacc("TRN2", target_bir_lowering=False, num_devices=1)
    rope, ident, corr = shape_tables()
    columns = lambda g: g.reshape(-1, P).T
    given = {
        "x": x[0], "meta_tokens": meta_tokens, "norm_mix": columns(norm_mix[0]), "w_in": w_in[0], "q_norm": q_norm[0],
        "k_norm": k_norm[0], "attn_out_norm": columns(attn_out_norm[0]), "w_pool": w_pool[0], "pool_scale": columns(pool_scale[0]),
        "w_out": w_out[0], "norm_ffn": columns(norm_ffn[0]), "w_ffn_in": w_ffn_in[0], "w_ffn_down": w_ffn_down[0],
        "norm_final": norm_final, "rope": rope, "ident": ident, "corr": corr,
    }
    arrays = {f"in_{k}": np.ascontiguousarray(v) for k, v in given.items()}
    args = [nc.dram_tensor(k, a.shape, mybir.dt.from_np(a.dtype), kind="ExternalInput").ap() for k, a in arrays.items()]
    out = nc.dram_tensor("out_x", (SEQ, D), F32, kind="ExternalOutput").ap()
    build(nc, *args, out)
    r = run_bass_kernel_spmd(nc, [arrays], core_ids=[0])
    return r.results[0]["out_x"].reshape(1, SEQ, D)
```

```python
import math
from contextlib import ExitStack

import numpy as np

import concourse.bass as bass
import concourse.mybir as mybir

F32 = mybir.dt.float32
F32R = mybir.dt.float32r
ACT = mybir.ActivationFunctionType
ALU = mybir.AluOpType
AX = mybir.AxisListType
ds = bass.ds

P = 128
D = 1024
SEQ = 2048
META = 16
GRID_W = 64
HEADS, KV, HD = 8, 2, 64
DA = HEADS * HD
DKV = KV * HD
DP = 512
GROUPS = 4
WINDOWS = (2, 4, 8, 16)
DIN = DA + 2 * DKV + DP
DFF = 2816
EPS = 1e-6
ROPE_THETA = 10000.0

L = META + SEQ
KT = D // P
NT = SEQ // P
CT = 2
CW = CT * P
NCH = NT // CT
U0 = DA + 2 * DKV
NKT = NT + 1
QK = DA + DKV
NH = HEADS + KV
FT = DFF // P
FC = 4
FW = FC * P
NFC = NT // FC


def split_hi(act, hi, src, scale=1.0):
    return act.activation(hi, src, ACT.Copy, scale=scale)


def matmul3(pe, out, st_hi, st_lo, mv_hi, mv_lo, start, stop):
    pe.matmul(out, st_hi, mv_hi, start=start, stop=False)
    pe.matmul(out, st_hi, mv_lo, start=False, stop=False)
    return pe.matmul(out, st_lo, mv_hi, start=False, stop=stop)


class Shared:
    pass


def project(nc, m, x, meta, rope, w_in, norm_mix, q_norm, k_norm):
    with ExitStack() as ctx:
        sb = lambda n, s, d=F32: ctx.enter_context(nc.sbuf_tensor(n, s, d))
        sem = lambda n: ctx.enter_context(nc.semaphore(n))
        ident, ps = m.ident, m.ps
        win_hi = sb("win_hi", [P, KT, DIN], F32R)
        win_lo = sb("win_lo", [P, KT, DIN], F32R)
        x_raw = sb("x_raw", [P, CT, D])
        x_meta = sb("x_meta", [META, D])
        xn = sb("xn", [P, CT, D])
        xn_meta = sb("xn_meta", [META, D])
        hT_hi = sb("hT_hi", [P, KT, CW], F32R)
        hT_lo = sb("hT_lo", [P, KT, CW], F32R)
        hm_hi = sb("hm_hi", [P, KT, META], F32R)
        hm_lo = sb("hm_lo", [P, KT, META], F32R)
        hm = sb("hm", [P, KT, META])
        u_out = sb("u_out", [P, 2, CW])
        w_stage = sb("w_stage", [P, 2, DIN])
        qkv = sb("qkv", [P, CT, QK + DKV])
        sq = sb("sq", [P, QK])
        t1 = sb("t1", [P, QK])
        t2 = sb("t2", [P, QK])
        q_out = sb("q_out", [P, CT, DA])
        k_tok = sb("k_tok", [P, CT, KV, 2, HD])
        cs = sb("cs", [P, CT, 2, HD])
        cs_meta = sb("cs_meta", [META, 2, HD])
        g_in = sb("g_in", [P, KT])
        g_qk = sb("g_qk", [P, 2, HD])
        eps = m.eps
        ssx = sb("ssx", [P, 3])
        sdx = sb("sdx", [P, 3])
        rsx = sb("rsx", [P, 3])
        ssh = sb("ssh", [P, NH])
        sdh = sb("sdh", [P, NH])
        rsh = sb("rsh", [P, NH])

        const_in = sem("p_const_in")
        x_in = [sem(f"p_x_in{j}") for j in range(CT)]
        cs_in = [sem(f"p_cs_in{j}") for j in range(CT)]
        w_staged = [sem(f"p_w_staged{j}") for j in range(2)]
        w_hi_done, w_lo_done = sem("p_w_hi_done"), sem("p_w_lo_done")
        x_ssq, x_sd, x_rs, xn_done = sem("p_x_ssq"), sem("p_x_sd"), sem("p_x_rs"), sem("p_xn_done")
        t_done, h_hi_done, h_lo_done = sem("p_t_done"), sem("p_h_hi_done"), sem("p_h_lo_done")
        hm_done = sem("p_hm_done")
        u_done, u_evac = sem("p_u_done"), sem("p_u_evac")
        u_store = [sem(f"p_u_store{j}") for j in range(2)]
        q_done, q_evac, kv_done, kv_evac = sem("p_q_done"), sem("p_q_evac"), sem("p_kv_done"), sem("p_kv_evac")
        sq_done, gain_done, head_sd, v_hi_done = sem("p_sq_done"), sem("p_gain_done"), sem("p_head_sd"), sem("p_v_hi_done")
        post, qkv_free = sem("p_post"), sem("p_qkv_free")
        q_store = [sem(f"p_q_store{j}") for j in range(CT)]
        kt_done, k_hi_done, k_lo_done = sem("p_kt_done"), sem("p_k_hi_done"), sem("p_k_lo_done")

        POST = 9

        block = ctx.enter_context(nc.Block())

        @block.sync
        def _(sp):
            for dst, src in (
                (ident[:], m.ident_in),
                (x_meta[:], meta),
                (g_in[:], norm_mix),
                (g_qk[:, 0, :], q_norm.unsqueeze(0).broadcast_to([P, HD])),
                (g_qk[:, 1, :], k_norm.unsqueeze(0).broadcast_to([P, HD])),
                (cs_meta[:], rope[SEQ:L].rearrange("p (a n) -> p a n", a=2)),
            ):
                sp.dma_start(dst, src).then_inc(const_in, 16)
            for j in range(CT):
                sp.dma_start(x_raw[:, j, :], x[j * P:(j + 1) * P]).then_inc(x_in[j], 16)
            for k in range(KT):
                if k >= 2:
                    sp.wait_ge(w_lo_done, k - 1)
                sp.dma_start(w_stage[:, k % 2, :], w_in[k * P:(k + 1) * P]).then_inc(w_staged[k % 2], 16)

            for j in range(2):
                sp.sem_inc(u_store[j], 16)
            for j in range(CT):
                sp.sem_inc(q_store[j], 16)
            sp.wait_ge(u_evac, 1)
            sp.dma_start(m.u_d[:, :, 0:META].rearrange("g p n -> p g n"),
                         u_out[:, 0, 0:GROUPS * META].rearrange("p (g n) -> p g n", g=GROUPS)).then_inc(u_store[0], 16)

            def chunk(c, more):
                for j in range(CT):
                    sp.wait_ge(qkv_free, 2 * c + j + 1)
                    sp.dma_start(cs[:, j], rope[ds(c * CW + j * P, P)].rearrange("p (a n) -> p a n", a=2)).then_inc(cs_in[j], 16)
                if more:
                    for j in range(CT):
                        sp.wait_ge(xn_done, 2 * c + j + 2)
                        sp.dma_start(x_raw[:, j, :], x[ds(c * CW + (j + CT) * P, P)]).then_inc(x_in[j], 16)
                for f in range(GROUPS):
                    sp.wait_ge(u_evac, 4 * c + f + 2)
                    sp.dma_start(m.u_d[f, :, ds(c * CW + META, CW)], u_out[:, f % 2, :]).then_inc(u_store[f % 2], 16)
                for j in range(CT):
                    sp.wait_ge(post, POST * (2 * c + j + 2))
                    sp.dma_start(m.q_d[ds(c * CW + j * P, P)], q_out[:, j, :]).then_inc(q_store[j], 16)

            with sp.Fori(0, NCH - 1) as c:
                chunk(c, True)
            chunk(NCH - 1, False)
            sp.wait_ge(u_store[0], 16 * (2 + 2 * NCH))
            sp.wait_ge(u_store[1], 16 * (1 + 2 * NCH))
            for j in range(CT):
                sp.wait_ge(q_store[j], 16 * (NCH + 1))

        @block.gpsimd
        def _(pool):
            def head_gain(n, rows, j, h0):
                lo = h0 * HD
                src = qkv[0:rows, j, lo:QK]
                pool.tensor_tensor(sq[0:rows, lo:QK], src, src, ALU.mult).then_inc(sq_done, 1)
                pool.wait_ge(sq_done, n + 1)
                parts = ([(0, DA, 0)] if h0 == 0 else []) + [(DA, QK, 1)]
                for a, b, which in parts:
                    v = qkv[0:rows, j, a:b].rearrange("p (h n) -> p h n", n=HD)
                    g = g_qk[0:rows, which, :].unsqueeze(1).broadcast_to([rows, (b - a) // HD, HD])
                    pool.tensor_tensor(v, v, g, ALU.mult).then_inc(gain_done, 1)

            pool.wait_ge(const_in, 96)
            pool.wait_ge(kv_evac, 1)
            head_gain(0, META, 1, HEADS)
            with pool.Fori(0, NCH) as c:
                for j in range(CT):
                    pool.wait_ge(q_evac, 2 * c + j + 2)
                    pool.wait_ge(kv_evac, 2 * c + j + 2)
                    pool.wait_ge(post, POST * (2 * c + j) + 2)
                    head_gain(2 * c + j + 1, P, j, 0)

        @block.scalar
        def _(act):
            def norm(n, src, junk, rows, col):
                act.activation(junk, src, ACT.Square, accum_out=ssx[0:rows, col:col + 1]).then_inc(x_ssq, 1)
                act.wait_ge(x_ssq, n)
                act.activation(sdx[0:rows, col:col + 1], ssx[0:rows, col:col + 1], ACT.Sqrt,
                               scale=1.0 / D, bias=eps[0:rows]).then_inc(x_sd, 1)

            def norm_tile(c, j):
                act.wait_ge(x_in[j], 16 * (c + 1))
                act.wait_ge(t_done, 8 * c + 1)
                norm(2 * c + j + 2, x_raw[:, j, :], xn[:, j, :], P, j)

            def head_norm(n, rows, h0):
                act.wait_ge(post, POST * n + 2)
                act.activation(sdh[0:rows, h0:NH], ssh[0:rows, h0:NH], ACT.Sqrt,
                               scale=1.0 / HD, bias=eps[0:rows]).then_inc(head_sd, 1)

            def h_evac(c):
                for k in range(KT):
                    act.wait_ge(t_done, 8 * c + k + 2)
                    split_hi(act, hT_hi[:, k, :], ps[:, k % 2, 0:CW], g_in[:, k:k + 1]).then_inc(h_hi_done, 1)

            def u_out_evac(c):
                for f in range(GROUPS):
                    act.wait_ge(u_done, 4 * c + f + 2)
                    act.wait_ge(u_store[f % 2], 16 * (2 * c + f // 2 + (2 if f % 2 == 0 else 1)))
                    act.copy(u_out[:, f % 2, :], ps[:, 2 + f, 0:CW]).then_inc(u_evac, 1)

            def k_evac(c):
                for g in range(KV):
                    act.wait_ge(kt_done, 2 * c + g + 2)
                    split_hi(act, m.k_st[:, g, ds(c * CW, CW)], ps[:, g, 0:CW]).then_inc(k_hi_done, 1)

            def qkv_evac(c, j):
                i = 2 * c + j
                act.wait_ge(qkv_free, i + 1)
                act.wait_ge(q_done, i + 1)
                act.copy(qkv[:, j, 0:DA], ps[:, 6, :]).then_inc(q_evac, 1)
                act.wait_ge(kv_done, i + 2)
                act.copy(qkv[:, j, DA:], ps[:, 7, 0:2 * DKV]).then_inc(kv_evac, 1)
                act.wait_ge(kv_evac, i + 2)
                v = qkv[:, j, QK:].rearrange("p (g n) -> p g n", g=KV)
                act.copy(m.v_st[:, ds(i, 1), :, 0:HD].rearrange("p a g n -> p (a g) n"), v).then_inc(v_hi_done, 1)
                head_norm(i + 1, P, 0)

            act.wait_ge(m.eps_set, 1)
            act.wait_ge(const_in, 96)
            norm(1, x_meta[:], xn_meta[:], META, 2)
            act.wait_ge(hm_done, 1)
            split_hi(act, hm_hi[:], hm[:]).then_inc(h_hi_done, 1)
            for j in range(CT):
                norm_tile(0, j)
            for k in range(KT):
                act.wait_ge(w_staged[k % 2], 16 * (k // 2 + 1))
                split_hi(act, win_hi[:, k, :], w_stage[:, k % 2, :]).then_inc(w_hi_done, 1)
            act.wait_ge(u_done, 1)
            act.copy(u_out[:, 0, 0:GROUPS * META].rearrange("p (g n) -> p g n", g=GROUPS),
                     ps[:, 2:6, 0:META]).then_inc(u_evac, 1)
            act.sem_inc(q_evac, 1)
            act.wait_ge(kv_done, 1)
            act.copy(qkv[0:META, 1, DA:], ps[0:META, 7, 0:2 * DKV]).then_inc(kv_evac, 1)
            act.wait_ge(kv_evac, 1)
            act.copy(m.v_st[0:META, NT, :, 0:HD],
                     qkv[0:META, 1, QK:].rearrange("p (g n) -> p g n", g=KV)).then_inc(v_hi_done, 1)
            head_norm(0, META, HEADS)
            h_evac(0)
            u_out_evac(0)
            act.wait_ge(kt_done, 1)
            split_hi(act, m.k_st[:, :, SEQ:L],
                     ps[:, 0, 0:KV * META].rearrange("p (g n) -> p g n", g=KV)).then_inc(k_hi_done, 1)
            with act.Fori(0, NCH - 1) as c:
                for j in range(CT):
                    qkv_evac(c, j)
                    norm_tile(c + 1, j)
                h_evac(c + 1)
                u_out_evac(c + 1)
                k_evac(c)
            for j in range(CT):
                qkv_evac(NCH - 1, j)
            k_evac(NCH - 1)

        @block.vector
        def _(dve):
            dve.memset(eps[:], EPS).then_inc(m.eps_set, 1)
            dve.memset(m.v_st[:, :, :, HD].bitcast(F32), 1.0).then_inc(m.v_ones_set, 1)
            dve.sem_inc(h_lo_done, 1)
            dve.sem_inc(k_lo_done, 2)
            dve.sem_inc(qkv_free, 1)

            def norm(n, out, src, rows, col):
                dve.wait_ge(x_sd, n)
                dve.reciprocal(rsx[0:rows, col:col + 1], sdx[0:rows, col:col + 1]).then_inc(x_rs, 1)
                dve.wait_ge(x_rs, n)
                dve.tensor_scalar(out, src, rsx[0:rows, col:col + 1], None, ALU.mult).then_inc(xn_done, 1)

            def norm_tile(c, j):
                norm(2 * c + j + 2, xn[:, j, :], x_raw[:, j, :], P, j)

            def h_evac(c):
                for k in range(KT):
                    dve.wait_ge(h_hi_done, 8 * c + k + 2)
                    dve.scalar_tensor_tensor(hT_lo[:, k, :], ps[:, k % 2, 0:CW], g_in[:, k:k + 1],
                                             hT_hi[:, k, :].bitcast(F32), ALU.mult, ALU.subtract).then_inc(h_lo_done, 1)

            def k_evac(c):
                for g in range(KV):
                    dve.wait_ge(k_hi_done, 2 * c + g + 2)
                    lo = m.k_st[HD:P, g, ds(c * CW, CW)]
                    dve.tensor_tensor(lo, ps[HD:P, g, 0:CW], lo.bitcast(F32), ALU.subtract).then_inc(k_lo_done, 1)

            def post_tile(n, rows, j, h0, v_lo, v_hi, table):
                base = POST * n
                lo, nh = h0 * HD, NH - h0
                dve.wait_ge(v_hi_done, n + 1)
                v = qkv[0:rows, j, QK:].rearrange("p (g n) -> p g n", g=KV)
                dve.tensor_tensor(v_lo, v, v_hi.bitcast(F32), ALU.subtract).then_inc(post, 1)
                dve.wait_ge(sq_done, n + 1)
                dve.tensor_reduce(ssh[0:rows, h0:NH], sq[0:rows, lo:QK].rearrange("p (h n) -> p h n", n=HD),
                                  AX.X, ALU.add).then_inc(post, 1)
                dve.wait_ge(gain_done, 2 * n + 1)
                if h0 == 0:
                    dve.wait_ge(post, base)
                cos = table[:, 0, :].unsqueeze(1).broadcast_to([rows, nh, HD])
                r3 = qkv[0:rows, j, lo:QK].rearrange("p (h n) -> p h n", n=HD)
                t1v = t1[0:rows, lo:QK].rearrange("p (h n) -> p h n", n=HD)
                dve.tensor_tensor(t1v, r3, cos, ALU.mult).then_inc(post, 1)
                r5 = qkv[0:rows, j, lo:QK].rearrange("p (h b n) -> p h b n", b=2, n=HD // 4)
                t5 = t2[0:rows, lo:QK].rearrange("p (h b n) -> p h b n", b=2, n=HD // 4)
                s5 = table[:, 1, :].rearrange("p (a b n) -> p a b n", a=2, b=2)
                for b in range(2):
                    src = r5[:, :, 1 - b, :].rearrange("p (h a) n -> p h a n", a=2)
                    dst = t5[:, :, b, :].rearrange("p (h a) n -> p h a n", a=2)
                    sin = s5[:, :, b, :].unsqueeze(1).broadcast_to([rows, nh, 2, HD // 4])
                    last = dve.tensor_tensor(dst, src, sin, ALU.mult).then_inc(post, 1)
                dve.wait_ge(post, base + 5)
                dve.sem_inc(qkv_free, 1)
                dve.tensor_tensor(t1[0:rows, lo:QK], t1[0:rows, lo:QK], t2[0:rows, lo:QK], ALU.add).then_inc(post, 1)
                dve.wait_ge(head_sd, n + 1)
                dve.reciprocal(rsh[0:rows, h0:NH], sdh[0:rows, h0:NH]).then_inc(post, 1)
                dve.wait_ge(post, base + 7)
                k_in = t1[0:rows, DA:QK].rearrange("p (g n) -> p g n", g=KV)
                rk = rsh[0:rows, HEADS:NH]
                if h0:
                    for dup in range(2):
                        dve.tensor_tensor(k_tok[0:rows, j, :, dup, :], k_in,
                                          rk.unsqueeze(2).broadcast_to([rows, KV, HD]), ALU.mult).then_inc(post, 1)
                else:
                    for g in range(KV):
                        last = dve.tensor_tensor(
                            k_tok[0:rows, j, g, :, :], k_in[:, g, :].unsqueeze(1).broadcast_to([rows, 2, HD]),
                            rk[:, g:g + 1].unsqueeze(2).broadcast_to([rows, 2, HD]), ALU.mult)
                        if g == KV - 1:
                            last.then_inc(post, 1)

            def post_full(c, j):
                i = 2 * c + j
                dve.wait_ge(cs_in[j], 16 * (c + 1))
                v = m.v_st[:, ds(i, 1), :, :].rearrange("p a g n -> p (a g) n")
                post_tile(i + 1, P, j, 0, v[:, :, HD + 1:], v[:, :, 0:HD], cs[:, j])
                dve.wait_ge(q_store[j], 16 * (c + 1))
                dve.tensor_tensor(q_out[:, j, :].rearrange("p (h n) -> p h n", n=HD),
                                  t1[:, 0:DA].rearrange("p (h n) -> p h n", n=HD),
                                  rsh[:, 0:HEADS].unsqueeze(2).broadcast_to([P, HEADS, HD]), ALU.mult).then_inc(post, 1)

            dve.wait_ge(const_in, 96)
            norm(1, xn_meta[:], x_meta[:], META, 2)
            dve.wait_ge(t_done, 1)
            dve.tensor_tensor(hm[:], ps[:, 1, 0:KT * META].rearrange("p (k n) -> p k n", k=KT),
                              g_in[:].unsqueeze(2).broadcast_to([P, KT, META]), ALU.mult).then_inc(hm_done, 1)
            dve.wait_ge(h_hi_done, 1)
            dve.tensor_tensor(hm_lo[:], hm[:], hm_hi[:].bitcast(F32), ALU.subtract).then_inc(h_lo_done, 1)
            for j in range(CT):
                norm_tile(0, j)
            for k in range(KT):
                dve.wait_ge(w_hi_done, k + 1)
                dve.tensor_tensor(win_lo[:, k, :], w_stage[:, k % 2, :], win_hi[:, k, :].bitcast(F32),
                                  ALU.subtract).then_inc(w_lo_done, 1)
            post_tile(0, META, 1, HEADS, m.v_st[0:META, NT, :, HD + 1:], m.v_st[0:META, NT, :, 0:HD], cs_meta)
            h_evac(0)
            dve.wait_ge(k_hi_done, 1)
            lo = m.k_st[HD:P, :, SEQ:L]
            dve.tensor_tensor(lo, ps[HD:P, 0, 0:KV * META].rearrange("p (g n) -> p g n", g=KV),
                              lo.bitcast(F32), ALU.subtract).then_inc(k_lo_done, 1)
            with dve.Fori(0, NCH - 1) as c:
                for j in range(CT):
                    post_full(c, j)
                    norm_tile(c + 1, j)
                h_evac(c + 1)
                k_evac(c)
            for j in range(CT):
                post_full(NCH - 1, j)
            k_evac(NCH - 1)

        @block.tensor
        def _(pe):
            pe.wait_ge(const_in, 96)
            pe.wait_ge(xn_done, 1)
            for k in range(KT):
                last = pe.transpose(ps[:, 1, k * META:(k + 1) * META], xn_meta[:, k * P:(k + 1) * P],
                                    ident[0:META, 0:META])
            last.then_inc(t_done, 1)
            pe.wait_ge(h_lo_done, 2)
            pe.wait_ge(w_lo_done, KT)
            for f in range(GROUPS):
                w = slice(U0 + f * P, U0 + (f + 1) * P)
                for k in range(KT):
                    last = matmul3(pe, ps[:, 2 + f, 0:META], win_hi[:, k, w], win_lo[:, k, w],
                                   hm_hi[:, k, :], hm_lo[:, k, :], k == 0, k == KT - 1)
            last.then_inc(u_done, 1)
            for k in range(KT):
                last = matmul3(pe, ps[0:META, 7, 0:2 * DKV], hm_hi[:, k, :], hm_lo[:, k, :],
                               win_hi[:, k, DA:U0], win_lo[:, k, DA:U0], k == 0, k == KT - 1)
            last.then_inc(kv_done, 1)

            def h_transpose(c, k):
                pe.wait_ge(h_lo_done, 8 * c + k + 1)
                if k < 2:
                    pe.wait_ge(k_lo_done, 2 * c + 1)
                for j in range(CT):
                    last = pe.transpose(ps[:, k % 2, j * P:(j + 1) * P], xn[:, j, k * P:(k + 1) * P], ident[:])
                last.then_inc(t_done, 1)

            def u_products(c, k):
                pe.wait_ge(h_lo_done, 8 * c + k + 3)
                if k == 0:
                    pe.wait_ge(u_evac, 4 * c + 1)
                for f in range(GROUPS):
                    w = slice(U0 + f * P, U0 + (f + 1) * P)
                    last = matmul3(pe, ps[:, 2 + f, 0:CW], win_hi[:, k, w], win_lo[:, k, w],
                                   hT_hi[:, k, :], hT_lo[:, k, :], k == 0, k == KT - 1)
                    if k == KT - 1:
                        last.then_inc(u_done, 1)

            def k_transpose(c):
                for g in range(KV):
                    for j in range(CT):
                        last = pe.transpose(ps[:, g, j * P:(j + 1) * P],
                                            k_tok[:, j, g, :, :].rearrange("p a n -> p (a n)"), ident[:])
                    last.then_inc(kt_done, 1)

            def qkv_products(c):
                for j in range(CT):
                    t = slice(j * P, (j + 1) * P)
                    pe.wait_ge(q_evac, 2 * c + j + 1)
                    for k in range(KT):
                        last = matmul3(pe, ps[:, 6, :], hT_hi[:, k, t], hT_lo[:, k, t],
                                       win_hi[:, k, 0:DA], win_lo[:, k, 0:DA], k == 0, k == KT - 1)
                    last.then_inc(q_done, 1)
                    pe.wait_ge(kv_evac, 2 * c + j + 1)
                    for k in range(KT):
                        last = matmul3(pe, ps[:, 7, 0:2 * DKV], hT_hi[:, k, t], hT_lo[:, k, t],
                                       win_hi[:, k, DA:U0], win_lo[:, k, DA:U0], k == 0, k == KT - 1)
                    last.then_inc(kv_done, 1)

            def h_and_u(c):
                pe.wait_ge(xn_done, 2 * c + 3)
                for k in range(KT):
                    h_transpose(c, k)
                    if k:
                        u_products(c, k - 1)
                u_products(c, KT - 1)

            h_and_u(0)
            pe.wait_ge(post, POST)
            for g in range(KV):
                last = pe.transpose(ps[:, 0, g * META:(g + 1) * META],
                                    k_tok[0:META, 1, g, :, :].rearrange("p a n -> p (a n)"), ident[0:META, 0:META])
            last.then_inc(kt_done, 1)
            qkv_products(0)
            with pe.Fori(1, NCH) as c:
                h_and_u(c)
                pe.wait_ge(post, 2 * POST * c + POST - 1)
                k_transpose(c - 1)
                qkv_products(c)
            pe.wait_ge(post, 2 * POST * NCH + POST - 1)
            k_transpose(NCH - 1)


def attend(nc, m):
    HG = HEADS // KV
    W = HG * P
    ROW = 2 * HD
    HALF = 1024
    CHUNKS = 2 * HG
    SCALE = HD ** -0.5
    RING = 9
    LAG = 4
    CHUNK_AT = (1, 2, 3, 5, 7, 9, 11, 12)
    OUT_AT, TAIL_AT, Q2_AT = LAG + 1, LAG + 2, 14
    with ExitStack() as ctx:
        sb = lambda n, s, d=F32: ctx.enter_context(nc.sbuf_tensor(n, s, d))
        sem = lambda n: ctx.enter_context(nc.semaphore(n))
        ident, ps = m.ident, m.ps
        k_one = sb("k_one", [HD + 1, KV, L], F32R)
        q_raw = sb("q_raw", [P, KV, HG, ROW + 1])
        q_hi = sb("q_hi", [P, KV, W], F32R)
        q_lo = sb("q_lo", [HD + 1, KV, W], F32R)
        probs = sb("probs", [P, RING, W])
        p_hi = sb("p_hi", [P, RING, W], F32R)
        p_lo = sb("p_lo", [P, RING, W], F32R)
        oT = sb("oT", [HD + 1, W])
        o_out = sb("o_out", [P, KV, HG * HD])
        mx = sb("mx", [P, KV, HG, 3])
        mx_all = sb("mx_all", [P, HG])
        rden = sb("rden", [P, HG])

        k_copied = sem("a_k_copied")
        q_in = [sem(f"a_q_in{g}") for g in range(KV)]
        o_store = [sem(f"a_o_store{g}") for g in range(KV)]
        ones_set = sem("a_ones_set")
        q_turned, q_hi_done, q_lo_done = sem("a_q_turned"), sem("a_q_hi_done"), sem("a_q_lo_done")
        q_max_turned = sem("a_q_max_turned")
        chunk_done, chunk_max = sem("a_chunk_done"), sem("a_chunk_max")
        tail_done, tail_max = sem("a_tail_done"), sem("a_tail_max")
        max_done, neg_max_done = sem("a_max_done"), sem("a_neg_max_done")
        scored, exp_done, hi_done, lo_done = sem("a_scored"), sem("a_exp_done"), sem("a_hi_done"), sem("a_lo_done")
        valued, oT_done = sem("a_valued"), sem("a_oT_done")
        out_done, rden_done, o_done = sem("a_out_done"), sem("a_rden_done"), sem("a_o_done")
        VALUES, MISC = 6, 7

        def rows(kt):
            return P if kt < NT else META

        def before(kt):
            if kt >= RING:
                return 0, kt - RING
            return 1, kt + RING * ((NKT - 1 - kt) // RING)

        block = ctx.enter_context(nc.Block())

        @block.sync
        def _(sp):
            def load_q(qt, g):
                src = m.q_d[ds(qt * P, P), g * HG * HD:(g + 1) * HG * HD].rearrange("p (h n) -> p h n", n=HD)
                for a in range(2):
                    sp.dma_start(q_raw[:, g, :, a * HD:(a + 1) * HD], src).then_inc(q_in[g], 16)

            def step(qt, g, ahead=True):
                s = 2 * qt + g
                if ahead:
                    sp.wait_ge(q_max_turned, s + 2)
                    load_q(qt + 1 + g, 1 - g)
                sp.wait_ge(o_done, s + 1)
                sp.dma_start(m.o_d[ds(qt * P, P), g * HG * HD:(g + 1) * HG * HD], o_out[:, g, :]).then_inc(o_store[g], 16)

            load_q(0, 0)
            load_q(0, 1)
            for g in range(KV):
                sp.sem_inc(o_store[g], 16)
            sp.wait_ge(q_max_turned, 1)
            load_q(1, 0)
            with sp.Fori(0, NT - 2) as qt:
                for g in range(KV):
                    step(qt, g)
            step(NT - 2, 0)
            step(NT - 2, 1, ahead=False)
            for g in range(KV):
                step(NT - 1, g, ahead=False)
            for g in range(KV):
                sp.wait_ge(o_store[g], 16 * (NT + 1))

        @block.tensor
        def _(pe):
            def turn_q(x, g, loads):
                pe.wait_ge(q_in[g], 32 * loads)
                if not isinstance(x, int) or x > 0:
                    pe.wait_ge(q_lo_done, x)
                for h in range(HG):
                    last = pe.transpose(ps[:, MISC, h * P:(h + 1) * P], q_raw[:, g, h, 0:ROW], ident[:])
                last.then_inc(q_turned, 1)

            def score_chunk(x, g, c):
                h, half = c // 2, c % 2
                if c == 0:
                    pe.wait_ge(q_hi_done, x + 1)
                if c >= 2 or not isinstance(x, int) or x > 0:
                    pe.wait_ge(chunk_max, CHUNKS * x + c - 1)
                for b in range(2):
                    k0 = HALF * half + 512 * b
                    last = pe.matmul(ps[:, 2 * half + b, :], q_hi[:, g, h * P:(h + 1) * P],
                                     m.k_st[:, g, k0:k0 + 512], start=True, stop=True)
                last.then_inc(chunk_done, 1)

            def score_tail(x, g):
                for h in range(HG):
                    last = pe.matmul(ps[:, MISC, h * META:(h + 1) * META], q_hi[:, g, h * P:(h + 1) * P],
                                     m.k_st[:, g, SEQ:L], start=True, stop=True)
                last.then_inc(tail_done, 1)

            def turn_max(x, g):
                pe.wait_ge(neg_max_done, x + 1)
                for h in range(HG):
                    last = pe.transpose(ps[0:HD + 1, MISC, h * P:(h + 1) * P], q_raw[:, g, h, HD:ROW + 1], ident[:])
                last.then_inc(q_max_turned, 1)

            def score(s, g, kt):
                r, bank = rows(kt), 4 + (g + kt) % 2
                if kt == 0:
                    pe.wait_ge(q_lo_done, s + 1)
                if kt >= 2 or not isinstance(s, int) or s > 0:
                    pe.wait_ge(exp_done, NKT * s + kt - 1)
                keys = slice(kt * P, kt * P + r)
                pe.matmul(ps[0:r, bank, :], m.k_st[:, g, keys], q_hi[:, g, :], start=True, stop=False)
                pe.matmul(ps[0:r, bank, :], k_one[:, g, keys], q_lo[:, g, :], start=False, stop=True).then_inc(scored, 1)

            def values(s, g, kt):
                r = rows(kt)
                pe.wait_ge(lo_done, NKT * s + kt + 1)
                if kt == 0 and (not isinstance(s, int) or s > 0):
                    pe.wait_ge(oT_done, s)
                v_hi_one, v_lo = m.v_st[0:r, kt, g, 0:HD + 1], m.v_st[0:r, kt, g, HD + 1:]
                hi, lo = p_hi[0:r, kt % RING, :], p_lo[0:r, kt % RING, :]
                pe.matmul(ps[0:HD + 1, VALUES, :], v_hi_one, hi, start=kt == 0, stop=False)
                pe.matmul(ps[0:HD, VALUES, :], v_lo, hi, start=False, stop=False)
                pe.matmul(ps[0:HD + 1, VALUES, :], v_hi_one, lo, start=False, stop=kt == NKT - 1).then_inc(valued, 1)

            def output(s):
                pe.wait_ge(oT_done, s + 1)
                for h in range(HG):
                    last = pe.transpose(ps[:, MISC, h * (HD + 1):(h + 1) * (HD + 1)], oT[:, h * P:(h + 1) * P],
                                        ident[0:HD + 1, 0:HD + 1])
                last.then_inc(out_done, 1)

            def step(qt, g, first=False, prepare=True):
                s, og = 2 * qt + g, 1 - g
                for kt in range(NKT):
                    score(s, g, kt)
                    if prepare:
                        if kt == 0:
                            turn_q(s + 1, og, qt + 1 + g)
                        if kt in CHUNK_AT:
                            score_chunk(s + 1, og, CHUNK_AT.index(kt))
                        if kt == TAIL_AT:
                            if not first:
                                pe.wait_ge(o_done, s)
                            score_tail(s + 1, og)
                        if kt == Q2_AT:
                            turn_max(s + 1, og)
                    if kt >= LAG:
                        values(s, g, kt - LAG)
                    elif not first:
                        values(s - 1, og, NKT + kt - LAG)
                    if kt == OUT_AT and not first:
                        if prepare:
                            pe.wait_ge(q_hi_done, s + 2)
                        output(s - 1)

            pe.wait_ge(ones_set, 1)
            turn_q(0, 0, 1)
            for c in range(CHUNKS):
                score_chunk(0, 0, c)
                if c == 0:
                    score_tail(0, 0)
            turn_max(0, 0)
            pe.wait_ge(k_copied, 1)
            step(0, 0, first=True)
            step(0, 1)
            with pe.Fori(1, NT - 1) as qt:
                for g in range(KV):
                    step(qt, g)
            step(NT - 1, 0)
            step(NT - 1, 1, prepare=False)
            for kt in range(NKT - LAG, NKT):
                values(2 * NT - 1, 1, kt)
            pe.wait_ge(o_done, 2 * NT - 1)
            output(2 * NT - 1)

        @block.scalar
        def _(act):
            def q_high(x, g):
                act.wait_ge(q_turned, x + 1)
                split_hi(act, q_hi[:, g, :], ps[:, MISC, :]).then_inc(q_hi_done, 1)

            def exp(s, g, kt):
                r = rows(kt)
                act.wait_ge(scored, NKT * s + kt + 1)
                back, last = before(kt)
                if not (isinstance(s, int) and s < back):
                    act.wait_ge(lo_done, NKT * (s - back) + last + 1)
                act.activation(probs[0:r, kt % RING, :], ps[0:r, 4 + (g + kt) % 2, :], ACT.Exp,
                               scale=SCALE).then_inc(exp_done, 1)

            def high(s, kt):
                r = rows(kt)
                act.wait_ge(exp_done, NKT * s + kt + 1)
                back, last = before(kt)
                if not (isinstance(s, int) and s < back):
                    act.wait_ge(valued, NKT * (s - back) + last + 1)
                split_hi(act, p_hi[0:r, kt % RING, :], probs[0:r, kt % RING, :]).then_inc(hi_done, 1)

            def output(s):
                act.wait_ge(valued, NKT * (s + 1))
                if not (isinstance(s, int) and s == 0):
                    act.wait_ge(out_done, s)
                act.copy(oT[:], ps[0:HD + 1, VALUES, :]).then_inc(oT_done, 1)

            def step(s, g, first=False, prepare=True):
                for kt in range(NKT):
                    exp(s, g, kt)
                    if kt == 0 and prepare:
                        q_high(s + 1, 1 - g)
                    if kt:
                        high(s, kt - 1)
                    if kt == LAG - 1 and not first:
                        output(s - 1)
                high(s, NKT - 1)

            q_high(0, 0)
            act.copy(k_one[0:HD], m.k_st[0:HD].bitcast(F32)).then_inc(k_copied, 1)
            step(0, 0, first=True)
            step(1, 1)
            with act.Fori(1, NT - 1) as qt:
                for g in range(KV):
                    step(2 * qt + g, g)
            step(2 * NT - 2, 0)
            step(2 * NT - 1, 1, prepare=False)
            output(2 * NT - 1)

        @block.vector
        def _(dve):
            def low(s, kt):
                r = rows(kt)
                dve.wait_ge(hi_done, NKT * s + kt + 1)
                dve.tensor_tensor(p_lo[0:r, kt % RING, :], probs[0:r, kt % RING, :],
                                  p_hi[0:r, kt % RING, :].bitcast(F32), ALU.subtract).then_inc(lo_done, 1)

            def chunk_maximum(x, g, c):
                h, half = c // 2, c % 2
                dve.wait_ge(chunk_done, CHUNKS * x + c + 1)
                dve.tensor_reduce(mx[:, g, h, half:half + 1], ps[:, 2 * half:2 * half + 2, :].rearrange("p b n -> p (b n)"),
                                  AX.X, ALU.max).then_inc(chunk_max, 1)

            def tail_maximum(x, g):
                dve.wait_ge(tail_done, x + 1)
                dve.tensor_reduce(mx[:, g, :, 2], ps[:, MISC, 0:HG * META].rearrange("p (h n) -> p h n", n=META),
                                  AX.X, ALU.max).then_inc(tail_max, 1)

            def maximum(x, g):
                dve.wait_ge(chunk_max, CHUNKS * (x + 1))
                dve.wait_ge(tail_max, x + 1)
                dve.tensor_reduce(mx_all[:], mx[:, g], AX.X, ALU.max).then_inc(max_done, 1)
                dve.wait_ge(max_done, x + 1)
                dve.tensor_tensor(q_raw[:, g, :, ROW], q_raw[:, g, :, 0], mx_all[:], ALU.subtract).then_inc(neg_max_done, 1)

            def q_low(x, g):
                dve.wait_ge(q_max_turned, x + 1)
                dve.tensor_tensor(q_lo[:, g, :], ps[0:HD + 1, MISC, :], q_hi[0:HD + 1, g, :].bitcast(F32),
                                  ALU.subtract).then_inc(q_lo_done, 1)

            def normalise(qt, g):
                s = 2 * qt + g
                dve.wait_ge(out_done, s + 1)
                turned = ps[:, MISC, 0:HG * (HD + 1)].rearrange("p (h n) -> p h n", n=HD + 1)
                dve.reciprocal(rden[:], turned[:, :, HD]).then_inc(rden_done, 1)
                dve.wait_ge(rden_done, s + 1)
                dve.wait_ge(o_store[g], 16 * (qt + 1))
                dve.tensor_tensor(o_out[:, g, :].rearrange("p (h n) -> p h n", n=HD),
                                  turned[:, :, 0:HD],
                                  rden[:].unsqueeze(2).broadcast_to([P, HG, HD]), ALU.mult).then_inc(o_done, 1)

            def step(qt, g, first=False, prepare=True):
                s, og = 2 * qt + g, 1 - g
                for kt in range(NKT):
                    if prepare and kt + 1 in CHUNK_AT:
                        chunk_maximum(s + 1, og, CHUNK_AT.index(kt + 1))
                    if kt == OUT_AT - 2 and not first:
                        normalise(qt - 1 + g, og)
                    if prepare and kt == TAIL_AT:
                        tail_maximum(s + 1, og)
                    if prepare and kt == Q2_AT - 2:
                        maximum(s + 1, og)
                    if prepare and kt == Q2_AT:
                        q_low(s + 1, og)
                    low(s, kt)

            dve.memset(k_one[HD:HD + 1].bitcast(F32), 1.0).then_inc(ones_set, 1)
            chunk_maximum(0, 0, 0)
            tail_maximum(0, 0)
            for c in range(1, CHUNKS):
                chunk_maximum(0, 0, c)
            dve.wait_ge(q_in[0], 32)
            maximum(0, 0)
            q_low(0, 0)
            step(0, 0, first=True)
            step(0, 1)
            with dve.Fori(1, NT - 1) as qt:
                for g in range(KV):
                    step(qt, g)
            step(NT - 1, 0)
            step(NT - 1, 1, prepare=False)
            normalise(NT - 1, 1)


def mix(nc, m, x, w_pool, w_out, attn_norm, pool_scale):
    REACH = max(WINDOWS) // 2
    UW = CW + 2 * REACH
    LINKS = 9
    with ExitStack() as ctx:
        sb = lambda n, s, d=F32: ctx.enter_context(nc.sbuf_tensor(n, s, d))
        sem = lambda n: ctx.enter_context(nc.semaphore(n))
        ident, ps, eps = m.ident, m.ps, m.eps
        wo_hi = sb("wo_hi", [P, KT, D], F32R)
        wo_lo = sb("wo_lo", [P, KT, D], F32R)
        wp_hi = sb("wp_hi", [P, GROUPS, P], F32R)
        wp_lo = sb("wp_lo", [P, GROUPS, P], F32R)
        stage = sb("stage", [P, 2, D])
        u_raw = sb("u_raw", [P, GROUPS, UW])
        sums = [sb(f"window_sums{j}", [P, GROUPS, UW]) for j in range(2)]
        corr = sb("corr", [P, GROUPS, REACH + 1])
        d_raw = sb("d_raw", [P, GROUPS, CW])
        d_hi = sb("d_hi", [P, GROUPS, CW], F32R)
        d_lo = sb("d_lo", [P, GROUPS, CW], F32R)
        o_raw = sb("o_raw", [P, CT, DA])
        mt = sb("mt", [P, CT, D])
        mT_hi = sb("mT_hi", [P, KT, CW], F32R)
        mT_lo = sb("mT_lo", [P, KT, CW], F32R)
        x_res = sb("x_res", [P, CT, D])
        g_mix = sb("g_mix", [P, KT])
        ss = sb("mss", [P, CT, 2])
        sd = sb("msd", [P, CT, 2])
        rs = sb("mrs", [P, CT, 2])

        const_in, u_in, tail_set, pooled = sem("m_const_in"), sem("m_u_in"), sem("m_tail_set"), sem("m_pooled")
        w_staged = [sem(f"m_w_staged{j}") for j in range(2)]
        w_hi_done, w_lo_done = sem("m_w_hi_done"), sem("m_w_lo_done")
        o_in = [sem(f"m_o_in{j}") for j in range(CT)]
        x_in = [sem(f"m_x_in{j}") for j in range(CT)]
        x_store = [sem(f"m_x_store{j}") for j in range(CT)]
        d_hi_done, d_lo_done, y_done = sem("m_d_hi_done"), sem("m_d_lo_done"), sem("m_y_done")
        ssq_done, sd_done, rs_done, mt_done = sem("m_ssq_done"), sem("m_sd_done"), sem("m_rs_done"), sem("m_mt_done")
        t_done, hi_done, lo_done = sem("m_t_done"), sem("m_hi_done"), sem("m_lo_done")
        out_done, res_done = sem("m_out_done"), sem("m_res_done")

        block = ctx.enter_context(nc.Block())

        @block.sync
        def _(sp):
            sp.dma_start(u_raw[:], m.u_d[:, :, META - REACH:META - REACH + UW].rearrange("g p n -> p g n")).then_inc(u_in, 16)
            for dst, src in (
                (corr[:], m.corr_in),
                (g_mix[:, 0:4], attn_norm),
                (g_mix[:, 4:8], pool_scale),
            ):
                sp.dma_start(dst, src).then_inc(const_in, 16)
            sp.dma_start(stage[:, 0, 0:DP].rearrange("p (g n) -> p g n", g=GROUPS),
                         w_pool.rearrange("g p n -> p g n")).then_inc(w_staged[0], 16)
            for j in range(CT):
                sp.dma_start(o_raw[:, j, :], m.o_d[j * P:(j + 1) * P]).then_inc(o_in[j], 16)
            for k in range(KT):
                if k >= 1:
                    sp.wait_ge(w_lo_done, k)
                sp.dma_start(stage[:, (k + 1) % 2, :], w_out[k * P:(k + 1) * P]).then_inc(w_staged[(k + 1) % 2], 16)

            def store(c):
                for j in range(CT):
                    sp.wait_ge(res_done, 2 * c + j + 3)
                    sp.dma_start(m.x2_d[ds(c * CW + j * P, P)], x_res[:, j, :]).then_inc(x_store[j], 16)

            def chunk(c, width):
                sp.wait_ge(pooled, LINKS * c)
                sp.dma_start(u_raw[:, :, 0:width],
                             m.u_d[:, :, ds(c * CW + META - REACH, width)].rearrange("g p n -> p g n")).then_inc(u_in, 16)
                for j in range(CT):
                    sp.wait_ge(mt_done, 2 * c + j - 1)
                    sp.dma_start(o_raw[:, j, :], m.o_d[ds(c * CW + j * P, P)]).then_inc(o_in[j], 16)
                store(c - 1)

            with sp.Fori(1, NCH - 1) as c:
                chunk(c, UW)
            chunk(NCH - 1, UW - REACH)
            store(NCH - 1)
            for j in range(CT):
                sp.wait_ge(x_store[j], 16 * (NCH + 1))

        @block.gpsimd
        def _(pool):
            def windows(c, last=False):
                links = [0]

                def link(ins):
                    ins.then_inc(pooled, 1)
                    links[0] += 1
                    pool.wait_ge(pooled, LINKS * c + links[0])

                if isinstance(c, int) and c == 0:
                    pool.wait_ge(const_in, 48)
                pool.wait_ge(u_in, 16 * (c + 1))
                src = u_raw
                for i in range(GROUPS):
                    h, dst = 1 << i, sums[i % 2]
                    n = UW - 2 * h + 1
                    link(pool.tensor_tensor(dst[:, i:, 0:n], src[:, i:, 0:n], src[:, i:, h:h + n], ALU.add))
                    src = dst
                for g, w in enumerate(WINDOWS):
                    a = REACH - w // 2
                    mean = sums[g % 2][:, g, a:a + CW]
                    link(pool.tensor_tensor(mean, mean, corr[:, g, REACH:].broadcast_to([P, CW]), ALU.mult))
                    if last:
                        end = mean[:, CW - REACH:CW]
                        link(pool.tensor_tensor(end, end, corr[:, g, 0:REACH], ALU.mult))
                if not isinstance(c, int) or c > 0:
                    pool.wait_ge(d_lo_done, c)
                for g, w in enumerate(WINDOWS):
                    a = REACH - w // 2
                    ins = pool.tensor_tensor(d_raw[:, g, :], sums[g % 2][:, g, a:a + CW],
                                             u_raw[:, g, REACH:REACH + CW], ALU.subtract)
                link(ins)

            def residual_in(c):
                for j in range(CT):
                    pool.wait_ge(x_store[j], 16 * (c + 1))
                    pool.dma_start(x_res[:, j, :], x[ds(c * CW + j * P, P)]).then_inc(x_in[j], 16)

            for j in range(CT):
                pool.sem_inc(x_store[j], 16)
            windows(0)
            with pool.Fori(0, NCH - 2) as c:
                residual_in(c)
                windows(c + 1)
            residual_in(NCH - 2)
            pool.wait_ge(u_in, 16 * NCH)
            pool.memset(u_raw[:, :, UW - REACH:UW], 0.0).then_inc(tail_set, 1)
            pool.wait_ge(tail_set, 1)
            windows(NCH - 1, last=True)
            residual_in(NCH - 1)

        @block.scalar
        def _(act):
            def split_d(c):
                act.wait_ge(y_done, 2 * c + 1)
                act.wait_ge(pooled, LINKS * (c + 1) + (GROUPS if isinstance(c, int) and c == NCH - 1 else 0))
                split_hi(act, d_hi[:], d_raw[:]).then_inc(d_hi_done, 1)

            def norm_tile(c, j):
                i = 2 * c + j
                act.wait_ge(o_in[j], 16 * (c + 1))
                act.wait_ge(t_done, 8 * c + 1)
                act.activation(mt[:, j, 0:DA], o_raw[:, j, :], ACT.Square, accum_out=ss[:, j, 0:1]).then_inc(ssq_done, 1)
                act.wait_ge(y_done, i + 2)
                act.activation(mt[:, j, DA:], ps[:, j, :], ACT.Square, accum_out=ss[:, j, 1:2]).then_inc(ssq_done, 1)
                act.wait_ge(ssq_done, 2 * i + 2)
                act.activation(sd[:, j, :], ss[:, j, :], ACT.Sqrt, scale=1.0 / DA, bias=eps[:]).then_inc(sd_done, 1)

            def evac(c):
                for k in range(KT):
                    act.wait_ge(t_done, 8 * c + k + 2)
                    split_hi(act, mT_hi[:, k, :], ps[:, 2 + k % 2, 0:CW], g_mix[:, k:k + 1]).then_inc(hi_done, 1)

            act.sem_inc(y_done, 1)
            act.sem_inc(t_done, 1)
            act.wait_ge(const_in, 48)
            act.wait_ge(w_staged[0], 16)
            split_hi(act, wp_hi[:], stage[:, 0, 0:DP].rearrange("p (g n) -> p g n", g=GROUPS)).then_inc(w_hi_done, 1)
            split_d(0)
            for j in range(CT):
                norm_tile(0, j)
            for k in range(KT):
                act.wait_ge(w_staged[(k + 1) % 2], 16 * ((k + 1) // 2 + 1))
                split_hi(act, wo_hi[:, k, :], stage[:, (k + 1) % 2, :]).then_inc(w_hi_done, 1)
            with act.Fori(0, NCH - 2) as c:
                evac(c)
                split_d(c + 1)
                for j in range(CT):
                    norm_tile(c + 1, j)
            evac(NCH - 2)
            split_d(NCH - 1)
            for j in range(CT):
                norm_tile(NCH - 1, j)
            evac(NCH - 1)

        @block.vector
        def _(dve):
            def split_d(c):
                dve.wait_ge(d_hi_done, c + 1)
                dve.tensor_tensor(d_lo[:], d_raw[:], d_hi[:].bitcast(F32),
                                  ALU.subtract).then_inc(d_lo_done, 1)

            def norm_tile(c, j):
                i = 2 * c + j
                dve.wait_ge(sd_done, i + 1)
                dve.reciprocal(rs[:, j, :], sd[:, j, :]).then_inc(rs_done, 1)
                dve.wait_ge(rs_done, i + 1)
                dve.tensor_scalar(mt[:, j, 0:DA], o_raw[:, j, :], rs[:, j, 0:1], None, ALU.mult)
                dve.tensor_scalar(mt[:, j, DA:], ps[:, j, :], rs[:, j, 1:2], None, ALU.mult).then_inc(mt_done, 1)

            def evac(c):
                for k in range(KT):
                    dve.wait_ge(hi_done, 8 * c + k + 1)
                    dve.scalar_tensor_tensor(mT_lo[:, k, :], ps[:, 2 + k % 2, 0:CW], g_mix[:, k:k + 1],
                                             mT_hi[:, k, :].bitcast(F32), ALU.mult, ALU.subtract).then_inc(lo_done, 1)

            def residual(c, j):
                dve.wait_ge(out_done, 2 * c + j + 1)
                dve.wait_ge(x_in[j], 16 * (c + 1))
                dve.tensor_tensor(x_res[:, j, :], ps[:, 4 + 2 * j:6 + 2 * j, :].rearrange("p b n -> p (b n)"),
                                  x_res[:, j, :], ALU.add).then_inc(res_done, 1)

            dve.sem_inc(lo_done, 2)
            dve.sem_inc(res_done, 2)
            dve.wait_ge(const_in, 48)
            dve.wait_ge(w_hi_done, 1)
            dve.tensor_tensor(wp_lo[:], stage[:, 0, 0:DP].rearrange("p (g n) -> p g n", g=GROUPS),
                              wp_hi[:].bitcast(F32), ALU.subtract).then_inc(w_lo_done, 1)
            split_d(0)
            for j in range(CT):
                norm_tile(0, j)
            for k in range(KT):
                dve.wait_ge(w_hi_done, k + 2)
                dve.tensor_tensor(wo_lo[:, k, :], stage[:, (k + 1) % 2, :], wo_hi[:, k, :].bitcast(F32),
                                  ALU.subtract).then_inc(w_lo_done, 1)
            with dve.Fori(0, NCH - 1) as c:
                evac(c)
                split_d(c + 1)
                residual(c, 0)
                for j in range(CT):
                    norm_tile(c + 1, j)
                residual(c, 1)
            evac(NCH - 1)
            residual(NCH - 1, 0)
            residual(NCH - 1, 1)

        @block.tensor
        def _(pe):
            def pool_map(c, j):
                t = slice(j * P, (j + 1) * P)
                if j == 0:
                    pe.wait_ge(d_lo_done, c + 1)
                for g in range(GROUPS):
                    last = matmul3(pe, ps[:, j, g * P:(g + 1) * P], d_hi[:, g, t], d_lo[:, g, t],
                                   wp_hi[:, g, :], wp_lo[:, g, :], True, True)
                last.then_inc(y_done, 1)

            def transposes(c):
                pe.wait_ge(mt_done, 2 * c + 2)
                for k in range(KT):
                    pe.wait_ge(lo_done, 8 * c + k + 1)
                    for j in range(CT):
                        last = pe.transpose(ps[:, 2 + k % 2, j * P:(j + 1) * P], mt[:, j, k * P:(k + 1) * P], ident[:])
                    last.then_inc(t_done, 1)

            def project_out(c, j):
                t = slice(j * P, (j + 1) * P)
                pe.wait_ge(res_done, 2 * c + j + 1)
                for half in range(2):
                    w = slice(half * 512, (half + 1) * 512)
                    for k in range(KT):
                        if j == 0 and half == 0:
                            pe.wait_ge(lo_done, 8 * c + k + 3)
                        last = matmul3(pe, ps[:, 4 + 2 * j + half, :], mT_hi[:, k, t], mT_lo[:, k, t],
                                       wo_hi[:, k, w], wo_lo[:, k, w], k == 0, k == KT - 1)
                last.then_inc(out_done, 1)

            for j in range(CT):
                pool_map(0, j)
            pe.wait_ge(w_lo_done, KT + 1)
            with pe.Fori(0, NCH - 1) as c:
                transposes(c)
                project_out(c, 0)
                for j in range(CT):
                    pool_map(c + 1, j)
                project_out(c, 1)
            transposes(NCH - 1)
            project_out(NCH - 1, 0)
            project_out(NCH - 1, 1)


def feed(nc, m, w_ffn_in, w_ffn_down, norm_ffn, norm_final, out):
    UP_PAIRS, DOWN_PAIRS = FT, FT // 2
    PAIRS = UP_PAIRS + DOWN_PAIRS
    with ExitStack() as ctx:
        sb = lambda n, s, d=F32: ctx.enter_context(nc.sbuf_tensor(n, s, d))
        sem = lambda n: ctx.enter_context(nc.semaphore(n))
        ident, ps, eps = m.ident, m.ps, m.eps
        x2 = sb("x2", [P, FC, D])
        hT_hi = sb("fT_hi", [P, KT, FW], F32R)
        hT_lo = sb("fT_lo", [P, KT, FW], F32R)
        gu_hi = sb("gu_hi", [P, FT, FW], F32R)
        gu_lo = sb("gu_lo", [P, FT, FW], F32R)
        w_raw = sb("w_raw", [P, 2, D])
        w_hi = sb("w_hi", [P, 2, D], F32R)
        w_lo = sb("w_lo", [P, 2, D], F32R)
        silu = sb("silu", [P, FW])
        gu = sb("gu", [P, FW])
        res = sb("res", [P, FC, D])
        junk = sb("junk", [P, D])
        g_final = sb("g_final", [P, D])
        g_ffn = sb("g_ffn", [P, KT])
        ss = sb("fss", [P, 2, FC])
        sd = sb("fsd", [P, 2, FC])
        rs = sb("frs", [P, 2, FC])

        const_in, x2_in = sem("f_const_in"), sem("f_x2_in")
        w_in = [sem(f"f_w_in{j}") for j in range(2)]
        w_hi_done, w_lo_done, w_used = sem("f_w_hi_done"), sem("f_w_lo_done"), sem("f_w_used")
        ssq_done, sd_done, rs_done, xn_done = sem("f_ssq_done"), sem("f_sd_done"), sem("f_rs_done"), sem("f_xn_done")
        t_done, h_hi_done, h_lo_done = sem("f_t_done"), sem("f_h_hi_done"), sem("f_h_lo_done")
        silu_done, gu_done, gu_hi_done, gu_lo_done = sem("f_silu_done"), sem("f_gu_done"), sem("f_gu_hi_done"), sem("f_gu_lo_done")
        down_done, res_done = sem("f_down_done"), sem("f_res_done")
        res_in = [sem(f"f_res_in{j}") for j in range(FC)]
        out_store = [sem(f"f_out_store{j}") for j in range(FC)]
        fssq_done, fsd_done, frs_done, fin_done = sem("f_fssq_done"), sem("f_fsd_done"), sem("f_frs_done"), sem("f_fin_done")

        block = ctx.enter_context(nc.Block())

        @block.sync
        def _(sp):
            def load(b, slot, src):
                sp.wait_ge(w_lo_done, b + 1)
                sp.dma_start(w_raw[:, slot, :].rearrange("p (k n) -> p k n", n=src.shape[-1]), src).then_inc(w_in[slot], 16)

            w_up = w_ffn_in.rearrange("(k p) n -> p k n", p=P)
            with sp.Fori(0, NFC) as c:
                with sp.Fori(0, UP_PAIRS) as f:
                    for a in range(2):
                        load(2 * PAIRS * c + 2 * f + a, a, w_up[:, :, ds(f * P + a * DFF, P)])
                with sp.Fori(0, DOWN_PAIRS) as i:
                    for a in range(2):
                        load(2 * PAIRS * c + 2 * i + (2 * UP_PAIRS + a), a,
                             w_ffn_down[ds(i * 2 * P + a * P, P)].unsqueeze(1))

        @block.gpsimd
        def _(pool):
            def load_x2(c):
                pool.dma_start(x2[:], m.x2_d[ds(c * FW, FW)].rearrange("(j p) n -> p j n", p=P)).then_inc(x2_in, 16)

            def load_res(c):
                for j in range(FC):
                    pool.wait_ge(out_store[j], 16 * (c + 1))
                    pool.dma_start(res[:, j, :], m.x2_d[ds(c * FW + j * P, P)]).then_inc(res_in[j], 16)

            for j in range(FC):
                pool.sem_inc(out_store[j], 16)
            load_x2(0)
            pool.dma_start(g_ffn[:], norm_ffn).then_inc(const_in, 16)
            pool.dma_start(g_final[:], norm_final.unsqueeze(0).broadcast_to([P, D])).then_inc(const_in, 16)
            with pool.Fori(0, NFC - 1) as c:
                load_res(c)
                pool.wait_ge(t_done, KT * (c + 1))
                load_x2(c + 1)
            load_res(NFC - 1)
            for j in range(FC):
                pool.wait_ge(out_store[j], 16 * (NFC + 1))

        @block.scalar
        def _(act):
            def split(w, slot):
                act.wait_ge(w_in[slot], 16 * w + 16)
                act.wait_ge(w_used, 2 * w + slot + 1)
                split_hi(act, w_hi[:, slot, :], w_raw[:, slot, :]).then_inc(w_hi_done, 1)

            def norm_tile(c, j):
                act.wait_ge(x2_in, 16 * (c + 1))
                act.activation(junk[:], x2[:, j, :], ACT.Square, accum_out=ss[:, 0, j:j + 1]).then_inc(ssq_done, 1)
                act.wait_ge(ssq_done, FC * c + j + 1)
                act.activation(sd[:, 0, j:j + 1], ss[:, 0, j:j + 1], ACT.Sqrt, scale=1.0 / D, bias=eps[:]).then_inc(sd_done, 1)

            def evac(c):
                for k in range(KT):
                    act.wait_ge(t_done, KT * c + k + 1)
                    split_hi(act, hT_hi[:, k, :], ps[:, k % 2, :], g_ffn[:, k:k + 1]).then_inc(h_hi_done, 1)

            def up(c):
                with act.Fori(0, UP_PAIRS) as f:
                    act.wait_ge(w_used, 2 * PAIRS * c + 2 * f + 3)
                    act.activation(silu[:], ps[:, 2, :], ACT.Silu).then_inc(silu_done, 1)
                    split(PAIRS * c + f + 1, 0)
                    act.wait_ge(gu_done, UP_PAIRS * c + f + 2)
                    split_hi(act, gu_hi[:, ds(f, 1), :].rearrange("p a n -> p (a n)"), gu[:]).then_inc(gu_hi_done, 1)
                    split(PAIRS * c + f + 1, 1)

            def down(c, normed):
                cuts = (0, 3, 6, 9, DOWN_PAIRS) if normed else (0, DOWN_PAIRS - 1)
                for j, (a, b) in enumerate(zip(cuts, cuts[1:])):
                    with act.Fori(a, b) as i:
                        for slot in range(2):
                            split(PAIRS * c + i + (UP_PAIRS + 1), slot)
                    if normed:
                        norm_tile(c + 1, j)

            def final(c):
                for j in range(FC):
                    act.wait_ge(res_done, FC * c + j + FC + 1)
                    act.activation(junk[:], res[:, j, :], ACT.Square, accum_out=ss[:, 1, j:j + 1]).then_inc(fssq_done, 1)
                    act.wait_ge(fssq_done, FC * c + j + 1)
                    act.activation(sd[:, 1, j:j + 1], ss[:, 1, j:j + 1], ACT.Sqrt, scale=1.0 / D, bias=eps[:]).then_inc(fsd_done, 1)
                for j in range(FC):
                    act.wait_ge(fin_done, FC * c + j + 1)
                    act.dma_start(out[ds(c * FW + j * P, P)], res[:, j, :]).then_inc(out_store[j], 16)

            act.sem_inc(silu_done, 1)
            act.wait_ge(const_in, 32)
            split(0, 0)
            split(0, 1)
            for j in range(FC):
                norm_tile(0, j)
            evac(0)
            with act.Fori(0, NFC - 1) as c:
                up(c)
                down(c, True)
                evac(c + 1)
                final(c)
            up(NFC - 1)
            down(NFC - 1, False)
            final(NFC - 1)

        @block.vector
        def _(dve):
            def split(w, slot):
                dve.wait_ge(w_hi_done, 2 * w + slot + 1)
                dve.tensor_tensor(w_lo[:, slot, :], w_raw[:, slot, :], w_hi[:, slot, :].bitcast(F32),
                                  ALU.subtract).then_inc(w_lo_done, 1)

            def norm_tile(c, j):
                dve.wait_ge(sd_done, FC * c + j + 1)
                dve.reciprocal(rs[:, 0, j:j + 1], sd[:, 0, j:j + 1]).then_inc(rs_done, 1)
                dve.wait_ge(rs_done, FC * c + j + 1)
                dve.tensor_scalar(x2[:, j, :], x2[:, j, :], rs[:, 0, j:j + 1], None, ALU.mult).then_inc(xn_done, 1)

            def evac(c):
                for k in range(KT):
                    dve.wait_ge(h_hi_done, KT * c + k + 1)
                    dve.scalar_tensor_tensor(hT_lo[:, k, :], ps[:, k % 2, :], g_ffn[:, k:k + 1],
                                             hT_hi[:, k, :].bitcast(F32), ALU.mult, ALU.subtract).then_inc(h_lo_done, 1)

            def up(c):
                with dve.Fori(0, UP_PAIRS) as f:
                    split(PAIRS * c + f + 1, 0)
                    dve.wait_ge(silu_done, UP_PAIRS * c + f + 2)
                    dve.wait_ge(w_used, 2 * PAIRS * c + 2 * f + 4)
                    dve.tensor_tensor(gu[:], silu[:], ps[:, 3, :], ALU.mult).then_inc(gu_done, 1)
                    dve.wait_ge(gu_hi_done, UP_PAIRS * c + f + 1)
                    dve.tensor_tensor(gu_lo[:, ds(f, 1), :].rearrange("p a n -> p (a n)"), gu[:],
                                      gu_hi[:, ds(f, 1), :].rearrange("p a n -> p (a n)").bitcast(F32),
                                      ALU.subtract).then_inc(gu_lo_done, 1)
                    split(PAIRS * c + f + 1, 1)

            def down(c, normed):
                cuts = (0, 3, 6, 9, DOWN_PAIRS) if normed else (0, DOWN_PAIRS - 1)
                for j, (a, b) in enumerate(zip(cuts, cuts[1:])):
                    with dve.Fori(a, b) as i:
                        for slot in range(2):
                            split(PAIRS * c + i + (UP_PAIRS + 1), slot)
                    if normed:
                        norm_tile(c + 1, j)

            def residual(c, j):
                dve.wait_ge(down_done, FC * c + j + 1)
                dve.wait_ge(res_in[j], 16 * (c + 1))
                dve.tensor_tensor(res[:, j, :], ps[:, 2 * j:2 * j + 2, :].rearrange("p b n -> p (b n)"),
                                  res[:, j, :], ALU.add).then_inc(res_done, 1)

            def final(c):
                for j in range(FC):
                    dve.wait_ge(fsd_done, FC * c + j + 1)
                    dve.reciprocal(rs[:, 1, j:j + 1], sd[:, 1, j:j + 1]).then_inc(frs_done, 1)
                    dve.wait_ge(frs_done, FC * c + j + 1)
                    dve.scalar_tensor_tensor(res[:, j, :], res[:, j, :], rs[:, 1, j:j + 1], g_final[:],
                                             ALU.mult, ALU.mult).then_inc(fin_done, 1)

            dve.sem_inc(w_lo_done, 2)
            dve.sem_inc(h_lo_done, 2)
            dve.sem_inc(gu_done, 1)
            dve.sem_inc(res_done, FC)
            dve.wait_ge(const_in, 32)
            split(0, 0)
            split(0, 1)
            for j in range(FC):
                norm_tile(0, j)
            evac(0)
            with dve.Fori(0, NFC - 1) as c:
                up(c)
                down(c, True)
                residual(c, 0)
                residual(c, 1)
                evac(c + 1)
                residual(c, 2)
                residual(c, 3)
                final(c)
            up(NFC - 1)
            down(NFC - 1, False)
            for j in range(FC):
                residual(NFC - 1, j)
            final(NFC - 1)

        @block.tensor
        def _(pe):
            pe.sem_inc(w_used, 2)
            with pe.Fori(0, NFC) as c:
                pe.wait_ge(xn_done, FC * (c + 1))
                pe.wait_ge(res_done, FC * c + 1)
                for k in range(KT):
                    pe.wait_ge(h_lo_done, KT * c + k + 1)
                    if k == KT - 1:
                        pe.wait_ge(res_done, FC * c + 2)
                    for j in range(FC):
                        last = pe.transpose(ps[:, k % 2, j * P:(j + 1) * P], x2[:, j, k * P:(k + 1) * P], ident[:])
                    last.then_inc(t_done, 1)
                with pe.Fori(0, UP_PAIRS) as f:
                    for a in range(2):
                        pe.wait_ge(w_lo_done, 2 * PAIRS * c + 2 * f + a + 3)
                        pe.wait_ge(gu_done if a else silu_done, UP_PAIRS * c + f + 1)
                        for k in range(KT):
                            if a == 0:
                                pe.wait_ge(h_lo_done, KT * c + k + 3)
                            w = slice(k * P, (k + 1) * P)
                            last = matmul3(pe, ps[:, 2 + a, :], w_hi[:, a, w], w_lo[:, a, w],
                                           hT_hi[:, k, :], hT_lo[:, k, :], k == 0, k == KT - 1)
                        last.then_inc(w_used, 1)
                pe.wait_ge(res_done, FC * c + FC)
                for f in range(FT):
                    slot = f % 2
                    pe.wait_ge(w_lo_done, 2 * PAIRS * c + (2 * UP_PAIRS + f + 3))
                    pe.wait_ge(gu_lo_done, UP_PAIRS * c + f + 1)
                    if f == 0:
                        pe.wait_ge(silu_done, UP_PAIRS * c + UP_PAIRS + 1)
                        pe.wait_ge(gu_done, UP_PAIRS * c + UP_PAIRS + 1)
                    for j in range(FC):
                        t = slice(j * P, (j + 1) * P)
                        for half in range(2):
                            w = slice(half * 512, (half + 1) * 512)
                            last = matmul3(pe, ps[:, 2 * j + half, :], gu_hi[:, f, t], gu_lo[:, f, t],
                                           w_hi[:, slot, w], w_lo[:, slot, w], f == 0, f == FT - 1)
                        if f == FT - 1:
                            last.then_inc(down_done, 1)
                    if f < FT - 1:
                        last.then_inc(w_used, 1)
                pe.wait_ge(down_done, FC * (c + 1))
                pe.sem_inc(w_used, 1)


def build(nc, x, meta_tokens, norm_mix, w_in, q_norm, k_norm, attn_out_norm, w_pool, pool_scale, w_out,
          norm_ffn, w_ffn_in, w_ffn_down, norm_final, rope, ident, corr, out):
    m = Shared()
    m.ident_in, m.corr_in = ident, corr
    m.q_d = nc.dram_tensor("q_d", (SEQ, DA), F32).ap()
    m.u_d = nc.dram_tensor("u_d", (GROUPS, P, L), F32).ap()
    m.o_d = nc.dram_tensor("o_d", (SEQ, DA), F32).ap()
    m.x2_d = nc.dram_tensor("x2_d", (SEQ, D), F32).ap()
    with ExitStack() as ctx:
        m.ident = ctx.enter_context(nc.sbuf_tensor("ident", [P, P], F32))
        m.eps = ctx.enter_context(nc.sbuf_tensor("eps", [P, 1], F32))
        m.ps = ctx.enter_context(nc.psum_tensor("ps", [P, 8, 512], F32))
        m.eps_set = ctx.enter_context(nc.semaphore("eps_set"))
        m.v_ones_set = ctx.enter_context(nc.semaphore("v_ones_set"))
        with ExitStack() as kv:
            m.k_st = kv.enter_context(nc.sbuf_tensor("k_st", [P, KV, L], F32R))
            m.v_st = kv.enter_context(nc.sbuf_tensor("v_st", [P, NKT, KV, 2 * HD + 1], F32R))
            project(nc, m, x, meta_tokens, rope, w_in, norm_mix, q_norm, k_norm)
            attend(nc, m)
        mix(nc, m, x, w_pool, w_out, attn_out_norm, pool_scale)
        feed(nc, m, w_ffn_in, w_ffn_down, norm_ffn, norm_final, out)


def shape_tables():
    pairs = HD // 4
    f32 = np.float32
    t = np.arange(SEQ)
    row = (t // GRID_W - SEQ // GRID_W // 2).astype(f32)
    col = (t % GRID_W - GRID_W // 2).astype(f32)
    freqs = f32(ROPE_THETA) ** (-np.arange(pairs, dtype=f32) / f32(pairs))
    ang = np.zeros((L, 2, pairs), f32)
    ang[:SEQ, 0] = row[:, None] * freqs
    ang[:SEQ, 1] = col[:, None] * freqs
    cos, sin = np.cos(ang), np.sin(ang)
    table = np.stack([np.stack([cos, cos], 2), np.stack([-sin, sin], 2)], 1)
    corr = np.ones((P, GROUPS, 9), f32)
    for g, w in enumerate(WINDOWS):
        corr[:, g, 8] = 1.0 / w
        for i in range(8):
            pos = L - 8 + i
            corr[:, g, i] = w / (min(pos + w // 2, L) - (pos - w // 2))
    return table.reshape(L, 2 * HD).astype(f32), np.eye(P, dtype=f32), corr


def kernel(x, meta_tokens, norm_mix, w_in, q_norm, k_norm, attn_out_norm, w_pool, pool_scale, w_out,
           norm_ffn, w_ffn_in, w_ffn_down, norm_final):
    import concourse.bacc as bacc
    from concourse.bass_utils import run_bass_kernel_spmd

    nc = bacc.Bacc("TRN2", target_bir_lowering=False, num_devices=1)
    rope, ident, corr = shape_tables()
    columns = lambda g: g.reshape(-1, P).T
    given = {
        "x": x[0], "meta_tokens": meta_tokens, "norm_mix": columns(norm_mix[0]), "w_in": w_in[0], "q_norm": q_norm[0],
        "k_norm": k_norm[0], "attn_out_norm": columns(attn_out_norm[0]), "w_pool": w_pool[0], "pool_scale": columns(pool_scale[0]),
        "w_out": w_out[0], "norm_ffn": columns(norm_ffn[0]), "w_ffn_in": w_ffn_in[0], "w_ffn_down": w_ffn_down[0],
        "norm_final": norm_final, "rope": rope, "ident": ident, "corr": corr,
    }
    arrays = {f"in_{k}": np.ascontiguousarray(v) for k, v in given.items()}
    args = [nc.dram_tensor(k, a.shape, mybir.dt.from_np(a.dtype), kind="ExternalInput").ap() for k, a in arrays.items()]
    out = nc.dram_tensor("out_x", (SEQ, D), F32, kind="ExternalOutput").ap()
    build(nc, *args, out)
    r = run_bass_kernel_spmd(nc, [arrays], core_ids=[0])
    return r.results[0]["out_x"].reshape(1, SEQ, D)
```

```python
from contextlib import ExitStack

import numpy as np

import concourse.bass as bass
import concourse.mybir as mybir

F32 = mybir.dt.float32
F32R = mybir.dt.float32r
ACT = mybir.ActivationFunctionType
ALU = mybir.AluOpType
AX = mybir.AxisListType
ds = bass.ds

P = 128
D = 1024
SEQ = 2048
META = 16
GRID_W = 64
HEADS, KV, HD = 8, 2, 64
DA = HEADS * HD
DKV = KV * HD
DP = 512
GROUPS = 4
WINDOWS = (2, 4, 8, 16)
DIN = DA + 2 * DKV + DP
DFF = 2816
EPS = 1e-6
ROPE_THETA = 10000.0

L = META + SEQ
KT = D // P
NT = SEQ // P
CT = 2
CW = CT * P
NCH = NT // CT
U0 = DA + 2 * DKV
UPAD = L + 16
NKT = NT + 1
QK = DA + DKV
NH = HEADS + KV
WO_AHEAD = 4
FT = DFF // P
FC = 4
FW = FC * P
NFC = NT // FC


def split_hi(act, hi, src, scale=1.0):
    return act.activation(hi, src, ACT.Copy, scale=scale)


def matmul3(pe, out, st_hi, st_lo, mv_hi, mv_lo, start, stop):
    pe.matmul(out, st_hi, mv_hi, start=start, stop=False)
    pe.matmul(out, st_hi, mv_lo, start=False, stop=False)
    return pe.matmul(out, st_lo, mv_hi, start=False, stop=stop)


class Shared:
    pass


def project(nc, m, x, meta, rope, w_in, norm_mix, q_norm, k_norm):
    with ExitStack() as ctx:
        sb = lambda n, s, d=F32: ctx.enter_context(nc.sbuf_tensor(n, s, d))
        sem = lambda n: ctx.enter_context(nc.semaphore(n))
        ident, ps = m.ident, m.ps
        win_hi = sb("win_hi", [P, KT, DIN], F32R)
        win_lo = sb("win_lo", [P, KT, DIN], F32R)
        x_raw = sb("x_raw", [P, CT, D])
        x_meta = sb("x_meta", [META, D])
        xn = sb("xn", [P, CT, D])
        xn_meta = sb("xn_meta", [META, D])
        hT_hi = sb("hT_hi", [P, KT, CW + META], F32R)
        hT_lo = sb("hT_lo", [P, KT, CW + META], F32R)
        hm_hi, hm_lo = hT_hi[:, :, CW:], hT_lo[:, :, CW:]
        u_meta = sb("u_meta", [P, GROUPS, META])
        hm = sb("hm", [P, KT, META])
        u_out = sb("u_out", [P, 2, CW])
        w_stage = sb("w_stage", [P, 2, DIN])
        qkv = sb("qkv", [P, CT, QK + DKV])
        sq = sb("sq", [P, QK])
        t1 = sb("t1", [P, QK])
        t2 = sb("t2", [P, QK])
        q_out = sb("q_out", [P, CT, DA])
        k_tok = sb("k_tok", [P, CT, KV, 2, HD])
        cs = sb("cs", [P, CT, 2, HD])
        cs_meta = sb("cs_meta", [META, 2, HD])
        g_in = sb("g_in", [P, KT])
        g_qk = sb("g_qk", [P, 2, HD])
        eps = m.eps
        ssx = sb("ssx", [P, 3])
        sdx = sb("sdx", [P, 3])
        rsx = sb("rsx", [P, 3])
        ssh = sb("ssh", [P, NH])
        sdh = sb("sdh", [P, NH])
        rsh = sb("rsh", [P, NH])

        const_in = sem("p_const_in")
        x_in = [sem(f"p_x_in{j}") for j in range(CT)]
        cs_in = [sem(f"p_cs_in{j}") for j in range(CT)]
        w_staged = [sem(f"p_w_staged{j}") for j in range(2)]
        w_hi_done, w_lo_done = sem("p_w_hi_done"), sem("p_w_lo_done")
        x_ssq, x_sd, x_rs, xn_done = sem("p_x_ssq"), sem("p_x_sd"), sem("p_x_rs"), sem("p_xn_done")
        t_done, h_hi_done, h_lo_done = sem("p_t_done"), sem("p_h_hi_done"), sem("p_h_lo_done")
        hm_done = sem("p_hm_done")
        u_done, u_evac = sem("p_u_done"), sem("p_u_evac")
        u_meta_evac, u_meta_store = sem("p_u_meta_evac"), sem("p_u_meta_store")
        u_store = [sem(f"p_u_store{j}") for j in range(2)]
        q_done, q_evac, kv_done, kv_evac = sem("p_q_done"), sem("p_q_evac"), sem("p_kv_done"), sem("p_kv_evac")
        sq_done, gain_done, head_sd, v_hi_done = sem("p_sq_done"), sem("p_gain_done"), sem("p_head_sd"), sem("p_v_hi_done")
        post, qkv_free = sem("p_post"), sem("p_qkv_free")
        q_store = [sem(f"p_q_store{j}") for j in range(CT)]
        kt_done, k_hi_done, k_lo_done = sem("p_kt_done"), sem("p_k_hi_done"), sem("p_k_lo_done")

        POST = 9

        block = ctx.enter_context(nc.Block())

        @block.sync
        def _(sp):
            for dst, src in (
                (ident[:], m.ident_in),
                (x_meta[:], meta),
                (g_in[:], norm_mix),
                (g_qk[:, 0, :], q_norm.unsqueeze(0).broadcast_to([P, HD])),
                (g_qk[:, 1, :], k_norm.unsqueeze(0).broadcast_to([P, HD])),
                (cs_meta[:], rope[SEQ:L].rearrange("p (a n) -> p a n", a=2)),
            ):
                sp.dma_start(dst, src).then_inc(const_in, 16)
            for j in range(CT):
                sp.dma_start(x_raw[:, j, :], x[j * P:(j + 1) * P]).then_inc(x_in[j], 16)
            for k in range(KT):
                if k >= 2:
                    sp.wait_ge(w_lo_done, k - 1)
                sp.dma_start(w_stage[:, k % 2, :], w_in[k * P:(k + 1) * P]).then_inc(w_staged[k % 2], 16)

            def load_x(c):
                for j in range(CT):
                    sp.wait_ge(xn_done, 2 * c + j)
                    sp.dma_start(x_raw[:, j, :], x[ds(c * CW + j * P, P)]).then_inc(x_in[j], 16)

            load_x(1)
            for j in range(2):
                sp.sem_inc(u_store[j], 16)
            for j in range(CT):
                sp.sem_inc(q_store[j], 16)
            def chunk(c, more):
                for j in range(CT):
                    sp.wait_ge(qkv_free, 2 * c + j + 1)
                    sp.dma_start(cs[:, j], rope[ds(c * CW + j * P, P)].rearrange("p (a n) -> p a n", a=2)).then_inc(cs_in[j], 16)
                if more:
                    load_x(c + 2)
                for f in range(GROUPS):
                    sp.wait_ge(u_evac, 4 * c + f + 1)
                    sp.dma_start(m.u_d[f, :, ds(c * CW + META, CW)], u_out[:, f % 2, :]).then_inc(u_store[f % 2], 16)
                for j in range(CT):
                    sp.wait_ge(post, POST * (2 * c + j + 2))
                    sp.dma_start(m.q_d[ds(c * CW + j * P, P)], q_out[:, j, :]).then_inc(q_store[j], 16)

            with sp.Fori(0, NCH - 2) as c:
                chunk(c, True)
            chunk(NCH - 2, False)
            chunk(NCH - 1, False)
            sp.wait_ge(u_meta_evac, 1)
            sp.dma_start(m.u_d[:, :, 0:META].rearrange("g p n -> p g n"), u_meta[:]).then_inc(u_meta_store, 16)
            sp.wait_ge(u_meta_store, 16)
            sp.wait_ge(u_store[0], 16 * (1 + 2 * NCH))
            sp.wait_ge(u_store[1], 16 * (1 + 2 * NCH))
            for j in range(CT):
                sp.wait_ge(q_store[j], 16 * (NCH + 1))

        @block.gpsimd
        def _(pool):
            def head_gain(n, rows, j, h0):
                lo = h0 * HD
                src = qkv[0:rows, j, lo:QK]
                pool.tensor_tensor(sq[0:rows, lo:QK], src, src, ALU.mult).then_inc(sq_done, 1)
                pool.wait_ge(sq_done, n + 1)
                parts = ([(0, DA, 0)] if h0 == 0 else []) + [(DA, QK, 1)]
                for a, b, which in parts:
                    v = qkv[0:rows, j, a:b].rearrange("p (h n) -> p h n", n=HD)
                    g = g_qk[0:rows, which, :].unsqueeze(1).broadcast_to([rows, (b - a) // HD, HD])
                    pool.tensor_tensor(v, v, g, ALU.mult).then_inc(gain_done, 1)

            pool.wait_ge(const_in, 96)
            pool.wait_ge(kv_evac, 1)
            head_gain(0, META, 1, HEADS)
            with pool.Fori(0, NCH) as c:
                for j in range(CT):
                    pool.wait_ge(q_evac, 2 * c + j + 2)
                    pool.wait_ge(kv_evac, 2 * c + j + 2)
                    pool.wait_ge(post, POST * (2 * c + j) + 2)
                    head_gain(2 * c + j + 1, P, j, 0)

        @block.scalar
        def _(act):
            def norm(n, src, junk, rows, col):
                act.activation(junk, src, ACT.Square, accum_out=ssx[0:rows, col:col + 1]).then_inc(x_ssq, 1)
                act.wait_ge(x_ssq, n)
                act.activation(sdx[0:rows, col:col + 1], ssx[0:rows, col:col + 1], ACT.Sqrt,
                               scale=1.0 / D, bias=eps[0:rows]).then_inc(x_sd, 1)

            def norm_tile(c, j):
                act.wait_ge(x_in[j], 16 * (c + 1))
                act.wait_ge(t_done, 8 * c + 1)
                norm(2 * c + j + 2, x_raw[:, j, :], xn[:, j, :], P, j)

            def head_norm(n, rows, h0):
                act.wait_ge(post, POST * n + 2)
                act.activation(sdh[0:rows, h0:NH], ssh[0:rows, h0:NH], ACT.Sqrt,
                               scale=1.0 / HD, bias=eps[0:rows]).then_inc(head_sd, 1)

            def h_evac(c):
                for k in range(KT):
                    act.wait_ge(t_done, 8 * c + k + 2)
                    split_hi(act, hT_hi[:, k, 0:CW], ps[:, k % 2, 0:CW], g_in[:, k:k + 1]).then_inc(h_hi_done, 1)

            def u_out_evac(c):
                for f in range(GROUPS):
                    act.wait_ge(u_done, 4 * c + f + 1)
                    act.wait_ge(u_store[f % 2], 16 * (2 * c + f // 2 + 1))
                    act.copy(u_out[:, f % 2, :], ps[:, 2 + f, 0:CW]).then_inc(u_evac, 1)

            def k_evac(c):
                for g in range(KV):
                    act.wait_ge(kt_done, 2 * c + g + 2)
                    split_hi(act, m.k_st[:, g, ds(c * CW, CW)], ps[:, g, 0:CW]).then_inc(k_hi_done, 1)

            def qkv_evac(c, j):
                i = 2 * c + j
                act.wait_ge(qkv_free, i + 1)
                act.wait_ge(q_done, i + 1)
                act.copy(qkv[:, j, 0:DA], ps[:, 6, :]).then_inc(q_evac, 1)
                act.wait_ge(kv_done, i + 2)
                act.copy(qkv[:, j, DA:], ps[:, 7, 0:2 * DKV]).then_inc(kv_evac, 1)
                act.wait_ge(kv_evac, i + 2)
                v = qkv[:, j, QK:].rearrange("p (g n) -> p g n", g=KV)
                act.copy(m.v_st[:, ds(i, 1), :, 0:HD].rearrange("p a g n -> p (a g) n"), v).then_inc(v_hi_done, 1)

            def k_meta_evac():
                act.wait_ge(kt_done, 1)
                split_hi(act, m.k_st[:, :, SEQ:L],
                         ps[:, 0, 0:KV * META].rearrange("p (g n) -> p g n", g=KV)).then_inc(k_hi_done, 1)

            def chunk(c, first=False, last=False):
                if not last:
                    for j in range(CT):
                        norm_tile(c + 1, j)
                qkv_evac(c, 0)
                if first:
                    k_meta_evac()
                else:
                    k_evac(c - 1)
                head_norm(2 * c + 1, P, 0)
                if first:
                    act.wait_ge(u_done, GROUPS)
                    act.copy(u_meta[:], ps[:, 2:6, CW:CW + META]).then_inc(u_meta_evac, 1)
                    u_out_evac(0)
                    h_evac(1)
                    qkv_evac(0, 1)
                else:
                    qkv_evac(c, 1)
                    if last:
                        head_norm(2 * c + 2, P, 0)
                    else:
                        h_evac(c + 1)
                    u_out_evac(c)
                if not last:
                    head_norm(2 * c + 2, P, 0)

            act.wait_ge(m.eps_set, 1)
            act.wait_ge(const_in, 96)
            norm(1, x_meta[:], xn_meta[:], META, 2)
            act.wait_ge(hm_done, 1)
            split_hi(act, hm_hi, hm[:]).then_inc(h_hi_done, 1)
            for j in range(CT):
                norm_tile(0, j)
            h_evac(0)
            for k in range(KT):
                act.wait_ge(w_staged[k % 2], 16 * (k // 2 + 1))
                split_hi(act, win_hi[:, k, :], w_stage[:, k % 2, :]).then_inc(w_hi_done, 1)
            act.sem_inc(q_evac, 1)
            act.wait_ge(kv_done, 1)
            act.copy(qkv[0:META, 1, DA:], ps[0:META, 0, 0:2 * DKV]).then_inc(kv_evac, 1)
            act.wait_ge(kv_evac, 1)
            act.copy(m.v_st[0:META, NT, :, 0:HD],
                     qkv[0:META, 1, QK:].rearrange("p (g n) -> p g n", g=KV)).then_inc(v_hi_done, 1)
            head_norm(0, META, HEADS)
            chunk(0, first=True)
            with act.Fori(1, NCH - 1) as c:
                chunk(c)
            chunk(NCH - 1, last=True)
            k_evac(NCH - 1)

        @block.vector
        def _(dve):
            dve.memset(eps[:], EPS).then_inc(m.eps_set, 1)
            dve.memset(m.v_st[:, :, :, HD].bitcast(F32), 1.0).then_inc(m.v_ones_set, 1)
            dve.sem_inc(h_lo_done, 1)
            dve.sem_inc(k_lo_done, 2)
            dve.sem_inc(qkv_free, 1)

            def norm(n, out, src, rows, col):
                dve.wait_ge(x_sd, n)
                dve.reciprocal(rsx[0:rows, col:col + 1], sdx[0:rows, col:col + 1]).then_inc(x_rs, 1)
                dve.wait_ge(x_rs, n)
                dve.tensor_scalar(out, src, rsx[0:rows, col:col + 1], None, ALU.mult).then_inc(xn_done, 1)

            def norm_tile(c, j):
                norm(2 * c + j + 2, xn[:, j, :], x_raw[:, j, :], P, j)

            def h_evac(c):
                for k in range(KT):
                    dve.wait_ge(h_hi_done, 8 * c + k + 2)
                    dve.scalar_tensor_tensor(hT_lo[:, k, 0:CW], ps[:, k % 2, 0:CW], g_in[:, k:k + 1],
                                             hT_hi[:, k, 0:CW].bitcast(F32), ALU.mult, ALU.subtract).then_inc(h_lo_done, 1)

            def k_evac(c):
                for g in range(KV):
                    dve.wait_ge(k_hi_done, 2 * c + g + 2)
                    lo = m.k_st[HD:P, g, ds(c * CW, CW)]
                    dve.tensor_tensor(lo, ps[HD:P, g, 0:CW], lo.bitcast(F32), ALU.subtract).then_inc(k_lo_done, 1)

            def post_tile(n, rows, j, h0, v_lo, v_hi, table):
                base = POST * n
                lo, nh = h0 * HD, NH - h0
                dve.wait_ge(v_hi_done, n + 1)
                v = qkv[0:rows, j, QK:].rearrange("p (g n) -> p g n", g=KV)
                dve.tensor_tensor(v_lo, v, v_hi.bitcast(F32), ALU.subtract).then_inc(post, 1)
                dve.wait_ge(sq_done, n + 1)
                dve.tensor_reduce(ssh[0:rows, h0:NH], sq[0:rows, lo:QK].rearrange("p (h n) -> p h n", n=HD),
                                  AX.X, ALU.add).then_inc(post, 1)
                dve.wait_ge(gain_done, 2 * n + 1)
                if h0 == 0:
                    dve.wait_ge(post, base)
                cos = table[:, 0, :].unsqueeze(1).broadcast_to([rows, nh, HD])
                r3 = qkv[0:rows, j, lo:QK].rearrange("p (h n) -> p h n", n=HD)
                t1v = t1[0:rows, lo:QK].rearrange("p (h n) -> p h n", n=HD)
                dve.tensor_tensor(t1v, r3, cos, ALU.mult).then_inc(post, 1)
                r5 = qkv[0:rows, j, lo:QK].rearrange("p (h b n) -> p h b n", b=2, n=HD // 4)
                t5 = t2[0:rows, lo:QK].rearrange("p (h b n) -> p h b n", b=2, n=HD // 4)
                s5 = table[:, 1, :].rearrange("p (a b n) -> p a b n", a=2, b=2)
                for b in range(2):
                    src = r5[:, :, 1 - b, :].rearrange("p (h a) n -> p h a n", a=2)
                    dst = t5[:, :, b, :].rearrange("p (h a) n -> p h a n", a=2)
                    sin = s5[:, :, b, :].unsqueeze(1).broadcast_to([rows, nh, 2, HD // 4])
                    dve.tensor_tensor(dst, src, sin, ALU.mult).then_inc(post, 1)
                dve.wait_ge(post, base + 5)
                dve.sem_inc(qkv_free, 1)
                dve.tensor_tensor(t1[0:rows, lo:QK], t1[0:rows, lo:QK], t2[0:rows, lo:QK], ALU.add).then_inc(post, 1)
                dve.wait_ge(head_sd, n + 1)
                dve.reciprocal(rsh[0:rows, h0:NH], sdh[0:rows, h0:NH]).then_inc(post, 1)
                dve.wait_ge(post, base + 7)
                k_in = t1[0:rows, DA:QK].rearrange("p (g n) -> p g n", g=KV)
                rk = rsh[0:rows, HEADS:NH]
                if h0:
                    for dup in range(2):
                        dve.tensor_tensor(k_tok[0:rows, j, :, dup, :], k_in,
                                          rk.unsqueeze(2).broadcast_to([rows, KV, HD]), ALU.mult).then_inc(post, 1)
                else:
                    for g in range(KV):
                        last = dve.tensor_tensor(
                            k_tok[0:rows, j, g, :, :], k_in[:, g, :].unsqueeze(1).broadcast_to([rows, 2, HD]),
                            rk[:, g:g + 1].unsqueeze(2).broadcast_to([rows, 2, HD]), ALU.mult)
                        if g == KV - 1:
                            last.then_inc(post, 1)

            def post_full(c, j):
                i = 2 * c + j
                dve.wait_ge(cs_in[j], 16 * (c + 1))
                v = m.v_st[:, ds(i, 1), :, :].rearrange("p a g n -> p (a g) n")
                post_tile(i + 1, P, j, 0, v[:, :, HD + 1:], v[:, :, 0:HD], cs[:, j])
                dve.wait_ge(q_store[j], 16 * (c + 1))
                dve.tensor_tensor(q_out[:, j, :].rearrange("p (h n) -> p h n", n=HD),
                                  t1[:, 0:DA].rearrange("p (h n) -> p h n", n=HD),
                                  rsh[:, 0:HEADS].unsqueeze(2).broadcast_to([P, HEADS, HD]), ALU.mult).then_inc(post, 1)

            def k_meta_evac():
                dve.wait_ge(k_hi_done, 1)
                lo = m.k_st[HD:P, :, SEQ:L]
                dve.tensor_tensor(lo, ps[HD:P, 0, 0:KV * META].rearrange("p (g n) -> p g n", g=KV),
                                  lo.bitcast(F32), ALU.subtract).then_inc(k_lo_done, 1)

            def chunk(c, first=False, last=False):
                if not last:
                    for j in range(CT):
                        norm_tile(c + 1, j)
                if first:
                    k_meta_evac()
                else:
                    k_evac(c - 1)
                post_full(c, 0)
                if not last:
                    h_evac(c + 1)
                post_full(c, 1)

            dve.wait_ge(const_in, 96)
            norm(1, xn_meta[:], x_meta[:], META, 2)
            dve.wait_ge(t_done, 1)
            dve.tensor_tensor(hm[:], ps[:, 1, 0:KT * META].rearrange("p (k n) -> p k n", k=KT),
                              g_in[:].unsqueeze(2).broadcast_to([P, KT, META]), ALU.mult).then_inc(hm_done, 1)
            dve.wait_ge(h_hi_done, 1)
            dve.tensor_tensor(hm_lo, hm[:], hm_hi.bitcast(F32), ALU.subtract).then_inc(h_lo_done, 1)
            for j in range(CT):
                norm_tile(0, j)
            h_evac(0)
            for k in range(KT):
                dve.wait_ge(w_hi_done, k + 1)
                dve.tensor_tensor(win_lo[:, k, :], w_stage[:, k % 2, :], win_hi[:, k, :].bitcast(F32),
                                  ALU.subtract).then_inc(w_lo_done, 1)
            post_tile(0, META, 1, HEADS, m.v_st[0:META, NT, :, HD + 1:], m.v_st[0:META, NT, :, 0:HD], cs_meta)
            chunk(0, first=True)
            with dve.Fori(1, NCH - 1) as c:
                chunk(c)
            chunk(NCH - 1, last=True)
            k_evac(NCH - 1)

        @block.tensor
        def _(pe):
            pe.wait_ge(const_in, 96)
            pe.wait_ge(xn_done, 1)
            for k in range(KT):
                last = pe.transpose(ps[:, 1, k * META:(k + 1) * META], xn_meta[:, k * P:(k + 1) * P],
                                    ident[0:META, 0:META])
            last.then_inc(t_done, 1)

            def h_transpose(c, k):
                pe.wait_ge(h_lo_done, 8 * c + k + 1)
                if k < 2:
                    pe.wait_ge(k_lo_done, 2 * c + 1)
                for j in range(CT):
                    last = pe.transpose(ps[:, k % 2, j * P:(j + 1) * P], xn[:, j, k * P:(k + 1) * P], ident[:])
                last.then_inc(t_done, 1)

            def u_products(c, k, first=False):
                if k == 0 and not first:
                    pe.wait_ge(u_evac, 4 * c)
                n = CW + META if first else CW
                for f in range(GROUPS):
                    w = slice(U0 + f * P, U0 + (f + 1) * P)
                    last = matmul3(pe, ps[:, 2 + f, 0:n], win_hi[:, k, w], win_lo[:, k, w],
                                   hT_hi[:, k, 0:n], hT_lo[:, k, 0:n], k == 0, k == KT - 1)
                    if k == KT - 1:
                        last.then_inc(u_done, 1)

            def k_transpose(c):
                pe.wait_ge(post, POST * (2 * c + 2) + POST - 1)
                for g in range(KV):
                    for j in range(CT):
                        last = pe.transpose(ps[:, g, j * P:(j + 1) * P],
                                            k_tok[:, j, g, :, :].rearrange("p a n -> p (a n)"), ident[:])
                    last.then_inc(kt_done, 1)

            def q_product(j, k):
                t = slice(j * P, (j + 1) * P)
                last = matmul3(pe, ps[:, 6, :], hT_hi[:, k, t], hT_lo[:, k, t],
                               win_hi[:, k, 0:DA], win_lo[:, k, 0:DA], k == 0, k == KT - 1)
                if k == KT - 1:
                    last.then_inc(q_done, 1)

            def kv_product(out, t, k):
                last = matmul3(pe, out, hT_hi[:, k, t], hT_lo[:, k, t],
                               win_hi[:, k, DA:U0], win_lo[:, k, DA:U0], k == 0, k == KT - 1)
                if k == KT - 1:
                    last.then_inc(kv_done, 1)

            def qkv_products(c, j, first=False):
                pe.wait_ge(q_evac, 2 * c + j + 1)
                for k in range(KT):
                    if j == 0:
                        pe.wait_ge(h_lo_done, 8 * c + k + 3)
                    q_product(j, k)
                if first:
                    k_meta_transpose()
                pe.wait_ge(kv_evac, 2 * c + j + 1)
                for k in range(KT):
                    kv_product(ps[:, 7, 0:2 * DKV], slice(j * P, (j + 1) * P), k)
                    if first:
                        if k == 0:
                            pe.wait_ge(xn_done, 5)
                        h_transpose(1, k)

            def opening():
                pe.wait_ge(h_lo_done, KT + 2)
                for k in range(KT):
                    pe.wait_ge(w_lo_done, k + 1)
                    u_products(0, k, first=True)
                    kv_product(ps[0:META, 0, 0:2 * DKV], slice(CW, CW + META), k)
                    q_product(0, k)
                    kv_product(ps[:, 7, 0:2 * DKV], slice(0, P), k)

            def k_meta_transpose():
                pe.wait_ge(post, POST)
                for g in range(KV):
                    last = pe.transpose(ps[:, 0, g * META:(g + 1) * META],
                                        k_tok[0:META, 1, g, :, :].rearrange("p a n -> p (a n)"), ident[0:META, 0:META])
                last.then_inc(kt_done, 1)

            def chunk(c, last=False):
                qkv_products(c, 0)
                k_transpose(c - 1)
                qkv_products(c, 1)
                if not last:
                    pe.wait_ge(xn_done, 2 * c + 5)
                for k in range(KT):
                    u_products(c, k)
                    if not last:
                        h_transpose(c + 1, k)

            pe.wait_ge(xn_done, 3)
            for k in range(KT):
                h_transpose(0, k)
            opening()
            qkv_products(0, 1, first=True)
            with pe.Fori(1, NCH - 1) as c:
                chunk(c)
            chunk(NCH - 1, last=True)
            k_transpose(NCH - 1)


def attend(nc, m, w_pool, w_out):
    HG = HEADS // KV
    W = HG * P
    ROW = 2 * HD
    HALF = 1024
    CHUNKS = 2 * HG
    SCALE = HD ** -0.5
    RING, P_RING = 9, 6
    LAG = 4
    CHUNK_AT = (1, 3, 4, 6, 7, 9, 10, 12)
    OUT_AT, TAIL_AT, Q2_AT = 6, 8, 15
    with ExitStack() as ctx:
        sb = lambda n, s, d=F32: ctx.enter_context(nc.sbuf_tensor(n, s, d))
        sem = lambda n: ctx.enter_context(nc.semaphore(n))
        ident, ps = m.ident, m.ps
        k_one = sb("k_one", [HD + 1, KV, L], F32R)
        q_raw = sb("q_raw", [P, KV, HG, ROW + 1])
        q_hi = sb("q_hi", [P, KV, W], F32R)
        q_lo = sb("q_lo", [HD + 1, KV, W], F32R)
        probs = sb("probs", [P, P_RING, W])
        p_hi = sb("p_hi", [P, RING, W], F32R)
        p_lo = sb("p_lo", [P, RING, W], F32R)
        oT = sb("oT", [HD + 1, W])
        o_out = sb("o_out", [P, KV, HG * HD])
        mx = sb("mx", [P, KV, HG, 3])
        mx_all = sb("mx_all", [P, HG])
        rden = sb("rden", [P, HG])
        window_sums = [sb(f"window_sums{j}", [P, UPAD]) for j in range(2)]
        corr = sb("corr", [P, GROUPS, 8])

        u_in, pooled, w_out_in = sem("a_u_in"), sem("a_pooled"), sem("a_w_out_in")
        k_copied = sem("a_k_copied")
        q_in = [sem(f"a_q_in{g}") for g in range(KV)]
        o_store = [sem(f"a_o_store{g}") for g in range(KV)]
        ones_set = sem("a_ones_set")
        q_turned, q_hi_done, q_lo_done = sem("a_q_turned"), sem("a_q_hi_done"), sem("a_q_lo_done")
        q_max_turned = sem("a_q_max_turned")
        chunk_done, chunk_max = sem("a_chunk_done"), sem("a_chunk_max")
        tail_done, tail_max = sem("a_tail_done"), sem("a_tail_max")
        max_done, neg_max_done = sem("a_max_done"), sem("a_neg_max_done")
        scored, exp_done, hi_done, lo_done = sem("a_scored"), sem("a_exp_done"), sem("a_hi_done"), sem("a_lo_done")
        valued, oT_done = sem("a_valued"), sem("a_oT_done")
        out_done, rden_done, o_done = sem("a_out_done"), sem("a_rden_done"), sem("a_o_done")
        VALUES, MISC = 6, 7

        def rows(kt):
            return P if kt < NT else META

        def before(kt, ring):
            if kt >= ring:
                return 0, kt - ring
            return 1, kt + ring * ((NKT - 1 - kt) // ring)

        block = ctx.enter_context(nc.Block())

        @block.sync
        def _(sp):
            def load_q(qt, g):
                src = m.q_d[ds(qt * P, P), g * HG * HD:(g + 1) * HG * HD].rearrange("p (h n) -> p h n", n=HD)
                for a in range(2):
                    sp.dma_start(q_raw[:, g, :, a * HD:(a + 1) * HD], src).then_inc(q_in[g], 16)

            def step(qt, g, ahead=True):
                s = 2 * qt + g
                if ahead:
                    sp.wait_ge(q_max_turned, s + 2)
                    load_q(qt + 1 + g, 1 - g)
                sp.wait_ge(o_done, s + 1)
                sp.dma_start(m.o_d[ds(qt * P, P), g * HG * HD:(g + 1) * HG * HD], o_out[:, g, :]).then_inc(o_store[g], 16)

            load_q(0, 0)
            load_q(0, 1)
            for g in range(KV):
                sp.sem_inc(o_store[g], 16)
            sp.wait_ge(q_max_turned, 1)
            load_q(1, 0)
            sp.dma_start(m.u_sb[:, :, 0:L], m.u_d.rearrange("g p n -> p g n")).then_inc(u_in, 16)
            sp.dma_start(corr[:], m.corr_in).then_inc(u_in, 16)
            sp.dma_start(m.wp_raw[:], w_pool.rearrange("g p n -> p g n")).then_inc(w_out_in, 16)
            for k in range(WO_AHEAD):
                sp.dma_start(m.wo_raw[:, k, :], w_out[k * P:(k + 1) * P]).then_inc(w_out_in, 16)
            with sp.Fori(0, NT - 2) as qt:
                for g in range(KV):
                    step(qt, g)
            step(NT - 2, 0)
            step(NT - 2, 1, ahead=False)
            for g in range(KV):
                step(NT - 1, g, ahead=False)
            sp.wait_ge(w_out_in, 16 * (WO_AHEAD + 1))
            for g in range(KV):
                sp.wait_ge(o_store[g], 16 * (NT + 1))

        @block.gpsimd
        def _(pool):
            pooling_windows(pool, m.u_sb, window_sums, corr, u_in, pooled)

        @block.tensor
        def _(pe):
            def turn_q(x, g, loads):
                pe.wait_ge(q_in[g], 32 * loads)
                if not isinstance(x, int) or x > 0:
                    pe.wait_ge(q_lo_done, x)
                for h in range(HG):
                    last = pe.transpose(ps[:, MISC, h * P:(h + 1) * P], q_raw[:, g, h, 0:ROW], ident[:])
                last.then_inc(q_turned, 1)

            def score_chunk(x, g, c):
                h, half = c // 2, c % 2
                if c == 0:
                    pe.wait_ge(q_hi_done, x + 1)
                if c >= 2 or not isinstance(x, int) or x > 0:
                    pe.wait_ge(chunk_max, CHUNKS * x + c - 1)
                for b in range(2):
                    k0 = HALF * half + 512 * b
                    last = pe.matmul(ps[:, 2 * half + b, :], q_hi[:, g, h * P:(h + 1) * P],
                                     m.k_st[:, g, k0:k0 + 512], start=True, stop=True)
                last.then_inc(chunk_done, 1)

            def score_tail(x, g):
                for h in range(HG):
                    last = pe.matmul(ps[:, MISC, h * META:(h + 1) * META], q_hi[:, g, h * P:(h + 1) * P],
                                     m.k_st[:, g, SEQ:L], start=True, stop=True)
                last.then_inc(tail_done, 1)

            def turn_max(x, g):
                pe.wait_ge(neg_max_done, x + 1)
                for h in range(HG):
                    last = pe.transpose(ps[0:HD + 1, MISC, h * P:(h + 1) * P], q_raw[:, g, h, HD:ROW + 1], ident[:])
                last.then_inc(q_max_turned, 1)

            def score(s, g, kt):
                r, bank = rows(kt), 4 + (g + kt) % 2
                if kt == 0:
                    pe.wait_ge(q_lo_done, s + 1)
                if kt >= 2 or not isinstance(s, int) or s > 0:
                    pe.wait_ge(exp_done, NKT * s + kt - 1)
                keys = slice(kt * P, kt * P + r)
                pe.matmul(ps[0:r, bank, :], m.k_st[:, g, keys], q_hi[:, g, :], start=True, stop=False)
                pe.matmul(ps[0:r, bank, :], k_one[:, g, keys], q_lo[:, g, :], start=False, stop=True).then_inc(scored, 1)

            def values(s, g, kt):
                r = rows(kt)
                pe.wait_ge(lo_done, NKT * s + kt + 1)
                if kt == 0 and (not isinstance(s, int) or s > 0):
                    pe.wait_ge(oT_done, s)
                v_hi_one, v_lo = m.v_st[0:r, kt, g, 0:HD + 1], m.v_st[0:r, kt, g, HD + 1:]
                hi, lo = p_hi[0:r, kt % RING, :], p_lo[0:r, kt % RING, :]
                pe.matmul(ps[0:HD + 1, VALUES, :], v_hi_one, hi, start=kt == 0, stop=False)
                pe.matmul(ps[0:HD, VALUES, :], v_lo, hi, start=False, stop=False)
                pe.matmul(ps[0:HD + 1, VALUES, :], v_hi_one, lo, start=False, stop=kt == NKT - 1).then_inc(valued, 1)

            def output(s):
                pe.wait_ge(oT_done, s + 1)
                for h in range(HG):
                    last = pe.transpose(ps[:, MISC, h * (HD + 1):(h + 1) * (HD + 1)], oT[:, h * P:(h + 1) * P],
                                        ident[0:HD + 1, 0:HD + 1])
                last.then_inc(out_done, 1)

            def step(qt, g, first=False, prepare=True):
                s, og = 2 * qt + g, 1 - g
                for kt in range(NKT):
                    score(s, g, kt)
                    if prepare:
                        if kt == 0:
                            turn_q(s + 1, og, qt + 1 + g)
                        if kt in CHUNK_AT:
                            score_chunk(s + 1, og, CHUNK_AT.index(kt))
                        if kt == TAIL_AT:
                            if not first:
                                pe.wait_ge(o_done, s)
                            score_tail(s + 1, og)
                        if kt == Q2_AT:
                            turn_max(s + 1, og)
                    if kt >= LAG:
                        values(s, g, kt - LAG)
                    elif not first:
                        values(s - 1, og, NKT + kt - LAG)
                    if kt == OUT_AT and not first:
                        if prepare:
                            pe.wait_ge(q_hi_done, s + 2)
                        output(s - 1)

            pe.wait_ge(ones_set, 1)
            turn_q(0, 0, 1)
            for c in range(CHUNKS):
                score_chunk(0, 0, c)
                if c == 0:
                    score_tail(0, 0)
            turn_max(0, 0)
            pe.wait_ge(k_copied, 1)
            step(0, 0, first=True)
            step(0, 1)
            with pe.Fori(1, NT - 1) as qt:
                for g in range(KV):
                    step(qt, g)
            step(NT - 1, 0)
            step(NT - 1, 1, prepare=False)
            for kt in range(NKT - LAG, NKT):
                values(2 * NT - 1, 1, kt)
            pe.wait_ge(o_done, 2 * NT - 1)
            output(2 * NT - 1)

        @block.scalar
        def _(act):
            def q_high(x, g):
                act.wait_ge(q_turned, x + 1)
                split_hi(act, q_hi[:, g, :], ps[:, MISC, :]).then_inc(q_hi_done, 1)

            def exp(s, g, kt):
                r = rows(kt)
                act.wait_ge(scored, NKT * s + kt + 1)
                back, last = before(kt, P_RING)
                if not (isinstance(s, int) and s < back):
                    act.wait_ge(lo_done, NKT * (s - back) + last + 1)
                act.activation(probs[0:r, kt % P_RING, :], ps[0:r, 4 + (g + kt) % 2, :], ACT.Exp,
                               scale=SCALE).then_inc(exp_done, 1)

            def high(s, kt):
                r = rows(kt)
                act.wait_ge(exp_done, NKT * s + kt + 1)
                back, last = before(kt, RING)
                if not (isinstance(s, int) and s < back):
                    act.wait_ge(valued, NKT * (s - back) + last + 1)
                split_hi(act, p_hi[0:r, kt % RING, :], probs[0:r, kt % P_RING, :]).then_inc(hi_done, 1)

            def output(s):
                act.wait_ge(valued, NKT * (s + 1))
                if not (isinstance(s, int) and s == 0):
                    act.wait_ge(out_done, s)
                act.copy(oT[:], ps[0:HD + 1, VALUES, :]).then_inc(oT_done, 1)

            def step(s, g, first=False, prepare=True):
                for kt in range(NKT):
                    exp(s, g, kt)
                    if kt == 0 and prepare:
                        q_high(s + 1, 1 - g)
                    if kt:
                        high(s, kt - 1)
                    if kt == LAG - 1 and not first:
                        output(s - 1)
                high(s, NKT - 1)

            q_high(0, 0)
            act.copy(k_one[0:HD], m.k_st[0:HD].bitcast(F32)).then_inc(k_copied, 1)
            step(0, 0, first=True)
            step(1, 1)
            with act.Fori(1, NT - 1) as qt:
                for g in range(KV):
                    step(2 * qt + g, g)
            step(2 * NT - 2, 0)
            step(2 * NT - 1, 1, prepare=False)
            output(2 * NT - 1)

        @block.vector
        def _(dve):
            def low(s, kt):
                r = rows(kt)
                dve.wait_ge(hi_done, NKT * s + kt + 1)
                dve.tensor_tensor(p_lo[0:r, kt % RING, :], probs[0:r, kt % P_RING, :],
                                  p_hi[0:r, kt % RING, :].bitcast(F32), ALU.subtract).then_inc(lo_done, 1)

            def chunk_maximum(x, g, c):
                h, half = c // 2, c % 2
                dve.wait_ge(chunk_done, CHUNKS * x + c + 1)
                dve.tensor_reduce(mx[:, g, h, half:half + 1], ps[:, 2 * half:2 * half + 2, :].rearrange("p b n -> p (b n)"),
                                  AX.X, ALU.max).then_inc(chunk_max, 1)

            def tail_maximum(x, g):
                dve.wait_ge(tail_done, x + 1)
                dve.tensor_reduce(mx[:, g, :, 2], ps[:, MISC, 0:HG * META].rearrange("p (h n) -> p h n", n=META),
                                  AX.X, ALU.max).then_inc(tail_max, 1)

            def maximum(x, g):
                dve.wait_ge(chunk_max, CHUNKS * (x + 1))
                dve.wait_ge(tail_max, x + 1)
                dve.tensor_reduce(mx_all[:], mx[:, g], AX.X, ALU.max).then_inc(max_done, 1)
                dve.wait_ge(max_done, x + 1)
                dve.tensor_tensor(q_raw[:, g, :, ROW], q_raw[:, g, :, 0], mx_all[:], ALU.subtract).then_inc(neg_max_done, 1)

            def q_low(x, g):
                dve.wait_ge(q_max_turned, x + 1)
                dve.tensor_tensor(q_lo[:, g, :], ps[0:HD + 1, MISC, :], q_hi[0:HD + 1, g, :].bitcast(F32),
                                  ALU.subtract).then_inc(q_lo_done, 1)

            def normalise(qt, g):
                s = 2 * qt + g
                dve.wait_ge(out_done, s + 1)
                turned = ps[:, MISC, 0:HG * (HD + 1)].rearrange("p (h n) -> p h n", n=HD + 1)
                dve.reciprocal(rden[:], turned[:, :, HD]).then_inc(rden_done, 1)
                dve.wait_ge(rden_done, s + 1)
                dve.wait_ge(o_store[g], 16 * (qt + 1))
                dve.tensor_tensor(o_out[:, g, :].rearrange("p (h n) -> p h n", n=HD),
                                  turned[:, :, 0:HD],
                                  rden[:].unsqueeze(2).broadcast_to([P, HG, HD]), ALU.mult).then_inc(o_done, 1)

            def step(qt, g, first=False, prepare=True):
                s, og = 2 * qt + g, 1 - g
                for kt in range(NKT):
                    if prepare and kt + 1 in CHUNK_AT:
                        chunk_maximum(s + 1, og, CHUNK_AT.index(kt + 1))
                    if kt == OUT_AT - 1 and not first:
                        normalise(qt - 1 + g, og)
                    if prepare and kt == TAIL_AT:
                        tail_maximum(s + 1, og)
                    if prepare and kt == Q2_AT - 2:
                        maximum(s + 1, og)
                    if prepare and kt == Q2_AT - 1:
                        q_low(s + 1, og)
                    low(s, kt)

            dve.memset(k_one[HD:HD + 1].bitcast(F32), 1.0).then_inc(ones_set, 1)
            chunk_maximum(0, 0, 0)
            tail_maximum(0, 0)
            for c in range(1, CHUNKS):
                chunk_maximum(0, 0, c)
            dve.wait_ge(q_in[0], 32)
            maximum(0, 0)
            q_low(0, 0)
            step(0, 0, first=True)
            step(0, 1)
            with dve.Fori(1, NT - 1) as qt:
                for g in range(KV):
                    step(qt, g)
            step(NT - 1, 0)
            step(NT - 1, 1, prepare=False)
            normalise(NT - 1, 1)


def pooling_windows(pool, u, pool_ab, corr, u_in, chain):
    n = [0]

    def link(ins):
        n[0] += 1
        ins.then_inc(chain, 1)
        pool.wait_ge(chain, n[0])

    link(pool.memset(u[:, :, L:UPAD], 0.0))
    pool.wait_ge(u_in, 32)
    for g, w in enumerate(WINDOWS):
        src, have = u[:, g, :], 1
        reach = w // 2
        while have < w:
            have *= 2
            h = have // 2
            ahead = reach - have // 2
            a, b = META - ahead, L + ahead
            dst = pool_ab[(have.bit_length() + g) % 2]
            before, behind = (1, 0) if have == 2 else (h // 2, h // 2)
            link(pool.tensor_tensor(dst[:, a:b], src[:, a - before:b - before], src[:, a + behind:b + behind], ALU.add))
            src = dst
        link(pool.tensor_scalar(src[:, META:L], src[:, META:L], 1.0 / w, 1.0, ALU.mult, ALU.mult))
        link(pool.tensor_tensor(src[:, L - 8:L], src[:, L - 8:L], corr[:, g, :], ALU.mult))
        link(pool.tensor_tensor(u[:, g, META:L], src[:, META:L], u[:, g, META:L], ALU.subtract))


def mix(nc, m, x, w_out, attn_norm, pool_scale):
    with ExitStack() as ctx:
        sb = lambda n, s, d=F32: ctx.enter_context(nc.sbuf_tensor(n, s, d))
        sem = lambda n: ctx.enter_context(nc.semaphore(n))
        ident, ps, eps = m.ident, m.ps, m.eps
        wo_hi = sb("wo_hi", [P, KT, D], F32R)
        wo_lo = sb("wo_lo", [P, KT, D], F32R)
        wp_hi = sb("wp_hi", [P, GROUPS, P], F32R)
        wp_lo = sb("wp_lo", [P, GROUPS, P], F32R)
        d_hi = sb("d_hi", [P, GROUPS, CW], F32R)
        d_lo = sb("d_lo", [P, GROUPS, CW], F32R)
        o_raw = sb("o_raw", [P, CT, DA])
        mt = sb("mt", [P, CT, D])
        mT_hi = sb("mT_hi", [P, KT, CW], F32R)
        mT_lo = sb("mT_lo", [P, KT, CW], F32R)
        x_res = sb("x_res", [P, CT, D])
        g_mix = sb("g_mix", [P, KT])
        ss = sb("mss", [P, CT, 2])
        sd = sb("msd", [P, CT, 2])
        rs = sb("mrs", [P, CT, 2])

        const_in = sem("m_const_in")
        wo_in = [sem(f"m_wo_in{j}") for j in range(WO_AHEAD)]
        w_hi_done, w_lo_done = sem("m_w_hi_done"), sem("m_w_lo_done")
        o_in = [sem(f"m_o_in{j}") for j in range(CT)]
        x_in = [sem(f"m_x_in{j}") for j in range(CT)]
        x_store = [sem(f"m_x_store{j}") for j in range(CT)]
        d_hi_done, d_lo_done, y_done = sem("m_d_hi_done"), sem("m_d_lo_done"), sem("m_y_done")
        ssq_done, sd_done, rs_done, mt_done = sem("m_ssq_done"), sem("m_sd_done"), sem("m_rs_done"), sem("m_mt_done")
        t_done, hi_done, lo_done = sem("m_t_done"), sem("m_hi_done"), sem("m_lo_done")
        out_done, res_done = sem("m_out_done"), sem("m_res_done")

        block = ctx.enter_context(nc.Block())

        @block.sync
        def _(sp):
            for dst, src in (
                (g_mix[:, 0:4], attn_norm),
                (g_mix[:, 4:8], pool_scale),
            ):
                sp.dma_start(dst, src).then_inc(const_in, 16)
            for j in range(CT):
                sp.dma_start(o_raw[:, j, :], m.o_d[j * P:(j + 1) * P]).then_inc(o_in[j], 16)
            for k in range(WO_AHEAD, KT):
                sp.wait_ge(w_lo_done, k - WO_AHEAD + 2)
                sp.dma_start(m.wo_raw[:, k % WO_AHEAD, :], w_out[k * P:(k + 1) * P]).then_inc(wo_in[k % WO_AHEAD], 16)

            def store(c):
                for j in range(CT):
                    sp.wait_ge(res_done, 2 * c + j + 3)
                    sp.dma_start(m.x2_d[ds(c * CW + j * P, P)], x_res[:, j, :]).then_inc(x_store[j], 16)

            def chunk(c):
                for j in range(CT):
                    sp.wait_ge(mt_done, 2 * c + j - 1)
                    sp.dma_start(o_raw[:, j, :], m.o_d[ds(c * CW + j * P, P)]).then_inc(o_in[j], 16)
                store(c - 1)

            with sp.Fori(1, NCH) as c:
                chunk(c)
            store(NCH - 1)
            for j in range(CT):
                sp.wait_ge(x_store[j], 16 * (NCH + 1))

        @block.gpsimd
        def _(pool):
            def residual_in(c):
                for j in range(CT):
                    pool.wait_ge(x_store[j], 16 * (c + 1))
                    pool.dma_start(x_res[:, j, :], x[ds(c * CW + j * P, P)]).then_inc(x_in[j], 16)

            for j in range(CT):
                pool.sem_inc(x_store[j], 16)
            with pool.Fori(0, NCH) as c:
                residual_in(c)

        @block.scalar
        def _(act):
            def split_d(c):
                act.wait_ge(y_done, 2 * c + 1)
                split_hi(act, d_hi[:], m.u_sb[:, :, ds(c * CW + META, CW)]).then_inc(d_hi_done, 1)

            def norm_tile(c, j):
                i = 2 * c + j
                act.wait_ge(o_in[j], 16 * (c + 1))
                act.wait_ge(t_done, 8 * c + 1)
                act.activation(mt[:, j, 0:DA], o_raw[:, j, :], ACT.Square, accum_out=ss[:, j, 0:1]).then_inc(ssq_done, 1)
                act.wait_ge(y_done, i + 2)
                act.activation(mt[:, j, DA:], ps[:, j, :], ACT.Square, accum_out=ss[:, j, 1:2]).then_inc(ssq_done, 1)
                act.wait_ge(ssq_done, 2 * i + 2)
                act.activation(sd[:, j, :], ss[:, j, :], ACT.Sqrt, scale=1.0 / DA, bias=eps[:]).then_inc(sd_done, 1)

            def evac(c):
                for k in range(KT):
                    act.wait_ge(t_done, 8 * c + k + 2)
                    split_hi(act, mT_hi[:, k, :], ps[:, 2 + k % 2, 0:CW], g_mix[:, k:k + 1]).then_inc(hi_done, 1)

            act.sem_inc(y_done, 1)
            act.sem_inc(t_done, 1)
            act.wait_ge(const_in, 32)
            split_hi(act, wp_hi[:], m.wp_raw[:]).then_inc(w_hi_done, 1)
            split_d(0)
            for j in range(CT):
                norm_tile(0, j)
            evac(0)
            for k in range(KT):
                if k >= WO_AHEAD:
                    act.wait_ge(wo_in[k % WO_AHEAD], 16)
                split_hi(act, wo_hi[:, k, :], m.wo_raw[:, k % WO_AHEAD, :]).then_inc(w_hi_done, 1)
            with act.Fori(0, NCH - 1) as c:
                split_d(c + 1)
                for j in range(CT):
                    norm_tile(c + 1, j)
                evac(c + 1)

        @block.vector
        def _(dve):
            def split_d(c):
                dve.wait_ge(d_hi_done, c + 1)
                dve.tensor_tensor(d_lo[:], m.u_sb[:, :, ds(c * CW + META, CW)], d_hi[:].bitcast(F32),
                                  ALU.subtract).then_inc(d_lo_done, 1)

            def norm_tile(c, j):
                i = 2 * c + j
                dve.wait_ge(sd_done, i + 1)
                dve.reciprocal(rs[:, j, :], sd[:, j, :]).then_inc(rs_done, 1)
                dve.wait_ge(rs_done, i + 1)
                dve.tensor_scalar(mt[:, j, 0:DA], o_raw[:, j, :], rs[:, j, 0:1], None, ALU.mult)
                dve.tensor_scalar(mt[:, j, DA:], ps[:, j, :], rs[:, j, 1:2], None, ALU.mult).then_inc(mt_done, 1)

            def evac(c):
                for k in range(KT):
                    dve.wait_ge(hi_done, 8 * c + k + 1)
                    dve.scalar_tensor_tensor(mT_lo[:, k, :], ps[:, 2 + k % 2, 0:CW], g_mix[:, k:k + 1],
                                             mT_hi[:, k, :].bitcast(F32), ALU.mult, ALU.subtract).then_inc(lo_done, 1)

            def residual(c, j):
                dve.wait_ge(out_done, 2 * c + j + 1)
                dve.wait_ge(x_in[j], 16 * (c + 1))
                dve.tensor_tensor(x_res[:, j, :], ps[:, 4 + 2 * j:6 + 2 * j, :].rearrange("p b n -> p (b n)"),
                                  x_res[:, j, :], ALU.add).then_inc(res_done, 1)

            dve.sem_inc(lo_done, 2)
            dve.sem_inc(res_done, 2)
            dve.wait_ge(const_in, 32)
            dve.wait_ge(w_hi_done, 1)
            dve.tensor_tensor(wp_lo[:], m.wp_raw[:], wp_hi[:].bitcast(F32), ALU.subtract).then_inc(w_lo_done, 1)
            split_d(0)
            for j in range(CT):
                norm_tile(0, j)
            evac(0)
            for k in range(KT):
                dve.wait_ge(w_hi_done, k + 2)
                dve.tensor_tensor(wo_lo[:, k, :], m.wo_raw[:, k % WO_AHEAD, :], wo_hi[:, k, :].bitcast(F32),
                                  ALU.subtract).then_inc(w_lo_done, 1)
            with dve.Fori(0, NCH - 1) as c:
                split_d(c + 1)
                residual(c, 0)
                for j in range(CT):
                    norm_tile(c + 1, j)
                evac(c + 1)
                residual(c, 1)
            residual(NCH - 1, 0)
            residual(NCH - 1, 1)

        @block.tensor
        def _(pe):
            def pool_map(c, j):
                t = slice(j * P, (j + 1) * P)
                if j == 0:
                    pe.wait_ge(d_lo_done, c + 1)
                for g in range(GROUPS):
                    last = matmul3(pe, ps[:, j, g * P:(g + 1) * P], d_hi[:, g, t], d_lo[:, g, t],
                                   wp_hi[:, g, :], wp_lo[:, g, :], True, True)
                last.then_inc(y_done, 1)

            def transpose(c, k):
                if k == 0:
                    pe.wait_ge(mt_done, 2 * c + 2)
                pe.wait_ge(lo_done, 8 * c + k + 1)
                for j in range(CT):
                    last = pe.transpose(ps[:, 2 + k % 2, j * P:(j + 1) * P], mt[:, j, k * P:(k + 1) * P], ident[:])
                last.then_inc(t_done, 1)

            def project_out(c, j, first=False, following=False):
                t = slice(j * P, (j + 1) * P)
                pe.wait_ge(res_done, 2 * c + j + 1)
                for half in range(2):
                    w = slice(half * 512, (half + 1) * 512)
                    for k in range(KT):
                        if j == 0 and half == 0:
                            pe.wait_ge(lo_done, 8 * c + k + 3)
                            if first:
                                pe.wait_ge(w_lo_done, k + 2)
                        last = matmul3(pe, ps[:, 4 + 2 * j + half, :], mT_hi[:, k, t], mT_lo[:, k, t],
                                       wo_hi[:, k, w], wo_lo[:, k, w], k == 0, k == KT - 1)
                        if half == 1 and k == KT - 1:
                            last.then_inc(out_done, 1)
                        if half == 1 and following:
                            transpose(c + 1, k)

            for j in range(CT):
                pool_map(0, j)
            for k in range(KT):
                transpose(0, k)
            project_out(0, 0, first=True)
            for j in range(CT):
                pool_map(1, j)
            project_out(0, 1, following=True)
            with pe.Fori(1, NCH - 1) as c:
                project_out(c, 0)
                for j in range(CT):
                    pool_map(c + 1, j)
                project_out(c, 1, following=True)
            project_out(NCH - 1, 0)
            project_out(NCH - 1, 1)


def feed(nc, m, w_ffn_in, w_ffn_down, norm_ffn, norm_final, out):
    UP_PAIRS, DOWN_PAIRS = FT, FT // 2
    PAIRS = UP_PAIRS + DOWN_PAIRS
    HEAD = 1 + FC
    with ExitStack() as ctx:
        sb = lambda n, s, d=F32: ctx.enter_context(nc.sbuf_tensor(n, s, d))
        sem = lambda n: ctx.enter_context(nc.semaphore(n))
        ident, ps, eps = m.ident, m.ps, m.eps
        x2 = sb("x2", [P, FC, D])
        hT_hi = sb("fT_hi", [P, KT, FW], F32R)
        hT_lo = sb("fT_lo", [P, KT, FW], F32R)
        gu_hi = sb("gu_hi", [P, FT, FW], F32R)
        gu_lo = sb("gu_lo", [P, FT, FW], F32R)
        w_raw = sb("w_raw", [P, 2, D])
        w_hi = sb("w_hi", [P, 2, D], F32R)
        w_lo = sb("w_lo", [P, 2, D], F32R)
        silu = sb("silu", [P, FW])
        gu = sb("gu", [P, FW])
        res = sb("res", [P, FC, D])
        junk = sb("junk", [P, D])
        g_final = sb("g_final", [P, D])
        g_ffn = sb("g_ffn", [P, KT])
        ss = sb("fss", [P, 2, FC])
        sd = sb("fsd", [P, 2, FC])
        rs = sb("frs", [P, 2, FC])

        const_in = sem("f_const_in")
        x2_in = [sem(f"f_x2_in{j}") for j in range(FC)]
        w_in = [sem(f"f_w_in{j}") for j in range(2)]
        w_hi_done, w_lo_done, w_used = sem("f_w_hi_done"), sem("f_w_lo_done"), sem("f_w_used")
        ssq_done, sd_done, rs_done, xn_done = sem("f_ssq_done"), sem("f_sd_done"), sem("f_rs_done"), sem("f_xn_done")
        t_done, h_hi_done, h_lo_done = sem("f_t_done"), sem("f_h_hi_done"), sem("f_h_lo_done")
        silu_done, gu_done, gu_hi_done, gu_lo_done = sem("f_silu_done"), sem("f_gu_done"), sem("f_gu_hi_done"), sem("f_gu_lo_done")
        down_done, res_done = sem("f_down_done"), sem("f_res_done")
        res_in = [sem(f"f_res_in{j}") for j in range(FC)]
        out_store = [sem(f"f_out_store{j}") for j in range(FC)]
        fssq_done, fsd_done, frs_done, fin_done = sem("f_fssq_done"), sem("f_fsd_done"), sem("f_frs_done"), sem("f_fin_done")

        block = ctx.enter_context(nc.Block())

        @block.sync
        def _(sp):
            def load(b, slot, src):
                sp.wait_ge(w_lo_done, b + 1)
                sp.dma_start(w_raw[:, slot, :].rearrange("p (k n) -> p k n", n=src.shape[-1]), src).then_inc(w_in[slot], 16)

            w_up = w_ffn_in.rearrange("(k p) n -> p k n", p=P)

            def store(c, j):
                sp.wait_ge(fin_done, FC * c + j + 1)
                sp.dma_start(out[ds(c * FW + j * P, P)], res[:, j, :]).then_inc(out_store[j], 16)

            def load_x2(c, j):
                sp.dma_start(x2[:, j, :], m.x2_d[ds(c * FW + j * P, P)]).then_inc(x2_in[j], 16)

            def blocks(c, f0, f1):
                with sp.Fori(f0, f1) as f:
                    for a in range(2):
                        load(2 * PAIRS * c + 2 * f + a, a, w_up[:, :, ds(f * P + a * DFF, P)])

            def chunk(c, first=False, last=False):
                blocks(c, 0, HEAD + 2)
                for j in range(FC):
                    if not first:
                        store(c - 1, j)
                    blocks(c, HEAD + 2 + j, HEAD + 3 + j)
                blocks(c, HEAD + 2 + FC, UP_PAIRS - FC)
                if not last:
                    sp.wait_ge(t_done, KT * (c + 1))
                for j in range(FC):
                    if not last:
                        load_x2(c + 1, j)
                    blocks(c, UP_PAIRS - FC + j, UP_PAIRS - FC + j + 1)
                with sp.Fori(0, DOWN_PAIRS) as i:
                    for a in range(2):
                        load(2 * PAIRS * c + 2 * i + (2 * UP_PAIRS + a), a,
                             w_ffn_down[ds(i * 2 * P + a * P, P)].unsqueeze(1))

            for j in range(FC):
                load_x2(0, j)
            chunk(0, first=True)
            with sp.Fori(1, NFC - 1) as c:
                chunk(c)
            chunk(NFC - 1, last=True)
            for j in range(FC):
                store(NFC - 1, j)

        @block.gpsimd
        def _(pool):
            def load_res(c):
                for j in range(FC):
                    pool.wait_ge(out_store[j], 16 * (c + 1))
                    pool.dma_start(res[:, j, :], m.x2_d[ds(c * FW + j * P, P)]).then_inc(res_in[j], 16)

            for j in range(FC):
                pool.sem_inc(out_store[j], 16)
            pool.dma_start(g_ffn[:], norm_ffn).then_inc(const_in, 16)
            pool.dma_start(g_final[:], norm_final.unsqueeze(0).broadcast_to([P, D])).then_inc(const_in, 16)
            with pool.Fori(0, NFC) as c:
                load_res(c)
            for j in range(FC):
                pool.wait_ge(out_store[j], 16 * (NFC + 1))

        @block.scalar
        def _(act):
            def split(w, slot):
                act.wait_ge(w_in[slot], 16 * w + 16)
                act.wait_ge(w_used, 2 * w + slot + 1)
                split_hi(act, w_hi[:, slot, :], w_raw[:, slot, :]).then_inc(w_hi_done, 1)

            def norm_tile(c, j):
                act.wait_ge(x2_in[j], 16 * (c + 1))
                act.activation(junk[:], x2[:, j, :], ACT.Square, accum_out=ss[:, 0, j:j + 1]).then_inc(ssq_done, 1)
                act.wait_ge(ssq_done, FC * c + j + 1)
                act.activation(sd[:, 0, j:j + 1], ss[:, 0, j:j + 1], ACT.Sqrt, scale=1.0 / D, bias=eps[:]).then_inc(sd_done, 1)

            def evac(c):
                for k in range(KT):
                    act.wait_ge(t_done, KT * c + k + 1)
                    split_hi(act, hT_hi[:, k, :], ps[:, k % 2, :], g_ffn[:, k:k + 1]).then_inc(h_hi_done, 1)

            def up(c, f):
                act.wait_ge(w_used, 2 * PAIRS * c + 2 * f + 3)
                split(PAIRS * c + f + 1, 0)
                act.activation(silu[:], ps[:, 2, :], ACT.Silu).then_inc(silu_done, 1)
                act.wait_ge(gu_done, UP_PAIRS * c + f + 2)
                split_hi(act, gu_hi[:, ds(f, 1), :].rearrange("p a n -> p (a n)"), gu[:]).then_inc(gu_hi_done, 1)
                split(PAIRS * c + f + 1, 1)

            def down(c, normed):
                cuts = (0, 3, 6, 9, DOWN_PAIRS - 1) if normed else (0, DOWN_PAIRS - 1)
                for j, (a, b) in enumerate(zip(cuts, cuts[1:])):
                    with act.Fori(a, b) as i:
                        for slot in range(2):
                            split(PAIRS * c + i + (UP_PAIRS + 1), slot)
                    if normed:
                        norm_tile(c + 1, j)

            def final(c, j):
                act.wait_ge(res_done, FC * c + j + FC + 1)
                act.activation(junk[:], res[:, j, :], ACT.Square, accum_out=ss[:, 1, j:j + 1]).then_inc(fssq_done, 1)
                act.wait_ge(fssq_done, FC * c + j + 1)
                act.activation(sd[:, 1, j:j + 1], ss[:, 1, j:j + 1], ACT.Sqrt, scale=1.0 / D, bias=eps[:]).then_inc(fsd_done, 1)

            act.sem_inc(silu_done, 1)
            for j in range(FC):
                norm_tile(0, j)
            split(0, 0)
            split(0, 1)
            act.wait_ge(const_in, 32)
            evac(0)
            for f in range(HEAD):
                up(0, f)
            with act.Fori(0, NFC - 1) as c:
                with act.Fori(HEAD, UP_PAIRS) as f:
                    up(c, f)
                down(c, True)
                for slot in range(2):
                    split(PAIRS * (c + 1), slot)
                evac(c + 1)
                up(c + 1, 0)
                for j in range(FC):
                    up(c + 1, 1 + j)
                    final(c, j)
            with act.Fori(HEAD, UP_PAIRS) as f:
                up(NFC - 1, f)
            down(NFC - 1, False)
            for j in range(FC):
                final(NFC - 1, j)

        @block.vector
        def _(dve):
            def split(w, slot):
                dve.wait_ge(w_hi_done, 2 * w + slot + 1)
                dve.tensor_tensor(w_lo[:, slot, :], w_raw[:, slot, :], w_hi[:, slot, :].bitcast(F32),
                                  ALU.subtract).then_inc(w_lo_done, 1)

            def norm_tile(c, j):
                dve.wait_ge(sd_done, FC * c + j + 1)
                dve.reciprocal(rs[:, 0, j:j + 1], sd[:, 0, j:j + 1]).then_inc(rs_done, 1)
                dve.wait_ge(rs_done, FC * c + j + 1)
                dve.tensor_scalar(x2[:, j, :], x2[:, j, :], rs[:, 0, j:j + 1], None, ALU.mult).then_inc(xn_done, 1)

            def evac(c, k0=0, k1=KT):
                for k in range(k0, k1):
                    dve.wait_ge(h_hi_done, KT * c + k + 1)
                    dve.scalar_tensor_tensor(hT_lo[:, k, :], ps[:, k % 2, :], g_ffn[:, k:k + 1],
                                             hT_hi[:, k, :].bitcast(F32), ALU.mult, ALU.subtract).then_inc(h_lo_done, 1)

            def up(c, f):
                split(PAIRS * c + f + 1, 0)
                dve.wait_ge(silu_done, UP_PAIRS * c + f + 2)
                dve.wait_ge(w_used, 2 * PAIRS * c + 2 * f + 4)
                dve.tensor_tensor(gu[:], silu[:], ps[:, 3, :], ALU.mult).then_inc(gu_done, 1)
                dve.wait_ge(gu_hi_done, UP_PAIRS * c + f + 1)
                dve.tensor_tensor(gu_lo[:, ds(f, 1), :].rearrange("p a n -> p (a n)"), gu[:],
                                  gu_hi[:, ds(f, 1), :].rearrange("p a n -> p (a n)").bitcast(F32),
                                  ALU.subtract).then_inc(gu_lo_done, 1)
                split(PAIRS * c + f + 1, 1)

            def down(c, normed):
                cuts = (0, 3, 6, 9, DOWN_PAIRS - 1) if normed else (0, DOWN_PAIRS - 1)
                for j, (a, b) in enumerate(zip(cuts, cuts[1:])):
                    with dve.Fori(a, b) as i:
                        for slot in range(2):
                            split(PAIRS * c + i + (UP_PAIRS + 1), slot)
                    if normed:
                        norm_tile(c + 1, j)

            def residual(c, j):
                dve.wait_ge(down_done, FC * c + j + 1)
                dve.wait_ge(res_in[j], 16 * (c + 1))
                dve.tensor_tensor(res[:, j, :], ps[:, 2 * j:2 * j + 2, :].rearrange("p b n -> p (b n)"),
                                  res[:, j, :], ALU.add).then_inc(res_done, 1)

            def final(c, j):
                dve.wait_ge(fsd_done, FC * c + j + 1)
                dve.reciprocal(rs[:, 1, j:j + 1], sd[:, 1, j:j + 1]).then_inc(frs_done, 1)
                dve.wait_ge(frs_done, FC * c + j + 1)
                dve.scalar_tensor_tensor(res[:, j, :], res[:, j, :], rs[:, 1, j:j + 1], g_final[:],
                                         ALU.mult, ALU.mult).then_inc(fin_done, 1)

            dve.sem_inc(w_lo_done, 2)
            dve.sem_inc(h_lo_done, 2)
            dve.sem_inc(gu_done, 1)
            dve.sem_inc(res_done, FC)
            for j in range(FC):
                norm_tile(0, j)
            split(0, 0)
            split(0, 1)
            dve.wait_ge(const_in, 32)
            evac(0)
            for f in range(HEAD):
                up(0, f)
            with dve.Fori(0, NFC - 1) as c:
                with dve.Fori(HEAD, UP_PAIRS) as f:
                    up(c, f)
                down(c, True)
                split(PAIRS * (c + 1), 0)
                residual(c, 0)
                evac(c + 1, 0, 1)
                residual(c, 1)
                evac(c + 1, 1, 2)
                split(PAIRS * (c + 1), 1)
                evac(c + 1, 2)
                up(c + 1, 0)
                residual(c, 2)
                residual(c, 3)
                for j in range(FC):
                    up(c + 1, 1 + j)
                    final(c, j)
            with dve.Fori(HEAD, UP_PAIRS) as f:
                up(NFC - 1, f)
            down(NFC - 1, False)
            for j in range(FC):
                residual(NFC - 1, j)
            for j in range(FC):
                final(NFC - 1, j)

        @block.tensor
        def _(pe):
            pe.sem_inc(w_used, 2)
            with pe.Fori(0, NFC) as c:
                pe.wait_ge(xn_done, FC * (c + 1))
                pe.wait_ge(res_done, FC * c + 1)
                for n in range(KT + 5):
                    if n < KT:
                        pe.wait_ge(h_lo_done, KT * c + n + 1)
                        for j in range(FC):
                            last = pe.transpose(ps[:, n % 2, j * P:(j + 1) * P], x2[:, j, n * P:(n + 1) * P], ident[:])
                        last.then_inc(t_done, 1)
                    if n in (2, 5):
                        pe.wait_ge(w_lo_done, 2 * PAIRS * c + (3 if n == 2 else 4))
                    if n == 2:
                        pe.wait_ge(res_done, FC * c + 2)
                    for a, k in ((0, n - 2), (1, n - 5)):
                        if 0 <= k < KT:
                            if a == 0:
                                pe.wait_ge(h_lo_done, KT * c + k + 3)
                            w = slice(k * P, (k + 1) * P)
                            last = matmul3(pe, ps[:, 2 + a, :], w_hi[:, a, w], w_lo[:, a, w],
                                           hT_hi[:, k, :], hT_lo[:, k, :], k == 0, k == KT - 1)
                            if k == KT - 1:
                                last.then_inc(w_used, 1)
                with pe.Fori(1, UP_PAIRS) as f:
                    for a in range(2):
                        pe.wait_ge(w_lo_done, 2 * PAIRS * c + 2 * f + a + 3)
                        pe.wait_ge(gu_done if a else silu_done, UP_PAIRS * c + f + 1)
                        for k in range(KT):
                            w = slice(k * P, (k + 1) * P)
                            last = matmul3(pe, ps[:, 2 + a, :], w_hi[:, a, w], w_lo[:, a, w],
                                           hT_hi[:, k, :], hT_lo[:, k, :], k == 0, k == KT - 1)
                        last.then_inc(w_used, 1)
                pe.wait_ge(res_done, FC * c + FC)
                for f in range(FT):
                    slot = f % 2
                    pe.wait_ge(w_lo_done, 2 * PAIRS * c + (2 * UP_PAIRS + f + 3))
                    pe.wait_ge(gu_lo_done, UP_PAIRS * c + f + 1)
                    for j in range(FC):
                        if f == 0 and j == 1:
                            pe.wait_ge(silu_done, UP_PAIRS * c + UP_PAIRS + 1)
                            pe.wait_ge(gu_done, UP_PAIRS * c + UP_PAIRS + 1)
                        t = slice(j * P, (j + 1) * P)
                        for half in range(2):
                            w = slice(half * 512, (half + 1) * 512)
                            last = matmul3(pe, ps[:, 2 * j + half, :], gu_hi[:, f, t], gu_lo[:, f, t],
                                           w_hi[:, slot, w], w_lo[:, slot, w], f == 0, f == FT - 1)
                        if f == FT - 1:
                            last.then_inc(down_done, 1)
                    if f < FT - 1:
                        last.then_inc(w_used, 1)
                pe.wait_ge(down_done, FC * (c + 1))
                pe.sem_inc(w_used, 1)


def build(nc, x, meta_tokens, norm_mix, w_in, q_norm, k_norm, attn_out_norm, w_pool, pool_scale, w_out,
          norm_ffn, w_ffn_in, w_ffn_down, norm_final, rope, ident, corr, out):
    m = Shared()
    m.ident_in, m.corr_in = ident, corr
    m.q_d = nc.dram_tensor("q_d", (SEQ, DA), F32).ap()
    m.u_d = nc.dram_tensor("u_d", (GROUPS, P, L), F32).ap()
    m.o_d = nc.dram_tensor("o_d", (SEQ, DA), F32).ap()
    m.x2_d = nc.dram_tensor("x2_d", (SEQ, D), F32).ap()
    with ExitStack() as ctx:
        m.ident = ctx.enter_context(nc.sbuf_tensor("ident", [P, P], F32))
        m.eps = ctx.enter_context(nc.sbuf_tensor("eps", [P, 1], F32))
        m.ps = ctx.enter_context(nc.psum_tensor("ps", [P, 8, 512], F32))
        m.eps_set = ctx.enter_context(nc.semaphore("eps_set"))
        m.v_ones_set = ctx.enter_context(nc.semaphore("v_ones_set"))
        with ExitStack() as kv:
            m.k_st = kv.enter_context(nc.sbuf_tensor("k_st", [P, KV, L], F32R))
            m.v_st = kv.enter_context(nc.sbuf_tensor("v_st", [P, NKT, KV, 2 * HD + 1], F32R))
            project(nc, m, x, meta_tokens, rope, w_in, norm_mix, q_norm, k_norm)
            m.u_sb = kv.enter_context(nc.sbuf_tensor("u_sb", [P, GROUPS, UPAD], F32))
            m.wp_raw = kv.enter_context(nc.sbuf_tensor("wp_raw", [P, GROUPS, P], F32))
            m.wo_raw = kv.enter_context(nc.sbuf_tensor("wo_raw", [P, WO_AHEAD, D], F32))
            attend(nc, m, w_pool, w_out)
            mix(nc, m, x, w_out, attn_out_norm, pool_scale)
        feed(nc, m, w_ffn_in, w_ffn_down, norm_ffn, norm_final, out)


def shape_tables():
    pairs = HD // 4
    f32 = np.float32
    t = np.arange(SEQ)
    row = (t // GRID_W - SEQ // GRID_W // 2).astype(f32)
    col = (t % GRID_W - GRID_W // 2).astype(f32)
    freqs = f32(ROPE_THETA) ** (-np.arange(pairs, dtype=f32) / f32(pairs))
    ang = np.zeros((L, 2, pairs), f32)
    ang[:SEQ, 0] = row[:, None] * freqs
    ang[:SEQ, 1] = col[:, None] * freqs
    cos, sin = np.cos(ang), np.sin(ang)
    table = np.stack([np.stack([cos, cos], 2), np.stack([-sin, sin], 2)], 1)
    corr = np.ones((P, GROUPS, 8), f32)
    for g, w in enumerate(WINDOWS):
        for i in range(8):
            pos = L - 8 + i
            corr[:, g, i] = w / (min(pos + w // 2, L) - (pos - w // 2))
    return table.reshape(L, 2 * HD).astype(f32), np.eye(P, dtype=f32), corr


def kernel(x, meta_tokens, norm_mix, w_in, q_norm, k_norm, attn_out_norm, w_pool, pool_scale, w_out,
           norm_ffn, w_ffn_in, w_ffn_down, norm_final):
    import concourse.bacc as bacc
    from concourse.bass_utils import run_bass_kernel_spmd

    nc = bacc.Bacc("TRN2", target_bir_lowering=False, num_devices=1)
    rope, ident, corr = shape_tables()
    columns = lambda g: g.reshape(-1, P).T
    given = {
        "x": x[0], "meta_tokens": meta_tokens, "norm_mix": columns(norm_mix[0]), "w_in": w_in[0], "q_norm": q_norm[0],
        "k_norm": k_norm[0], "attn_out_norm": columns(attn_out_norm[0]), "w_pool": w_pool[0], "pool_scale": columns(pool_scale[0]),
        "w_out": w_out[0], "norm_ffn": columns(norm_ffn[0]), "w_ffn_in": w_ffn_in[0], "w_ffn_down": w_ffn_down[0],
        "norm_final": norm_final, "rope": rope, "ident": ident, "corr": corr,
    }
    arrays = {f"in_{k}": np.ascontiguousarray(v) for k, v in given.items()}
    args = [nc.dram_tensor(k, a.shape, mybir.dt.from_np(a.dtype), kind="ExternalInput").ap() for k, a in arrays.items()]
    out = nc.dram_tensor("out_x", (SEQ, D), F32, kind="ExternalOutput").ap()
    build(nc, *args, out)
    r = run_bass_kernel_spmd(nc, [arrays], core_ids=[0])
    return r.results[0]["out_x"].reshape(1, SEQ, D)
```
